# Optimizing a Trainium2 kernel written in Bass

```python
import jax
import jax.numpy as jnp
from jax import lax
import numpy as np
import math
import jax, jax.numpy as jnp

D_MODEL = 1024
BATCH = 1
SEQ = 512
DEPTH = 1

D_RNN = D_MODEL
N_LRU_BLOCKS = 16
LRU_BLOCK = D_RNN // N_LRU_BLOCKS
CONV_WIDTH = 4
LRU_C = 8.0
N_HEADS = 16
HEAD_DIM = 64
N_KV_GROUPS = 4
HEADS_PER_GROUP = N_HEADS // N_KV_GROUPS
D_ATTN = N_HEADS * HEAD_DIM
D_KV = N_KV_GROUPS * HEAD_DIM
CMP_LEN = 32
CMP_STRIDE = 16
CMP_HIDDEN = 256
SEL_LEN = 64
SEL_TOPK = 16
WINDOW = 512
Q_BLOCK = 64
FORCE_SCORE = 1e4
R_SEL = SEL_LEN // CMP_STRIDE
R_CMP = CMP_LEN // CMP_STRIDE
ALIBI_MAX_BIAS = 8.0
D_FF = 2816
D_PLE = 256
NORM_EPS = 1e-6

_IN_SIZES = (D_RNN, D_RNN, D_ATTN, D_KV, D_KV, D_KV, D_KV, D_KV, D_KV, 3 * N_HEADS, D_MODEL, D_MODEL)
D_IN = sum(_IN_SIZES)
IN_SPLITS = tuple(int(c) for c in np.cumsum(_IN_SIZES)[:-1])


def rmsnorm(x, g):
    x32 = x.astype(jnp.float32)
    y = x32 * lax.rsqrt(jnp.mean(x32 * x32, axis=-1, keepdims=True) + NORM_EPS)
    return (y * g.astype(jnp.float32)).astype(x.dtype)

def alibi_slopes():
    h = jnp.arange(1, N_HEADS + 1, dtype=jnp.float32)
    return jnp.exp2(-ALIBI_MAX_BIAS * h / N_HEADS)

def masked_softmax(s, mask):
    s = jnp.where(mask, s.astype(jnp.float32), -jnp.inf)
    m = jnp.max(s, axis=-1, keepdims=True)
    m = jnp.where(jnp.isfinite(m), m, 0.0)
    e = jnp.where(mask, jnp.exp(s - m), 0.0)
    return e / jnp.maximum(jnp.sum(e, axis=-1, keepdims=True), 1e-30)

def causal_conv(x, w, b):
    S = x.shape[1]
    xp = jnp.pad(x, ((0, 0), (CONV_WIDTH - 1, 0), (0, 0)))
    y = b
    for k in range(CONV_WIDTH):
        y = y + xp[:, k:k + S] * w[k]
    return y

def _lru_combine(c1, c2):
    a1, b1 = c1
    a2, b2 = c2
    return a1 * a2, a2 * b1 + b2

def rg_lru(xc, wa, ba, wx, bx, lam):
    B, S, _ = xc.shape
    xb = xc.reshape(B, S, N_LRU_BLOCKS, LRU_BLOCK)
    r = jax.nn.sigmoid(jnp.einsum('bsnd,nde->bsne', xb, wa).reshape(B, S, D_RNN) + ba)
    i = jax.nn.sigmoid(jnp.einsum('bsnd,nde->bsne', xb, wx).reshape(B, S, D_RNN) + bx)
    log_a = (-LRU_C * r.astype(jnp.float32)) * jax.nn.softplus(-lam.astype(jnp.float32))
    a = jnp.exp(log_a)
    b = jnp.sqrt(-jnp.expm1(2.0 * log_a)) * (i * xc).astype(jnp.float32)
    _, h = lax.associative_scan(_lru_combine, (a, b), axis=1)
    return h.astype(xc.dtype)

def compress(kv, pos, w1, w2):
    B, S, G, dh = kv.shape
    c = kv.reshape(B, S // CMP_STRIDE, CMP_STRIDE, G, dh)
    blk = jnp.concatenate([c[:, :-1], c[:, 1:]], axis=2)
    blk = blk + pos[:, None, :]
    nc = blk.shape[1]
    blk = blk.transpose(0, 1, 3, 2, 4).reshape(B, nc, G, CMP_LEN * dh)
    return jax.nn.gelu(blk @ w1) @ w2

def nsa(q, kc, vc, ks, vs, kw, vw, gates, slopes):
    B, S = q.shape[0], q.shape[1]
    G, R, dh = N_KV_GROUPS, HEADS_PER_GROUP, HEAD_DIM
    NQ = S // Q_BLOCK
    NB = S // SEL_LEN
    NC = kc.shape[1]
    topk = min(SEL_TOPK, NB)
    scale = HEAD_DIM ** -0.5
    slopes_g = slopes.reshape(G, R)[None, :, :, None, None]
    cmp_end = jnp.arange(NC) * CMP_STRIDE + (CMP_LEN - 1)
    kc_t = kc.transpose(0, 2, 1, 3)
    vc_t = vc.transpose(0, 2, 1, 3)
    ks_blk = ks.reshape(B, NB, SEL_LEN, G, dh).transpose(0, 3, 1, 2, 4)
    vs_blk = vs.reshape(B, NB, SEL_LEN, G, dh).transpose(0, 3, 1, 2, 4)
    kw_pad = jnp.pad(kw, ((0, 0), (WINDOW, 0), (0, 0), (0, 0)))
    vw_pad = jnp.pad(vw, ((0, 0), (WINDOW, 0), (0, 0), (0, 0)))
    q_blocks = q.reshape(B, NQ, Q_BLOCK, G, R, dh).transpose(1, 0, 2, 3, 4, 5)
    g_blocks = gates.reshape(B, NQ, Q_BLOCK, G, R, 3).transpose(1, 0, 2, 3, 4, 5)
    gather = jax.vmap(jax.vmap(lambda kb, idx: kb[idx]))
    blk_ids = jnp.arange(NB)

    def one_block(args):
        qb, qi, gi = args
        q0 = qb * Q_BLOCK
        t = q0 + jnp.arange(Q_BLOCK)
        qf = qi * scale
        dist_c = t[:, None] - cmp_end[None, :]
        s = jnp.einsum('bqgrd,bgcd->bgrqc', qf, kc_t) - slopes_g * dist_c
        p_cmp = masked_softmax(s, dist_c >= 0)
        o_cmp = jnp.einsum('bgrqc,bgcd->bqgrd', p_cmp.astype(vc_t.dtype), vc_t)
        imp = jnp.sum(p_cmp, axis=2)
        left = R_CMP - 1
        imp = jnp.pad(imp, ((0, 0), (0, 0), (0, 0), (left, R_SEL * NB - NC)))
        imp_slc = jnp.zeros(imp.shape[:3] + (NB,), jnp.float32)
        for m in range(R_SEL):
            for n in range(R_CMP):
                st = m - n + left
                imp_slc = imp_slc + imp[..., st:st + R_SEL * NB:R_SEL]
        cur = t // SEL_LEN
        valid = blk_ids[None, :] * SEL_LEN <= t[:, None]
        forced = (blk_ids[None, :] == 0) | (blk_ids[None, :] == cur[:, None]) | (blk_ids[None, :] == cur[:, None] - 1)
        score = jnp.where(valid, imp_slc, -1.0)
        score = jnp.where(forced & valid, FORCE_SCORE, score)
        _, idx = lax.top_k(score, topk)
        k_sel = gather(ks_blk, idx).reshape(B, G, Q_BLOCK, topk * SEL_LEN, dh)
        v_sel = gather(vs_blk, idx).reshape(B, G, Q_BLOCK, topk * SEL_LEN, dh)
        pos = (idx[..., None] * SEL_LEN + jnp.arange(SEL_LEN)).reshape(B, G, Q_BLOCK, topk * SEL_LEN)
        dist_s = t[None, None, :, None] - pos
        s = jnp.einsum('bqgrd,bgqkd->bgrqk', qf, k_sel) - slopes_g * dist_s[:, :, None]
        p_sel = masked_softmax(s, (dist_s >= 0)[:, :, None])
        o_slc = jnp.einsum('bgrqk,bgqkd->bqgrd', p_sel.astype(v_sel.dtype), v_sel)
        kwin = lax.dynamic_slice_in_dim(kw_pad, q0, WINDOW + Q_BLOCK, axis=1)
        vwin = lax.dynamic_slice_in_dim(vw_pad, q0, WINDOW + Q_BLOCK, axis=1)
        pos_w = q0 - WINDOW + jnp.arange(WINDOW + Q_BLOCK)
        dist_w = t[:, None] - pos_w[None, :]
        mask_w = (dist_w >= 0) & (dist_w < WINDOW) & (pos_w[None, :] >= 0)
        s = jnp.einsum('bqgrd,bkgd->bgrqk', qf, kwin) - slopes_g * dist_w
        p_win = masked_softmax(s, mask_w)
        o_win = jnp.einsum('bgrqk,bkgd->bqgrd', p_win.astype(vwin.dtype), vwin)
        g = jax.nn.sigmoid(gi)
        return g[..., 0:1] * o_cmp + g[..., 1:2] * o_slc + g[..., 2:3] * o_win

    o = lax.map(one_block, (jnp.arange(NQ), q_blocks, g_blocks))
    return o.transpose(1, 0, 2, 3, 4, 5).reshape(B, S, D_ATTN)

def first_inputs(seed: int = 0) -> dict:
    key = jax.random.key(seed)
    ks = jax.random.split(key, 32)
    f32 = jnp.float32

    def nrm(k, shape, fan_in):
        return jax.random.normal(k, shape, f32) * (fan_in ** -0.5)

    def gain(k):
        return 1.0 + 0.05 * jax.random.normal(k, (DEPTH, D_MODEL), f32)

    u = jax.random.uniform(ks[10], (DEPTH, D_RNN), f32, minval=0.9, maxval=0.999)
    s = u ** (1.0 / LRU_C)
    lam = jnp.log(s) - jnp.log1p(-s)
    return {
        'x': jax.random.normal(ks[0], (BATCH, SEQ, D_MODEL), f32),
        'p': jax.random.normal(ks[1], (DEPTH, BATCH, SEQ, D_PLE), f32),
        'norm_mix_pre': gain(ks[2]),
        'norm_mix_post': gain(ks[3]),
        'w_in': nrm(ks[4], (DEPTH, D_MODEL, D_IN), D_MODEL),
        'conv_w': nrm(ks[5], (DEPTH, CONV_WIDTH, D_RNN), CONV_WIDTH),
        'conv_b': 0.02 * jax.random.normal(ks[6], (DEPTH, D_RNN), f32),
        'lru_wa': nrm(ks[7], (DEPTH, N_LRU_BLOCKS, LRU_BLOCK, LRU_BLOCK), LRU_BLOCK),
        'lru_ba': 0.02 * jax.random.normal(ks[8], (DEPTH, D_RNN), f32),
        'lru_wx': nrm(ks[9], (DEPTH, N_LRU_BLOCKS, LRU_BLOCK, LRU_BLOCK), LRU_BLOCK),
        'lru_bx': 0.02 * jax.random.normal(ks[11], (DEPTH, D_RNN), f32),
        'lru_lambda': lam,
        'cmp_pos_k': 0.02 * jax.random.normal(ks[12], (DEPTH, CMP_LEN, HEAD_DIM), f32),
        'cmp_pos_v': 0.02 * jax.random.normal(ks[13], (DEPTH, CMP_LEN, HEAD_DIM), f32),
        'cmp_k_w1': nrm(ks[14], (DEPTH, CMP_LEN * HEAD_DIM, CMP_HIDDEN), CMP_LEN * HEAD_DIM),
        'cmp_k_w2': nrm(ks[15], (DEPTH, CMP_HIDDEN, HEAD_DIM), CMP_HIDDEN),
        'cmp_v_w1': nrm(ks[16], (DEPTH, CMP_LEN * HEAD_DIM, CMP_HIDDEN), CMP_LEN * HEAD_DIM),
        'cmp_v_w2': nrm(ks[17], (DEPTH, CMP_HIDDEN, HEAD_DIM), CMP_HIDDEN),
        'w_out': nrm(ks[18], (DEPTH, D_MODEL, D_MODEL), D_MODEL),
        'norm_ffn_pre': gain(ks[19]),
        'norm_ffn_post': gain(ks[20]),
        'ffn_w_gate_up': nrm(ks[21], (DEPTH, D_MODEL, 2 * D_FF), D_MODEL),
        'ffn_w_down': nrm(ks[22], (DEPTH, D_FF, D_MODEL), D_FF),
        'ple_w_proj': nrm(ks[23], (DEPTH, D_PLE, D_MODEL), D_PLE),
        'ple_w_gate': nrm(ks[24], (DEPTH, D_MODEL, D_MODEL), D_MODEL),
        'ple_b_gate': 0.02 * jax.random.normal(ks[25], (DEPTH, D_MODEL), f32),
    }

def first_block(x, p, norm_mix_pre, norm_mix_post, w_in, conv_w, conv_b, lru_wa, lru_ba, lru_wx, lru_bx,
              lru_lambda, cmp_pos_k, cmp_pos_v, cmp_k_w1, cmp_k_w2, cmp_v_w1, cmp_v_w2, w_out,
              norm_ffn_pre, norm_ffn_post, ffn_w_gate_up, ffn_w_down, ple_w_proj, ple_w_gate, ple_b_gate):
    B, S, _ = x.shape
    slopes = alibi_slopes()
    for i in range(DEPTH):
        h = rmsnorm(x, norm_mix_pre[i])
        z = h @ w_in[i]
        xr, gr, q, kc, vc, ksl, vsl, kw, vw, g_nsa, gm_rnn, gm_attn = jnp.split(z, IN_SPLITS, axis=-1)
        xr = causal_conv(xr, conv_w[i], conv_b[i])
        y_rnn = rg_lru(xr, lru_wa[i], lru_ba[i], lru_wx[i], lru_bx[i], lru_lambda[i]) * jax.nn.gelu(gr)
        kv_shape = (B, S, N_KV_GROUPS, HEAD_DIM)
        kc_c = compress(kc.reshape(kv_shape), cmp_pos_k[i], cmp_k_w1[i], cmp_k_w2[i])
        vc_c = compress(vc.reshape(kv_shape), cmp_pos_v[i], cmp_v_w1[i], cmp_v_w2[i])
        y_attn = nsa(q, kc_c, vc_c, ksl.reshape(kv_shape), vsl.reshape(kv_shape),
                     kw.reshape(kv_shape), vw.reshape(kv_shape), g_nsa, slopes)
        y = jax.nn.sigmoid(gm_rnn) * y_rnn + jax.nn.sigmoid(gm_attn) * y_attn
        x = x + rmsnorm(y @ w_out[i], norm_mix_post[i])
        h = rmsnorm(x, norm_ffn_pre[i])
        gate, up = jnp.split(h @ ffn_w_gate_up[i], 2, axis=-1)
        x = x + rmsnorm((jax.nn.silu(gate) * up) @ ffn_w_down[i], norm_ffn_post[i])
        x = x + jax.nn.sigmoid(x @ ple_w_gate[i] + ple_b_gate[i]) * (p[i] @ ple_w_proj[i])
    return x


DEPTH_2 = 2

N_MEM = 256
MIX_WIDTH = D_MODEL
N_GROUPS = 4
GROUP_WIDTH = MIX_WIDTH // N_GROUPS
CONF_WIDTH = 31
HG_HEADS = 4
HG_DK = GROUP_WIDTH // HG_HEADS
HG_DV = GROUP_WIDTH // HG_HEADS
HG_CHUNK = 64
SC_WIDTH = 3
MLA_HEADS = 4
MLA_NOPE = 64
MLA_ROPE = 32
MLA_V = GROUP_WIDTH // MLA_HEADS
MLA_Q_LORA = 256
MLA_KV_LORA = 128
ROPE_BASE = 10000.0
Q_BLOCK_2 = 128
XA_HEADS = 4
XA_HEAD_DIM = 64
D_FF_2 = -(-8 * D_MODEL // (3 * 256)) * 256
EPS = 1e-6
A_COLS = 2 * GROUP_WIDTH
B_COLS = 5 * GROUP_WIDTH
C_COLS = 3 * GROUP_WIDTH
D_COLS = MLA_Q_LORA + MLA_KV_LORA + MLA_ROPE
IN_COLS = A_COLS + B_COLS + C_COLS + D_COLS
SPLITS = [A_COLS, A_COLS + B_COLS, A_COLS + B_COLS + C_COLS]


def rms_norm(x, g):
    xf = x.astype(jnp.float32)
    y = xf * lax.rsqrt(jnp.mean(xf * xf, axis=-1, keepdims=True) + EPS)
    return (y * g.astype(jnp.float32)).astype(x.dtype)

def layer_norm(x, g, b):
    xf = x.astype(jnp.float32)
    mu = jnp.mean(xf, axis=-1, keepdims=True)
    xc = xf - mu
    y = xc * lax.rsqrt(jnp.mean(xc * xc, axis=-1, keepdims=True) + EPS)
    return (y * g.astype(jnp.float32) + b.astype(jnp.float32)).astype(x.dtype)

def depthwise_conv(x, w, b):
    c = x.shape[-1]
    y = lax.conv_general_dilated(x, w[:, None, :].astype(x.dtype), window_strides=(1,),
                                 padding='SAME', dimension_numbers=('NWC', 'WIO', 'NWC'),
                                 feature_group_count=c)
    return y + b.astype(x.dtype)

def rope_tables(positions):
    inv = ROPE_BASE ** (-jnp.arange(0, MLA_ROPE, 2, dtype=jnp.float32) / MLA_ROPE)
    ang = positions.astype(jnp.float32)[..., None] * inv
    return jnp.cos(ang)[:, :, None, :], jnp.sin(ang)[:, :, None, :]

def apply_rope(x, cos, sin):
    x1, x2 = jnp.split(x, 2, axis=-1)
    return jnp.concatenate([x1 * cos - x2 * sin, x2 * cos + x1 * sin], axis=-1).astype(x.dtype)

def blocked_attention(q, k, v):
    b, s, h, d = q.shape
    scale = d ** -0.5
    qb = q.reshape(b, s // Q_BLOCK_2, Q_BLOCK_2, h, d).transpose(1, 0, 2, 3, 4)

    def one_block(qblk):
        sc = jnp.einsum('bqhd,bkhd->bhqk', qblk, k).astype(jnp.float32) * scale
        p = jax.nn.softmax(sc, axis=-1)
        return jnp.einsum('bhqk,bkhe->bqhe', p.astype(v.dtype), v)

    out = lax.map(one_block, qb)
    return out.transpose(1, 0, 2, 3, 4).reshape(b, s, h, v.shape[-1])

def conformer_conv(ua, dw_w, dw_b, ln_g, ln_b):
    a, gate = jnp.split(ua, 2, axis=-1)
    h = a * jax.nn.sigmoid(gate)
    h = depthwise_conv(h, dw_w, dw_b)
    h = layer_norm(h, ln_g, ln_b)
    return jax.nn.silu(h)

def hgrn2_bidir(ub, lb_fwd, lb_bwd, onorm_g):
    b, s, _ = ub.shape
    f32 = jnp.float32
    q, zf, zb, v, g = jnp.split(ub, 5, axis=-1)

    def log_forget(z, lb):
        zf32 = z.astype(f32)
        return jnp.log(jax.nn.sigmoid(zf32) + lb * jax.nn.sigmoid(-zf32))

    rev = lambda t: t[:, ::-1]
    logf = jnp.stack([log_forget(zf, lb_fwd), log_forget(rev(zb), lb_bwd)])
    qd = jnp.stack([q, rev(q)]).astype(f32)
    vd = jnp.stack([v, rev(v)]).astype(f32)
    n_chunks = s // HG_CHUNK

    def to_chunks(t, d):
        return t.reshape(2, b, n_chunks, HG_CHUNK, HG_HEADS, d).transpose(2, 0, 1, 4, 3, 5)

    mask = jnp.tril(jnp.ones((HG_CHUNK, HG_CHUNK), dtype=f32))[..., None]

    def step(state, inp):
        qc, lfc, vc = inp
        bcum = jnp.cumsum(lfc, axis=-2)
        kc = -jnp.expm1(lfc)
        o_inter = jnp.einsum('zbhcd,zbhde->zbhce', qc * jnp.exp(bcum), state)
        diff = bcum[..., :, None, :] - bcum[..., None, :, :]
        decay = jnp.exp(diff * mask) * mask
        attn = jnp.sum(qc[..., :, None, :] * kc[..., None, :, :] * decay, axis=-1)
        o_intra = jnp.einsum('zbhts,zbhse->zbhte', attn, vc)
        blast = bcum[..., -1:, :]
        new_state = jnp.exp(blast[..., 0, :])[..., :, None] * state + \
            jnp.einsum('zbhsd,zbhse->zbhde', kc * jnp.exp(blast - bcum), vc)
        return new_state, o_inter + o_intra

    init = jnp.zeros((2, b, HG_HEADS, HG_DK, HG_DV), f32)
    _, ys = lax.scan(step, init, (to_chunks(qd, HG_DK), to_chunks(logf, HG_DK), to_chunks(vd, HG_DV)))
    ys = ys.transpose(1, 2, 0, 4, 3, 5).reshape(2, b, s, HG_HEADS, HG_DV)
    o = ys[0] + ys[1][:, ::-1]
    o = rms_norm(o, onorm_g.reshape(HG_HEADS, HG_DV)) * \
        jax.nn.silu(g.astype(f32)).reshape(b, s, HG_HEADS, HG_DV)
    return o.reshape(b, s, GROUP_WIDTH).astype(ub.dtype)

def short_gated_conv(uc, dw_w, dw_b):
    gb, gc, xin = jnp.split(uc, 3, axis=-1)
    return gb * depthwise_conv(gc * xin, dw_w, dw_b)

def mla(ud, cos, sin, qa_g, wuq, kva_g, wukv, qn_g, kn_g):
    b, s, _ = ud.shape
    cq, ckv, kr = jnp.split(ud, [MLA_Q_LORA, MLA_Q_LORA + MLA_KV_LORA], axis=-1)
    q = (rms_norm(cq, qa_g) @ wuq).reshape(b, s, MLA_HEADS, MLA_NOPE + MLA_ROPE)
    kv = (rms_norm(ckv, kva_g) @ wukv).reshape(b, s, MLA_HEADS, MLA_NOPE + MLA_V)
    k_nope, v = jnp.split(kv, [MLA_NOPE], axis=-1)
    k = jnp.concatenate([k_nope, jnp.broadcast_to(kr[:, :, None, :], (b, s, MLA_HEADS, MLA_ROPE))], axis=-1)
    q = rms_norm(q, qn_g)
    k = rms_norm(k, kn_g)
    q = jnp.concatenate([q[..., :MLA_NOPE], apply_rope(q[..., MLA_NOPE:], cos, sin)], axis=-1)
    k = jnp.concatenate([k[..., :MLA_NOPE], apply_rope(k[..., MLA_NOPE:], cos, sin)], axis=-1)
    return blocked_attention(q, k, v).reshape(b, s, MLA_HEADS * MLA_V)

def second_inputs(seed: int = 0) -> dict:
    key = jax.random.key(seed)
    ks = iter(jax.random.split(key, 40))
    L = DEPTH_2
    f32 = jnp.float32

    def nrm(shape, fan_in):
        return jax.random.normal(next(ks), shape, f32) * fan_in ** -0.5

    def gain(shape):
        return 1.0 + 0.01 * jax.random.normal(next(ks), shape, f32)

    def bias(shape):
        return 0.01 * jax.random.normal(next(ks), shape, f32)

    x = jax.random.normal(next(ks), (BATCH, SEQ, D_MODEL), f32)
    mem = jax.random.normal(next(ks), (BATCH, N_MEM, D_MODEL), f32)
    positions = jnp.arange(SEQ, dtype=jnp.int32)[None, :] + \
        jax.random.randint(next(ks), (BATCH, 1), 0, 1024, dtype=jnp.int32)
    return {
        "x": x,
        "mem": mem,
        "positions": positions,
        "g_mix": gain((L, D_MODEL)),
        "w_in": nrm((L, D_MODEL, IN_COLS), D_MODEL),
        "a_dw_w": nrm((L, CONF_WIDTH, GROUP_WIDTH), CONF_WIDTH),
        "a_dw_b": bias((L, GROUP_WIDTH)),
        "a_ln_g": gain((L, GROUP_WIDTH)),
        "a_ln_b": bias((L, GROUP_WIDTH)),
        "h_gamma": 0.5 * jax.random.normal(next(ks), (2, L, GROUP_WIDTH), f32),
        "h_onorm_g": gain((L, GROUP_WIDTH)),
        "c_dw_w": nrm((L, SC_WIDTH, GROUP_WIDTH), SC_WIDTH),
        "c_dw_b": bias((L, GROUP_WIDTH)),
        "m_qa_g": gain((L, MLA_Q_LORA)),
        "m_wuq": nrm((L, MLA_Q_LORA, MLA_HEADS * (MLA_NOPE + MLA_ROPE)), MLA_Q_LORA),
        "m_kva_g": gain((L, MLA_KV_LORA)),
        "m_wukv": nrm((L, MLA_KV_LORA, MLA_HEADS * (MLA_NOPE + MLA_V)), MLA_KV_LORA),
        "m_qn_g": gain((L, MLA_NOPE + MLA_ROPE)),
        "m_kn_g": gain((L, MLA_NOPE + MLA_ROPE)),
        "g_branch": gain((L, MIX_WIDTH)),
        "w_out": nrm((L, MIX_WIDTH, D_MODEL), MIX_WIDTH),
        "g_xq": gain((L, D_MODEL)),
        "g_mem": gain((L, D_MODEL)),
        "x_wq": nrm((L, D_MODEL, XA_HEADS * XA_HEAD_DIM), D_MODEL),
        "x_wkv": nrm((L, D_MODEL, 2 * XA_HEADS * XA_HEAD_DIM), D_MODEL),
        "x_qn_g": gain((L, XA_HEAD_DIM)),
        "x_kn_g": gain((L, XA_HEAD_DIM)),
        "x_wo": nrm((L, XA_HEADS * XA_HEAD_DIM, D_MODEL), XA_HEADS * XA_HEAD_DIM),
        "g_ffn": gain((L, D_MODEL)),
        "f_w13": nrm((L, D_MODEL, 2 * D_FF_2), D_MODEL),
        "f_w2": nrm((L, D_FF_2, D_MODEL), D_FF_2),
    }

def second_block(x, mem, positions, g_mix, w_in, a_dw_w, a_dw_b, a_ln_g, a_ln_b, h_gamma, h_onorm_g,
              c_dw_w, c_dw_b, m_qa_g, m_wuq, m_kva_g, m_wukv, m_qn_g, m_kn_g, g_branch, w_out,
              g_xq, g_mem, x_wq, x_wkv, x_qn_g, x_kn_g, x_wo, g_ffn, f_w13, f_w2):
    b, s, _ = x.shape
    n_mem = mem.shape[1]
    cos, sin = rope_tables(positions)
    p = jax.nn.softmax(h_gamma.astype(jnp.float32), axis=1)
    lower = jnp.cumsum(p, axis=1) - p[:, :1]
    for l in range(DEPTH_2):
        n = rms_norm(x, g_mix[l])
        u = n @ w_in[l]
        ua, ub, uc, ud = jnp.split(u, SPLITS, axis=-1)
        y_a = conformer_conv(ua, a_dw_w[l], a_dw_b[l], a_ln_g[l], a_ln_b[l])
        y_b = hgrn2_bidir(ub, lower[0, l], lower[1, l], h_onorm_g[l])
        y_c = short_gated_conv(uc, c_dw_w[l], c_dw_b[l])
        y_d = mla(ud, cos, sin, m_qa_g[l], m_wuq[l], m_kva_g[l], m_wukv[l], m_qn_g[l], m_kn_g[l])
        cat = jnp.concatenate([y_a, y_b, y_c, y_d], axis=-1).reshape(b, s, N_GROUPS, GROUP_WIDTH)
        cat = rms_norm(cat, g_branch[l].reshape(N_GROUPS, GROUP_WIDTH)).reshape(b, s, MIX_WIDTH)
        x = x + cat @ w_out[l]
        hq = rms_norm(x, g_xq[l])
        mn = rms_norm(mem, g_mem[l])
        q = (hq @ x_wq[l]).reshape(b, s, XA_HEADS, XA_HEAD_DIM)
        kv = (mn @ x_wkv[l]).reshape(b, n_mem, XA_HEADS, 2 * XA_HEAD_DIM)
        k, v = jnp.split(kv, 2, axis=-1)
        q = rms_norm(q, x_qn_g[l])
        k = rms_norm(k, x_kn_g[l])
        o = blocked_attention(q, k, v).reshape(b, s, XA_HEADS * XA_HEAD_DIM)
        x = x + o @ x_wo[l]
        h = rms_norm(x, g_ffn[l])
        a1, a3 = jnp.split(h @ f_w13[l], 2, axis=-1)
        x = x + (jax.nn.silu(a1) * a3) @ f_w2[l]
    return x


def setup_inputs(seed=0):
    out = dict(first_inputs(seed))
    for name, value in second_inputs(seed + 1).items():
        if name != "x":
            out[name + "_2"] = value
    return out


def reference(
    x, p, norm_mix_pre, norm_mix_post, w_in, conv_w, conv_b, lru_wa, lru_ba, lru_wx, lru_bx,
    lru_lambda, cmp_pos_k, cmp_pos_v, cmp_k_w1, cmp_k_w2, cmp_v_w1, cmp_v_w2, w_out,
    norm_ffn_pre, norm_ffn_post, ffn_w_gate_up, ffn_w_down, ple_w_proj, ple_w_gate, ple_b_gate,
    mem_2, positions_2, g_mix_2, w_in_2, a_dw_w_2, a_dw_b_2, a_ln_g_2, a_ln_b_2, h_gamma_2,
    h_onorm_g_2, c_dw_w_2, c_dw_b_2, m_qa_g_2, m_wuq_2, m_kva_g_2, m_wukv_2, m_qn_g_2, m_kn_g_2,
    g_branch_2, w_out_2, g_xq_2, g_mem_2, x_wq_2, x_wkv_2, x_qn_g_2, x_kn_g_2, x_wo_2, g_ffn_2,
    f_w13_2, f_w2_2,
):
    x = first_block(
        x, p, norm_mix_pre, norm_mix_post, w_in, conv_w, conv_b, lru_wa, lru_ba, lru_wx, lru_bx,
        lru_lambda, cmp_pos_k, cmp_pos_v, cmp_k_w1, cmp_k_w2, cmp_v_w1, cmp_v_w2, w_out,
        norm_ffn_pre, norm_ffn_post, ffn_w_gate_up, ffn_w_down, ple_w_proj, ple_w_gate,
        ple_b_gate,
    )
    return second_block(
        x, mem_2, positions_2, g_mix_2, w_in_2, a_dw_w_2, a_dw_b_2, a_ln_g_2, a_ln_b_2,
        h_gamma_2, h_onorm_g_2, c_dw_w_2, c_dw_b_2, m_qa_g_2, m_wuq_2, m_kva_g_2, m_wukv_2,
        m_qn_g_2, m_kn_g_2, g_branch_2, w_out_2, g_xq_2, g_mem_2, x_wq_2, x_wkv_2, x_qn_g_2,
        x_kn_g_2, x_wo_2, g_ffn_2, f_w13_2, f_w2_2,
    )


_drawn_inputs = setup_inputs


def setup_inputs(seed=0):
    import zlib

    import numpy as np

    out = dict(_drawn_inputs(seed))
    spreads = {}
    factors = {'lru_ba': 8.0,
     'lru_bx': 8.0,
     'cmp_pos_k': 8.0,
     'cmp_pos_v': 3.918,
     'ple_b_gate': 8.0,
     'g_mix_2': 4.815,
     'a_dw_b_2': 7.576,
     'a_ln_g_2': 8.0,
     'a_ln_b_2': 8.0,
     'h_onorm_g_2': 8.0,
     'c_dw_b_2': 8.0,
     'm_qa_g_2': 8.0,
     'm_kva_g_2': 8.0,
     'm_qn_g_2': 8.0,
     'm_kn_g_2': 8.0,
     'g_branch_2': 7.464,
     'g_xq_2': 8.0,
     'g_mem_2': 8.0,
     'x_qn_g_2': 8.0,
     'x_kn_g_2': 8.0,
     'g_ffn_2': 8.0}
    for name, (base, spread) in spreads.items():
        noise = np.random.default_rng([zlib.crc32(name.encode()), seed]).standard_normal(out[name].shape)
        drawn = base * np.exp(spread * noise) if base else spread * noise
        out[name] = jnp.asarray(drawn.astype(out[name].dtype))
    for name, factor in factors.items():
        out[name] = (out[name] * factor).astype(out[name].dtype)
    return out
```

```python
from contextlib import ExitStack

import numpy as np
import concourse.bass as bass
from concourse import mybir

F32 = mybir.dt.float32
I32 = mybir.dt.int32
ALU = mybir.AluOpType
ACT = mybir.ActivationFunctionType
AX = mybir.AxisListType

P = 128
S = 512
D = 1024
KT = D // P
TT = S // P
HEADS = 16
HD = 64
FF = 2816
FT = FF // P
CC = 32
EPS = 1e-6
BIG = 1e30
SLOTS = 4
CH = 1024


def table(fields):
    at, out = 0, {}
    for name, n in fields:
        out[name] = (at, n)
        at += n
    return out, at


CONST_FIELDS = [("ident", 128), ("ones", 128), ("halves", 128), ("dist", 512), ("zeros", 512),
                ("cmp_dist", TT * CC), ("cmp_neg", TT * CC), ("slopes", HEADS), ("eps", 1),
                ("rot", 96), ("inv_freq", 1), ("rope_row", 1), ("levels", 7 * 128)]
CONST, NCONST = table(CONST_FIELDS)
PAR1_FIELDS = [("mix_pre", KT), ("mix_post", KT), ("ffn_pre", KT), ("ffn_post", KT), ("conv_w", 4 * KT),
               ("conv_b", KT), ("ba", KT), ("bx", KT), ("lam", KT), ("ple_b", KT), ("wa", KT * P),
               ("wx", KT * P), ("w2k", 2 * P), ("w2v", 2 * HD), ("pos_k", 16), ("pos_v", 16),
               ("w_gate", KT * 48)]
PAR1, NPAR1 = table(PAR1_FIELDS)

PAR2_FIELDS = [("g_mix", KT), ("a_dw_w", 31 * 2), ("a_dw_b", 2), ("a_ln_g", 2), ("a_ln_b", 2), ("h_onorm", 2),
               ("c_dw_w", 3 * 2), ("c_dw_b", 2), ("qa", 2), ("kva", 1), ("qn", 1), ("kn", 1), ("g_branch", KT),
               ("g_xq", KT), ("g_mem", KT), ("x_qn", 1), ("x_kn", 1), ("g_ffn", KT)]
PAR2, NPAR2 = table(PAR2_FIELDS)

R_XR, R_GR, R_CMP_IN, R_KK, R_V, R_Q, R_GMR, R_GMA, R_W1K, R_W1V, R_WOUT = 0, 2, 4, 5, 6, 7, 9, 11, 13, 14, 15
R_FFN, R_DOWN, R_PLEG, R_PLEP = 17, 28, 34, 36
ROUNDS1 = 37
M_XR, M_GR, M_CMP_IN, M_KK, M_Q, M_GMR, M_GMA, M_W1K, M_W1V, M_WOUT = 0, 4, 8, 10, 12, 16, 20, 24, 25, 26
M_FFN, M_DOWN, M_PLEG, M_PLEP = 30, 52, 56, 60
PAIRS1 = 64
L_A, L_Z, L_QG, L_VCQ, L_KVX, L_C, L_UP, L_XKV, L_WOUT, L_XQO, L_FFN, L_DOWN = 0, 1, 2, 3, 4, 5, 6, 7, 8, 10, 11, 22
ROUNDS2 = 28
N_A, N_Z, N_QG, N_CQ, N_KVX, N_C, N_UQ, N_UK, N_UV, N_XK, N_WOUT, N_XQ, N_XO, N_FFN, N_DOWN = (
    0, 2, 4, 6, 7, 9, 11, 13, 15, 16, 17, 21, 22, 26, 48)
PAIRS2 = 52
JOBS = {}
for _name, _n in [("mix", 8), ("o0", 1), ("o1", 1), ("ln", 2), ("bA", 2), ("bB", 2), ("bC", 2), ("qa", 2), ("kva", 1),
                  *[(f"hd{i}", 1) for i in range(8)], ("bD", 2), ("mem", 8), ("xk0", 1), ("xk1", 1), ("xq", 8),
                  ("xh0", 1), ("xh1", 1), ("ffn", 8)]:
    JOBS[_name] = (len(JOBS), sum(n for _, _, n in JOBS.values()), _n)
NJOBS, NSQ2 = len(JOBS), 60
NM = 256
LAYERS = 2
HLEV = 9


def program(nc, wstream, const_d, par1_d, xT, pT, par2_d, gamma_d, memT, pos_d, out):
    with ExitStack() as ctx:
        top = [0]

        def sb(name, n):
            return ctx.enter_context(nc.sbuf_tensor(name, [P, n], F32))

        def sem(name):
            return ctx.enter_context(nc.semaphore(name))

        X = sb("X", KT * S)[:, :].rearrange("p (k n) -> p k n", k=KT)
        H = sb("H", KT * S)[:, :].rearrange("p (k n) -> p k n", k=KT)
        W = sb("W", SLOTS * CH)[:, :].rearrange("p (s n) -> p s n", s=SLOTS)
        CT = sb("CT", NCONST)
        PT1 = sb("PT1", NPAR1)
        WORK = sb("WORK", 34208)
        rstd = sb("rstd", S)[:, :]
        small = sb("small", 416)

        def c(name, a=0, b=None):
            at, n = CONST[name]
            return CT[:, at + a:at + (n if b is None else b)]

        def p1(name, a=0, b=None):
            at, n = PAR1[name]
            return PT1[:, at + a:at + (n if b is None else b)]

        def area(at, *shape):
            n = int(np.prod(shape))
            ap = WORK[:, at:at + n]
            if len(shape) == 2:
                return ap.rearrange("p (a b) -> p a b", a=shape[0])
            if len(shape) == 3:
                return ap.rearrange("p (a b c) -> p a b c", a=shape[0], b=shape[1])
            return ap

        ident = c("ident")
        ones = c("ones")

        G = area(0, KT, S)
        XR = area(4096, KT, 515)
        GA = area(4096, KT, S)
        Q = area(8216, KT, S)
        KK = area(12312, 4, S)
        KST = area(14360, 4, 2, 256)
        CB = area(14360, TT, HEADS, CC)
        KCD = area(16408, 2, 4, 256)
        K2 = area(18456, 16, 4, CC)
        V = area(20504, TT, S)
        YAT = area(22552, TT, D)
        T0 = 26648
        tmp = [area(T0 + i * S, S) for i in range(12)]
        VBD = area(T0 + 12 * S, 4, 256)
        ACTB = area(4096, FT, S)
        PP = area(0, 2, S)
        SQ = [tmp[10], tmp[11]]
        SG = [tmp[8], tmp[9]]
        GT = small[:, 0:192].rearrange("p (b h t) -> p b h t", b=3, h=HEADS)
        lru = small[:, 192:192 + 8 * KT].rearrange("p (f k) -> p f k", f=8)
        den = small[:, 256:256 + 64]
        sml = small[:, 320:416]
        KCT = area(T0 + 14 * S, 4 * CC)
        HK = area(T0 + 14 * S + 128, 2, 128)

        B = [ctx.enter_context(nc.psum_tensor(f"B{i}", [P, 512], F32)) for i in range(8)]

        const_in = sem("const_in")
        x_in = sem("x_in")
        p_in = sem("p_in")
        w_loaded = [sem(f"w_loaded{s}") for s in range(SLOTS)]
        chunk_done = sem("chunk_done")
        evac = [sem("evac0"), sem("evac1")]
        sq_full = sem("sq_full")
        sq_used = sem("sq_used")
        rstd_done = sem("rstd_done")
        h_done = sem("h_done")
        x_done = sem("x_done")
        pad_done = sem("pad_done")
        coef_done = sem("coef_done")
        coef_e = sem("coef_e")
        conv_done = sem("conv_done")
        gate_full = sem("gate_full")
        gate_read = sem("gate_read")
        lru_a = sem("lru_a")
        lru_t = sem("lru_t")
        lru_sqrt = sem("lru_sqrt")
        lru_y = sem("lru_y")
        v_evac = sem("v_evac")
        g_full = sem("g_full")
        g_evac = sem("g_evac")
        shuffled = sem("shuffled")
        k2_done = sem("k2_done")
        part_full = sem("part_full")
        kv2_full = sem("kv2_full")
        kv2_done = sem("kv2_done")
        cb_done = sem("cb_done")
        cs_full = sem("cs_full")
        cs_m = sem("cs_m")
        cs_e = sem("cs_e")
        cs_p = sem("cs_p")
        ct_full = sem("ct_full")
        ct_done = sem("ct_done")
        co_full = sem("co_full")
        co_done = sem("co_done")
        q_cur = sem("q_cur")
        sd_done = sem("sd_done")
        qk_full = sem("qk_full")
        sc_done = sem("sc_done")
        exp_done = sem("exp_done")
        tr_full = sem("tr_full")
        pt_act = sem("pt_act")
        pt_dve = sem("pt_dve")
        pv_full = sem("pv_full")
        o_done = sem("o_done")
        o_added = sem("o_added")
        yt_full = sem("yt_full")
        yt_done = sem("yt_done")
        out_done = sem("out_done")

        SIN, COS = area(0, S), area(S, S)
        MEM = area(1024, KT, NM)
        CAT = area(3072, KT, S)
        AH = area(7168, 2, 542)
        KF = area(8256, 2, 2, S)
        QH = area(10304, 2, S)
        GG = area(11328, 2, S)
        VH = area(12352, TT, 256)
        AD = area(13376, 2, TT, 2 * P)
        AO7 = area(15424, 4, TT, P)
        AO8 = area(17472, 4, TT, 256)
        PS = area(21568, 4, 2 * S)
        T1 = 25664
        tm2 = [area(T1 + i * S, S) for i in range(16)]
        QC = [area(T1 + i * 1024, 2 * S) for i in range(2)]
        KC = [area(T1 + 2048 + i * 1024, 2 * S) for i in range(2)]
        CQ = area(T1 + 4096, 2, S)
        CKV, KR = tm2[10], tm2[11]
        HS = [tm2[12], tm2[13]]
        QM = area(8256, 4, S)
        KM = area(10304, 4, S)
        VM = area(12352, TT, 256)
        OM = area(13376, TT, 256)
        MN = area(14400, KT, NM)
        XK = area(16448, 2, NM)
        XV = area(16960, 2, 256)
        XQ = area(17472, 2, S)
        OX = area(18496, TT, 256)
        OXT = area(19520, 2, S)
        RB = area(20544, S)
        AC2 = area(8256, FT, S)
        PALL = PT1[:, 0:LAYERS * NPAR2].rearrange("p (l n) -> p l n", l=LAYERS)
        PCUR = PT1[:, 300:300 + NPAR2]
        GAM = PT1[:, 440:448].rearrange("p (l n) -> p l n", l=2)
        LBS = PT1[:, 448:496].rearrange("p (f l n) -> p f l n", f=6, l=2)
        LBC = PT1[:, 496:504].rearrange("p (f n) -> p f n", f=2)
        GCX = PT1[:, 512:512 + 2 * 514].rearrange("p (a n) -> p a n", a=2)
        GB = PT1[:, 1600:1600 + 2 * S].rearrange("p (a n) -> p a n", a=2)

        def p2(name, a=0, b=None):
            at, n = PAR2[name]
            return PCUR[:, at + a:at + (n if b is None else b)]

        par2_in = sem("par2_in")
        mem_in = sem("mem_in")
        pos_in = sem("pos_in")
        rope_arg = sem("rope_arg")
        rope_done = sem("rope_done")
        gam_e = sem("gam_e")
        lb_done = sem("lb_done")
        cur_done = sem("cur_done")
        ap_done = sem("ap_done")
        h2_done = sem("h2_done")
        ah_done = sem("ah_done")
        edge_done = sem("edge_done")
        kf_done = sem("kf_done")
        hg_qk = sem("hg_qk")
        hg_up = sem("hg_up")
        hg_ps = sem("hg_ps")
        hg_mg = sem("hg_mg")
        hg_ev = sem("hg_ev")
        vh_evac = sem("vh_evac")
        vh_full = sem("vh_full")
        o_full = sem("o_full")
        oc_done = sem("oc_done")
        mean_full = sem("mean_full")
        cen_done = sem("cen_done")
        silu_in = sem("silu_in")
        cat_done = sem("cat_done")
        kr_done = sem("kr_done")
        rot_full = sem("rot_full")
        rope_t = sem("rope_t")
        qk_ready = sem("qk_ready")
        ot_full = sem("ot_full")
        ot_done = sem("ot_done")
        mn_done = sem("mn_done")
        xv_full = sem("xv_full")
        xv_done = sem("xv_done")
        layer_end = sem("layer_end")

        block = ctx.enter_context(nc.Block())

        def head(j, r, half):
            return 8 * j + 4 * half + r

        def n_act(n):
            return 2 * (n // 4) + min(n % 4, 2)

        def n_dve(n):
            return 2 * (n // 4) + max(n % 4 - 2, 0)

        def waits(eng, *them):
            them = [(sm, v if isinstance(v, int) else eng.to_reg(v)) for sm, v in them]
            eng.wait_ge(const_in, 32)
            for sm, v in them:
                eng.wait_ge(sm, v)

        @block.sync
        def _(sp):
            sp.dma_start(X, xT.rearrange("(k p) n -> p k n", p=P)).then_inc(x_in, 16)
            sp.dma_start(CT[:, :], const_d).then_inc(const_in, 16)
            sp.dma_start(PT1[:, :], par1_d).then_inc(const_in, 16)
            with sp.Fori(0, wstream.shape[0] // SLOTS) as i:
                for s in range(SLOTS):
                    sp.wait_ge(chunk_done, i * SLOTS + s + 1)
                    sp.dma_start(W[:, s, :], wstream[bass.ds(i * SLOTS + s, 1), :, :].rearrange("o p n -> p (o n)")
                                 ).then_inc(w_loaded[s], 16)
            for s in range(SLOTS):
                sp.wait_ge(w_loaded[s], 16 * (wstream.shape[0] // SLOTS))

        @block.tensor
        def _(pe):
            pe.sem_inc(chunk_done, SLOTS)

            def chunk(rnd, s):
                pe.wait_ge(w_loaded[s], 16 * (rnd + 1))

            def bank(pair, b):
                pe.wait_ge(evac[b], pair + 1)

            def column(slot, b, rhs, n=KT, at=0):
                for k in range(n):
                    mm = pe.matmul(B[b][:, 0:rhs(k).shape[-1]], W[:, slot, at + k * P:at + (k + 1) * P], rhs(k),
                                   start=(k == 0), stop=(k == n - 1))
                return mm

            def columns(rnd, pair, rhs, first=None, after=None):
                for s in range(4):
                    chunk(rnd, s)
                    bank(pair + s // 2, s % 2)
                    for k in range(KT):
                        if s == 0 and first is not None:
                            first(k)
                        mm = pe.matmul(B[s % 2][:, :], W[:, s, k * P:(k + 1) * P], rhs(k),
                                       start=(k == 0), stop=(k == KT - 1))
                    mm.then_inc(chunk_done, 1)
                    if after is not None:
                        after(s)

            def stat(n, first, last):
                pe.wait_ge(sq_full, n + 1)
                mm = pe.matmul(B[7][:, :], ones, SQ[n % 2], start=first, stop=last)
                mm.then_inc(sq_used, 1)

            h_tile = lambda k: H[:, k, :]

            def h_first(base):
                return lambda k: pe.wait_ge(h_done, base + k + 1)

            pe.wait_ge(const_in, 32)
            for k in range(KT):
                stat(k, k == 0, k == KT - 1)
            with pe.Fori(0, 2) as i:
                columns(R_XR + i, M_XR + 2 * i, h_tile, h_first(0))
            with pe.Fori(0, 2) as i:
                columns(R_GR + i, M_GR + 2 * i, h_tile)

            def gates(t):
                pe.wait_ge(conv_done, t + 1)
                if t:
                    pe.wait_ge(gate_read, t)
                pe.matmul(B[4][:, :], p1("wa", t * P, (t + 1) * P), tmp[t % 2], start=True, stop=True)
                pe.matmul(B[5][:, :], p1("wx", t * P, (t + 1) * P), tmp[t % 2], start=True, stop=True
                          ).then_inc(gate_full, 1)

            columns(R_CMP_IN, M_CMP_IN, h_tile, after=lambda s: gates(s))
            columns(R_KK, M_KK, h_tile, after=lambda s: gates(4 + s))
            VB = [2, 3, 6, 7]
            for s in range(4):
                chunk(R_V, s)
                for t in range(TT):
                    for kk in range(2):
                        k = 2 * s + kk
                        mm = pe.matmul(B[VB[t]][:, :], H[:, k, t * P:(t + 1) * P], W[:, s, kk * S:(kk + 1) * S],
                                       start=(k == 0), stop=(k == KT - 1), skip_group_check=True)
                mm.then_inc(chunk_done, 1)
            pe.wait_ge(v_evac, 1)
            for t in range(TT):
                for k in range(KT):
                    mm = pe.matmul(B[2][:, t * 48:(t + 1) * 48], H[:, k, t * P:(t + 1) * P],
                                   p1("w_gate", k * 48, (k + 1) * 48), start=(k == 0), stop=(k == KT - 1))
            mm.then_inc(g_full, 1)
            with pe.Fori(0, 2) as i:
                columns(R_Q + i, M_Q + 2 * i, h_tile)
            with pe.Fori(0, 2) as i:
                columns(R_GMR + i, M_GMR + 2 * i, h_tile)
            with pe.Fori(0, 2) as i:
                columns(R_GMA + i, M_GMA + 2 * i, h_tile)

            for kv, (rnd, pair) in enumerate([(R_W1K, M_W1K), (R_W1V, M_W1V)]):
                pe.wait_ge(k2_done, kv + 1)
                bank(pair, 0)
                bank(pair, 1)
                for s in range(4):
                    chunk(rnd, s)
                    for jj in range(4):
                        jp = 4 * s + jj
                        for ht in range(2):
                            mm = pe.matmul(B[ht][:, 0:128], W[:, s, jj * 256 + ht * P:jj * 256 + (ht + 1) * P],
                                           K2[:, jp, :, :].rearrange("p g c -> p (g c)"),
                                           start=(jp == 0), stop=(jp == 15), skip_group_check=True)
                    mm.then_inc(chunk_done, 1)
                pe.wait_ge(evac[0], pair + 2)
                pe.wait_ge(evac[1], pair + 2)
                if kv == 0:
                    for ht in range(2):
                        mm = pe.matmul(B[3][:, 0:128], p1("w2k", ht * P, (ht + 1) * P), HK[:, ht, :],
                                       start=(ht == 0), stop=(ht == 1))
                    mm.then_inc(kv2_full, 1)
                else:
                    pe.wait_ge(g_evac, 1)
                    for g in range(4):
                        for hh in range(4):
                            for ht in range(2):
                                mm = pe.matmul(B[2][32 * hh:32 * hh + 32, g * HD:(g + 1) * HD],
                                               HK[:, ht, g * CC:(g + 1) * CC], p1("w2v", ht * HD, (ht + 1) * HD),
                                               start=(ht == 0), stop=(ht == 1), skip_group_check=True)
                    mm.then_inc(kv2_full, 1)

            pe.wait_ge(kv2_done, 2)
            for t in range(TT):
                if t:
                    pe.wait_ge(cs_m, t)
                for h in range(HEADS):
                    g = h // 4
                    half = g % 2
                    tile = 4 * (g // 2) + h % 4
                    at = (4 * (g // 2) + h % 4) * CC
                    mm = pe.matmul(B[4 + half][:, at:at + CC], Q[64 * half:64 * half + 64, tile, t * P:(t + 1) * P],
                                   KCT[64 * half:64 * half + 64, g * CC:(g + 1) * CC], start=True, stop=True)
                mm.then_inc(cs_full, 1)
                pe.wait_ge(cs_p, t + 1)
                for g in range(4):
                    mm = pe.transpose(B[6][:, g * P:(g + 1) * P], tmp[0][:, g * P:(g + 1) * P], ident)
                mm.then_inc(ct_full, 1)
                pe.wait_ge(ct_done, t + 1)
                for g in range(4):
                    mm = pe.matmul(B[2 + g // 2][:, (g % 2) * 256:(g % 2 + 1) * 256], tmp[1][:, g * P:(g + 1) * P],
                                   VBD[:, g, :], start=True, stop=True)
                mm.then_inc(co_full, 1)
                pe.wait_ge(co_done, t + 1)

            def run_attention(n, groups, pts, steps):
                def do_qk(s):
                    lhsT, rhs, kts, v = steps[s]
                    pe.wait_ge(sc_done, n + s + 1)
                    pe.matmul(B[4 + s % 2][:, 0:rhs.shape[-1]], lhsT, rhs, start=True, stop=True
                              ).then_inc(qk_full, 1)

                def do_tr(s):
                    kts = steps[s][2]
                    pe.wait_ge(exp_done, n + s + 3)
                    q = s + 2
                    e = s - 2
                    if e % 4 < 2:
                        pe.wait_ge(pt_act, pts + 2 + n_act(e) + 1)
                    else:
                        pe.wait_ge(pt_dve, pts + 2 + n_dve(e) + 1)
                    for kt in range(kts):
                        mm = pe.transpose(B[6 + s % 2][:, kt * P:(kt + 1) * P],
                                          tmp[4 + s % 2][:, kt * P:(kt + 1) * P], ident)
                    mm.then_inc(tr_full, 1)

                def do_pv(s):
                    lhsT, rhs, kts, v = steps[s]
                    if s % 4 == 0:
                        pe.wait_ge(o_done, groups + s // 4 + 1)
                    if s % 4 < 2:
                        pe.wait_ge(pt_act, pts + 2 + n_act(s) + 1)
                    else:
                        pe.wait_ge(pt_dve, pts + 2 + n_dve(s) + 1)
                    for kt in range(kts):
                        mm = pe.matmul(B[2 + (s // 4) % 2][:, (s % 4) * HD:(s % 4 + 1) * HD],
                                       tmp[6 + s % 2][:, kt * P:(kt + 1) * P], v(kt),
                                       start=(kt == 0), stop=(kt == kts - 1))
                    mm.then_inc(pv_full, 1)

                for s in range(len(steps) + 3):
                    if s < len(steps):
                        do_qk(s)
                    if 2 <= s < len(steps) + 2:
                        do_tr(s - 2)
                    if s >= 3:
                        do_pv(s - 3)

            for j in range(2):
                with pe.Fori(0, 4) as r:
                    pe.wait_ge(q_cur, r + 4 * j + 1)
                    steps = []
                    for br in range(2):
                        for half in range(2):
                            for t in range(TT):
                                h0 = 64 * half
                                steps.append((tmp[3][h0:h0 + 64, t * P:(t + 1) * P],
                                              KK[h0:h0 + 64, 2 * br + j, 0:(t + 1) * P], t + 1,
                                              lambda kt, br=br, g=2 * j + half:
                                              V[:, kt, br * 256 + g * HD:br * 256 + (g + 1) * HD]))
                    run_attention(16 * r + 64 * j, 4 * r + 16 * j, 8 * r + 32 * j, steps)

            pe.wait_ge(o_added, 4 + 32)
            for k in range(KT):
                if k >= 2:
                    pe.wait_ge(yt_done, k - 1)
                for t in range(TT):
                    mm = pe.transpose(B[4 + k % 2][:, t * P:(t + 1) * P], YAT[:, t, k * P:(k + 1) * P], ident)
                mm.then_inc(yt_full, 1)

            def out_columns(rnd, pair, nsq, rhs, first=None):
                columns(rnd, pair, rhs, first, after=lambda s: stat_loop(nsq, s))

            g_tile = lambda k: G[:, k, :]
            for i in range(2):
                columns(R_WOUT + i, M_WOUT + 2 * i, g_tile,
                        (lambda k: pe.wait_ge(yt_done, k + 1)) if i == 0 else None,
                        after=lambda s, i=i: stat(8 + 4 * i + s - 1, 4 * i + s - 1 == 0, False) if 4 * i + s else None)
            stat(15, False, True)
            for k in range(KT):
                if k == 0:
                    pe.wait_ge(rstd_done, 2)
                stat(16 + k, k == 0, k == KT - 1)
            with pe.Fori(0, FT // 2) as i:
                columns(R_FFN + i, M_FFN + 2 * i, h_tile, h_first(8))

            def down(rnd0, pair0, nsq, inside=ACTB):
                for cix in range(4):
                    bank(pair0 + cix // 2, cix % 2)
                    for q in range(3):
                        ch = 3 * cix + q
                        chunk(rnd0 + ch // 4, ch % 4)
                        for kk in range(min(KT, FT - 8 * q)):
                            k = 8 * q + kk
                            mm = pe.matmul(B[cix % 2][:, :], W[:, ch % 4, kk * P:(kk + 1) * P], inside[:, k, :],
                                           start=(k == 0), stop=(k == FT - 1))
                        mm.then_inc(chunk_done, 1)
                    if nsq is not None and cix:
                        nsq(cix - 1)
                if nsq is not None:
                    nsq(3)

            pe.wait_ge(evac[1], M_DOWN + 1)
            for i in range(2):
                down(R_DOWN + 3 * i, M_DOWN + 2 * i,
                     lambda q, i=i: stat(24 + 4 * i + q, 4 * i + q == 0, 4 * i + q == 7))
            with pe.Fori(0, 2) as i:
                columns(R_PLEG + i, M_PLEG + 2 * i, lambda k: X[:, k, :], lambda k: pe.wait_ge(x_done, 8 + k + 1))
            pe.wait_ge(p_in, 16)
            for n in range(KT):
                if n % 4 == 0:
                    chunk(R_PLEP, n // 4)
                if n == KT - 1:
                    chunk(R_PLEP, 2)
                    chunk(R_PLEP, 3)
                bank(M_PLEP + n // 2, n % 2)
                for k in range(2):
                    at = (n % 4) * 256 + k * P
                    mm = pe.matmul(B[n % 2][:, :], W[:, n // 4, at:at + P], PP[:, k, :], start=(k == 0), stop=(k == 1))
                if n == KT - 1:
                    mm.then_inc(chunk_done, 3)
                else:
                    mm.then_inc(chunk_done if n % 4 == 3 else part_full, 1)

            with pe.Fori(0, LAYERS) as l:
                R0 = ROUNDS1 + ROUNDS2 * l
                M0 = PAIRS1 + PAIRS2 * l

                def stat2(job, q, lhsT=ones, parts=P, cols=S):
                    j, sq0, n = JOBS[job]
                    if q == 0:
                        pe.wait_ge(rstd_done, 4 + NJOBS * l + j)
                    pe.wait_ge(sq_full, 32 + NSQ2 * l + sq0 + q + 1)
                    pe.matmul(B[7][0:lhsT.shape[-1], 0:cols], lhsT, HS[(sq0 + q) % 2][0:parts, 0:cols],
                              start=(q == 0), stop=(q == n - 1)).then_inc(sq_used, 1)

                def h_wait(base):
                    return lambda k: pe.wait_ge(h2_done, 24 * l + base + k + 1)

                def one(rnd, s, pair, rhs, first=None):
                    chunk(R0 + rnd, s)
                    bank(M0 + pair, s % 2)
                    for k in range(KT):
                        if first is not None:
                            first(k)
                        r = rhs(k)
                        mm = pe.matmul(B[s % 2][:, 0:r.shape[-1]], W[:, s, k * P:(k + 1) * P], r,
                                       start=(k == 0), stop=(k == KT - 1))
                    mm.then_inc(chunk_done, 1)

                for q in range(KT):
                    stat2("mix", q)
                for rnd, pair in ((L_A, N_A), (L_Z, N_Z), (L_QG, N_QG)):
                    for s in range(4):
                        one(rnd, s, pair + s // 2, h_tile, h_wait(0) if rnd == 0 and s == 0 else None)

                def hg_step(st):
                    pe.wait_ge(hg_qk, 10 * l + st + 1)
                    q = QH.rearrange("p a n -> p (a n)") if st == 0 else QC[st % 2]
                    k = KC[st % 2]
                    for hi in range(2):
                        for half in range(2):
                            bk = 2 * hi + half
                            if st:
                                pe.wait_ge(hg_mg, 32 * l + 4 * (st - 1) + bk + 1)
                            elif hi == 0 and half == 0:
                                pe.wait_ge(rstd_done, 4 + NJOBS * l + 1)
                            r = slice(64 * half, 64 * half + 64)
                            for i2 in range(2):
                                for ht in range(2):
                                    at = ht * S + (2 * hi + i2) * P
                                    mm = pe.matmul(B[4 + bk][:, (2 * i2 + ht) * P:(2 * i2 + ht + 1) * P],
                                                   k[r, at:at + P], q[r, at:at + P], start=True, stop=True)
                            mm.then_inc(hg_ps, 1)

                def chunk_of(n):
                    rnd, s = L_VCQ + n // 4, n % 4
                    if n < 2:
                        chunk(R0 + rnd, s)
                        for t in range(TT):
                            for kk in range(4):
                                k = 4 * s + kk
                                mm = pe.matmul(B[2 + t // 2][:, (t % 2) * 256:(t % 2) * 256 + 256],
                                               H[:, k, t * P:(t + 1) * P], W[:, s, kk * 256:(kk + 1) * 256],
                                               start=(k == 0 and t % 2 == 0), stop=(k == KT - 1),
                                               skip_group_check=True)
                        mm.then_inc(chunk_done, 1)
                    else:
                        one(rnd, s, {0: N_CQ, 1: N_KVX + s // 2, 2: N_C + s // 2}[n // 4], h_tile)

                for n in range(12):
                    chunk_of(n)
                    if n < 8:
                        hg_step(n)
                for st in (8, 9):
                    pe.wait_ge(hg_qk, 10 * l + st + 1)
                    q, k = QC[st % 2], KC[st % 2]
                    for ht in range(2):
                        for half in range(2):
                            r = slice(64 * half, 64 * half + 64)
                            if st == 8:
                                pe.wait_ge(hg_mg, 32 * l + 32)
                                for i in range(TT):
                                    mm = pe.matmul(B[4 + 2 * ht + half][:, i * P:(i + 1) * P],
                                                   k[r, ht * S + i * P:ht * S + (i + 1) * P],
                                                   q[r, ht * S + (i ^ 1) * P:ht * S + (i ^ 1) * P + P],
                                                   start=True, stop=True)
                                mm.then_inc(hg_ps, 1)
                            else:
                                for ii in range(2):
                                    bk = 4 + 2 * ii + half
                                    pe.wait_ge(hg_ev, 12 * l + 4 * ht + 2 * ii + half + 1)
                                    for i2 in range(2):
                                        i = 2 * ii + i2
                                        o = ht * S + (1 - ii) * 256
                                        mm = pe.matmul(B[bk][:, i2 * 256:i2 * 256 + 256],
                                                       k[r, ht * S + i * P:ht * S + (i + 1) * P], q[r, o:o + 256],
                                                       start=True, stop=True)
                                    mm.then_inc(hg_ps, 1)
                pe.wait_ge(hg_ev, 12 * l + 12)
                for ht in range(2):
                    for half in range(2):
                        hd = 2 * ht + half
                        for t in range(TT):
                            for i in range(TT):
                                if i == t:
                                    a = AD[:, half, i, ht * P:(ht + 1) * P]
                                elif i == t ^ 1:
                                    a = AO7[:, 2 * ht + half, i, :]
                                else:
                                    a = AO8[:, 2 * ht + half, i, (t % 2) * P:(t % 2 + 1) * P]
                                mm = pe.matmul(B[2 + ht][64 * half:64 * half + 64, t * P:(t + 1) * P],
                                               VH[:, i, hd * HD:(hd + 1) * HD], a, start=(i == 0), stop=(i == TT - 1))
                    mm.then_inc(o_full, 1)
                for ht in range(2):
                    stat2(f"o{ht}", 0, c("halves"))
                pe.wait_ge(ah_done, 2 * l + 2)
                for t in range(2):
                    mm = pe.matmul(B[6][:, :], ones, CAT[:, t, :], start=(t == 0), stop=(t == 1))
                mm.then_inc(mean_full, 1)
                for q in range(2):
                    stat2("ln", q)
                for job in ("bA", "bB", "bC"):
                    for q in range(2):
                        stat2(job, q)
                for q in range(2):
                    stat2("qa", q)
                stat2("kva", 0)
                chunk(R0 + L_UP, 0)
                pe.wait_ge(ap_done, NJOBS * l + JOBS["qa"][0] + 1)

                def head_rope(i):
                    stat2(f"hd{i}", 0, ones[0:96, 0:96], 96)
                    pe.wait_ge(qk_ready, 16 * l + 2 * i + 1)
                    dst = (QM if i < 4 else KM)[0:96, i % 4, :]
                    pe.matmul(B[4 + i % 2][0:96, :], c("rot")[0:96, :], dst, start=True, stop=True).then_inc(rot_full, 1)

                for i in range(8):
                    h = i % 4
                    pair = (N_UQ if i < 4 else N_UK) + h // 2
                    bank(M0 + pair, i % 2)
                    if i < 4:
                        for k in range(2):
                            mm = pe.matmul(B[i % 2][0:96, :], W[:, 0, k * 384 + h * 96:k * 384 + h * 96 + 96], CQ[:, k, :],
                                           start=(k == 0), stop=(k == 1))
                        mm.then_inc(chunk_done if i == 3 else part_full, 1)
                    else:
                        if i == 4:
                            chunk(R0 + L_UP, 1)
                            pe.wait_ge(ap_done, NJOBS * l + JOBS["kva"][0] + 1)
                        pe.matmul(B[i % 2][0:64, :], W[:, 1, h * HD:(h + 1) * HD], CKV, start=True, stop=True
                                  ).then_inc(part_full, 1)
                    if i:
                        head_rope(i - 1)
                chunk(R0 + L_UP, 2)
                chunk(R0 + L_UP, 3)
                for b in range(2):
                    bank(M0 + N_UV, b)
                    for t in range(2):
                        mm = pe.matmul(B[b][:, t * 256:(t + 1) * 256], CKV[:, (2 * b + t) * P:(2 * b + t + 1) * P],
                                       W[:, 1, 256:512], start=True, stop=True)
                    if b == 0:
                        mm.then_inc(part_full, 1)
                mm.then_inc(chunk_done, 3)
                head_rope(7)
                pe.wait_ge(qk_ready, 16 * l + 16)
                pe.wait_ge(evac[0], M0 + N_UV + 2)
                pe.wait_ge(evac[1], M0 + N_UV + 2)
                n = 128 + 32 * l
                run_attention(n, 32 + 8 * l, 64 + 16 * l,
                              [(QM[0:96, h, t * P:(t + 1) * P], KM[0:96, h, :], TT,
                                lambda kt, h=h: VM[:, kt, h * HD:(h + 1) * HD]) for h in range(4) for t in range(TT)])

                def turn(src, cnt):
                    pe.wait_ge(o_done, 2 + cnt)
                    for f in range(2):
                        for t in range(TT):
                            mm = pe.transpose(B[4 + f][:, t * P:(t + 1) * P], src[:, t, f * P:(f + 1) * P], ident)
                        mm.then_inc(ot_full, 1)

                turn(OM, 32 + 8 * l + 4)
                for q in range(2):
                    stat2("bD", q)
                for q in range(KT):
                    stat2("mem", q, cols=NM)
                for s in range(2):
                    one(L_XKV, s, N_XK, lambda k: MN[:, k, :],
                        (lambda k: pe.wait_ge(mn_done, KT * l + k + 1)) if s == 0 else None)
                for s in range(2, 4):
                    chunk(R0 + L_XKV, s)
                    for t in range(2):
                        for kk in range(4):
                            k = 4 * (s - 2) + kk
                            mm = pe.matmul(B[2 + t][:, 0:256], MN[:, k, t * P:(t + 1) * P],
                                           W[:, s, kk * 256:(kk + 1) * 256], start=(k == 0), stop=(k == KT - 1))
                    mm.then_inc(chunk_done, 1)
                for f in range(2):
                    stat2(f"xk{f}", 0, c("halves"), cols=NM)
                pe.wait_ge(ap_done, NJOBS * l + JOBS["bD"][0] + 1)
                for rnd in range(2):
                    for s in range(4):
                        one(L_WOUT + rnd, s, N_WOUT + 2 * rnd + s // 2, lambda k: CAT[:, k, :])
                for q in range(KT):
                    stat2("xq", q)
                for s in range(2):
                    one(L_XQO, s, N_XQ, h_tile, h_wait(8) if s == 0 else None)
                for f in range(2):
                    stat2(f"xh{f}", 0, c("halves"))
                pe.wait_ge(ap_done, NJOBS * l + JOBS["xh1"][0] + 1)
                pe.wait_ge(xv_done, l + 1)
                run_attention(n + 16, 36 + 8 * l, 72 + 16 * l,
                              [(XQ[64 * (h % 2):64 * (h % 2) + 64, h // 2, t * P:(t + 1) * P],
                                XK[64 * (h % 2):64 * (h % 2) + 64, h // 2, :], 2,
                                lambda kt, h=h: XV[:, kt, h * HD:(h + 1) * HD]) for h in range(4) for t in range(TT)])
                turn(OX, 36 + 8 * l + 4)
                pe.wait_ge(ot_done, 4 * l + 4)
                for i in range(KT):
                    if i % 4 == 0:
                        chunk(R0 + L_XQO, 2 + i // 4)
                    bank(M0 + N_XO + i // 2, i % 2)
                    for k in range(2):
                        at = (i % 4) * 256 + k * P
                        mm = pe.matmul(B[i % 2][:, :], W[:, 2 + i // 4, at:at + P], OXT[:, k, :],
                                       start=(k == 0), stop=(k == 1))
                    mm.then_inc(chunk_done if i % 4 == 3 else part_full, 1)
                for q in range(KT):
                    stat2("ffn", q)
                with pe.Fori(0, FT // 2) as i:
                    columns(R0 + L_FFN + i, M0 + N_FFN + 2 * i, h_tile, h_wait(16))
                pe.wait_ge(evac[1], M0 + N_DOWN + 1)
                for i in range(2):
                    down(R0 + L_DOWN + 3 * i, M0 + N_DOWN + 2 * i, None, AC2)
                pe.sem_inc(sq_used, 1)

        @block.scalar
        def _(act):
            act.sem_inc(evac[0], 1)
            act.sem_inc(exp_done, 2)
            act.sem_inc(pt_act, 2)

            def full(n):
                act.wait_ge(chunk_done, n + 1 + SLOTS)

            def square(n, src):
                act.wait_ge(sq_used, n + 1)
                act.activation(SQ[n % 2], src, ACT.Square).then_inc(sq_full, 1)

            def rstds(n):
                act.wait_ge(sq_used, 2 + KT * (n + 1))
                act.activation(rstd, B[7][:, :], ACT.Ln, bias=c("eps"), scale=1.0 / D)
                act.drain()
                act.activation(rstd, rstd, ACT.Exp, scale=-0.5).then_inc(rstd_done, 1)

            act.wait_ge(const_in, 32)
            act.wait_ge(x_in, 16)
            for k in range(KT):
                square(k, X[:, k, :])
            rstds(0)
            act.wait_ge(coef_e, 1)
            act.activation(lru[:, 1, :], lru[:, 0, :], ACT.Exp, scale=-1.0).then_inc(coef_e, 1)
            with act.Fori(0, 2) as i:
                for s in range(4):
                    full(i * 4 + s + 4 * R_XR)
                    act.activation(XR[:, bass.ds(i * 4 + s, 1), 3:515], B[s % 2][:, :].unsqueeze(1), ACT.Identity
                                   ).then_inc(evac[s % 2], 1)
            act.preload_act_table(ACT.Gelu_apprx_tanh)
            with act.Fori(0, 2) as i:
                for s in range(4):
                    full(i * 4 + s + 4 * R_GR)
                    act.activation(G[:, bass.ds(i * 4 + s, 1), :], B[s % 2][:, :].unsqueeze(1), ACT.Gelu_apprx_tanh
                                   ).then_inc(evac[s % 2], 1)

            def lru_gates(t):
                act.wait_ge(gate_full, t + 1)
                if t == 0:
                    act.wait_ge(coef_done, 1)
                if t:
                    act.wait_ge(lru_t, t)
                act.activation(tmp[2], B[4][:, :], ACT.Tanh, bias=lru[:, 5, t:t + 1], scale=0.5)
                act.activation(tmp[3], B[5][:, :], ACT.Tanh, bias=lru[:, 6, t:t + 1], scale=0.5).then_inc(gate_read, 1)
                act.drain()
                if t >= 2:
                    act.wait_ge(lru_y, t - 1)
                act.activation(tmp[4], tmp[2], ACT.Tanh, bias=lru[:, 3, t:t + 1], scale=lru[:, 3, t:t + 1])
                act.activation(tmp[5 + t % 2], tmp[2], ACT.Exp, bias=lru[:, 4, t:t + 1], scale=lru[:, 4, t:t + 1]
                               ).then_inc(lru_a, 1)

            def lru_root(t):
                act.wait_ge(lru_t, t + 1)
                act.activation(tmp[9], tmp[9], ACT.Sqrt, scale=0.25).then_inc(lru_sqrt, 1)

            for t in range(8):
                full(4 * R_CMP_IN + t)
                if t < 4:
                    act.activation(KST[:, t, :, :], B[t % 2][:, :].rearrange("p (m r) -> p r m", r=2), ACT.Identity
                                   ).then_inc(evac[t % 2], 1)
                else:
                    act.activation(KK[:, t - 4, :], B[t % 2][:, :], ACT.Identity).then_inc(evac[t % 2], 1)
                if t:
                    lru_root(t - 1)
                lru_gates(t)
            lru_root(7)
            full(4 * R_V + 3)
            for t, b in enumerate([2, 3, 6, 7]):
                a = act.activation(V[:, t, :], B[b][:, :], ACT.Identity)
            a.then_inc(v_evac, 1)
            act.wait_ge(g_full, 1)
            act.activation(GT.rearrange("p b h t -> p t h b"),
                           B[2][:, 0:192].rearrange("p (t h b) -> p t h b", t=TT, h=HEADS), ACT.Sigmoid
                           ).then_inc(g_evac, 1)
            with act.Fori(0, 2) as i:
                for s in range(4):
                    full(i * 4 + s + 4 * R_Q)
                    act.activation(Q[:, bass.ds(i * 4 + s, 1), :], B[s % 2][:, :].unsqueeze(1), ACT.Identity,
                                   scale=HD ** -0.5).then_inc(evac[s % 2], 1)
            act.preload_act_table(ACT.Sigmoid)
            for t in range(8):
                full(4 * R_GMR + t)
                if t == 0:
                    act.wait_ge(lru_y, 8)
                if t >= 2:
                    act.wait_ge(lru_y, 8 + t - 1)
                act.activation(tmp[t % 2], B[t % 2][:, :], ACT.Sigmoid).then_inc(evac[t % 2], 1)
            with act.Fori(0, 2) as i:
                for s in range(4):
                    full(i * 4 + s + 4 * R_GMA)
                    act.activation(GA[:, bass.ds(i * 4 + s, 1), :], B[s % 2][:, :].unsqueeze(1), ACT.Sigmoid
                                   ).then_inc(evac[s % 2], 1)
            for kv, rnd in enumerate([R_W1K, R_W1V]):
                full(4 * rnd + 3)
                if kv:
                    act.wait_ge(kv2_full, 1)
                for ht in range(2):
                    act.activation(HK[:, ht, :], B[ht][:, 0:128], ACT.Gelu_apprx_tanh).then_inc(evac[ht], 1)
                act.wait_ge(kv2_full, kv + 1)
                if kv == 0:
                    act.activation(KCT, B[3][:, 0:128], ACT.Identity).then_inc(kv2_done, 1)
                else:
                    act.wait_ge(k2_done, 3)
                    for hh in range(4):
                        r = slice(32 * hh, 32 * hh + 32)
                        a = act.activation(VBD[r, :, hh * HD:(hh + 1) * HD],
                                           B[2][r, 0:256].rearrange("p (g d) -> p g d", g=4), ACT.Identity)
                    a.then_inc(kv2_done, 1)
            for t in range(TT):
                act.wait_ge(cs_m, t + 1)
                act.activation(tmp[0], tmp[0], ACT.Exp).then_inc(cs_e, 1)
                act.wait_ge(ct_full, t + 1)
                act.activation(tmp[1], B[6][:, :], ACT.Identity).then_inc(ct_done, 1)

            def run_attention(n, pts, steps):
                for s in range(len(steps) + 1):
                    if s < len(steps):
                        w = steps[s]
                        act.wait_ge(sc_done, n + s + 3)
                        act.wait_ge(tr_full, n + s + 1)
                        act.activation(tmp[4 + s % 2][:, 0:w], tmp[s % 2][:, 0:w], ACT.Exp, scale=-1.0,
                                       bias=sml[:, s:s + 1], accum_out=den[:, s:s + 1]).then_inc(exp_done, 1)
                    e = s - 1
                    if s >= 1 and e % 4 < 2:
                        act.wait_ge(tr_full, n + e + 3)
                        act.wait_ge(pv_full, n + e + 1)
                        act.activation(tmp[6 + e % 2][:, 0:steps[e]], B[6 + e % 2][:, 0:steps[e]], ACT.Identity
                                       ).then_inc(pt_act, 1)

            act.preload_act_table(ACT.Exp)
            act.wait_ge(co_done, TT)
            for j in range(2):
                with act.Fori(0, 4) as r:
                    act.wait_ge(sc_done, 16 * r + 64 * j + 2)
                    act.wait_ge(sd_done, 2 * r + 8 * j + 1)
                    act.activation(tmp[3], Q[:, bass.ds(r + 4 * j, 1), :].rearrange("p o n -> p (o n)"), ACT.Identity)
                    act.activation(sml[:, 20:22], c("slopes").rearrange("p (a r) -> p a r", r=4)[
                        :, 2 * j:2 * j + 2, bass.ds(r, 1)].rearrange("p a o -> p (a o)"), ACT.Identity
                                   ).then_inc(q_cur, 1)
                    run_attention(16 * r + 64 * j, 8 * r + 32 * j, [P * (t + 1) for _ in range(4) for t in range(TT)])

            def out_tile(ch, k, nsq):
                full(ch)
                act.wait_ge(sq_used, nsq + 1)
                act.activation(SQ[nsq % 2], B[k % 2][:, :], ACT.Square).then_inc(sq_full, 1)
                act.activation(H[:, k, :], B[k % 2][:, :], ACT.Identity).then_inc(evac[k % 2], 1)

            for k in range(KT):
                out_tile(4 * R_WOUT + k, k, 8 + k)
            rstds(1)
            for k in range(KT):
                act.wait_ge(x_done, k + 1)
                square(16 + k, X[:, k, :])
            act.wait_ge(h_done, 8)
            rstds(2)
            act.preload_act_table(ACT.Silu)
            with act.Fori(0, FT // 2) as i:
                for u in range(2):
                    m = 2 * i + u + M_FFN
                    full(4 * R_FFN + 4 * i + 2 * u)
                    act.wait_ge(evac[1], m)
                    act.activation(SG[u], B[0][:, :], ACT.Silu).then_inc(evac[0], 1)
            for k in range(KT):
                out_tile(4 * R_DOWN + 3 * k + 2, k, 24 + k)
            rstds(3)
            act.preload_act_table(ACT.Sigmoid)
            for k in range(KT):
                full(4 * R_PLEG + k)
                if k == 0:
                    act.wait_ge(x_done, 2 * KT)
                act.activation(H[:, k, :], B[k % 2][:, :], ACT.Sigmoid, bias=p1("ple_b", k, k + 1)
                               ).then_inc(evac[k % 2], 1)

            act.wait_ge(rope_arg, 1)
            act.activation(SIN, SIN, ACT.Sin)
            act.activation(COS, COS, ACT.Sin).then_inc(rope_done, 1)
            act.wait_ge(gam_e, 1)
            act.activation(LBS[:, 1], LBS[:, 0], ACT.Exp).then_inc(gam_e, 1)
            with act.Fori(0, LAYERS) as l:
                R0 = 4 * ROUNDS1 + 4 * ROUNDS2 * l
                M0 = PAIRS1 + PAIRS2 * l
                act.wait_ge(lb_done, 1)
                act.wait_ge(x_done, 24)
                act.wait_ge(layer_end, l + 1)
                act.activation(PCUR, PALL[:, bass.ds(l, 1), :].rearrange("p o n -> p (o n)"), ACT.Identity)
                act.activation(LBC, LBS[:, 4:6, bass.ds(l, 1), :].rearrange("p f o n -> p f (o n)"), ACT.Identity
                               ).then_inc(cur_done, 1)

                def sq2(job, q, src, parts=P, cols=S):
                    j, sq0, n = JOBS[job]
                    act.wait_ge(sq_used, 32 + NSQ2 * l + sq0 + q + 1)
                    act.activation(HS[(sq0 + q) % 2][0:parts, 0:cols], src, ACT.Square).then_inc(sq_full, 1)

                def rstd2(job, dim, parts=P, cols=S):
                    j, sq0, n = JOBS[job]
                    act.wait_ge(sq_used, 2 + 32 + NSQ2 * l + sq0 + n)
                    if j:
                        act.wait_ge(ap_done, NJOBS * l + j)
                    r = rstd[0:parts, 0:cols]
                    act.activation(r, B[7][0:parts, 0:cols], ACT.Ln, bias=c("eps")[0:parts], scale=1.0 / dim)
                    act.drain()
                    act.activation(r, r, ACT.Exp, scale=-0.5).then_inc(rstd_done, 1)

                def out2(rnd, s, dst, func=ACT.Identity, n=None):
                    full(R0 + 4 * rnd + s)
                    b = B[s % 2][:, :] if n is None else B[s % 2][:, 0:n]
                    act.activation(dst, b, func).then_inc(evac[s % 2], 1)

                for k in range(KT):
                    act.wait_ge(evac[k % 2], M0 + k // 2 - 4 + 2)
                    if k == 0:
                        act.wait_ge(layer_end, l + 1)
                    sq2("mix", k, X[:, k, :])
                rstd2("mix", D)
                for s in range(2):
                    out2(L_A, s, AH[:, s, 15:15 + S])
                for s in range(2, 4):
                    out2(L_A, s, tm2[s - 2], ACT.Sigmoid)
                for s in range(4):
                    full(R0 + 4 * L_Z + s)
                    act.activation(PS[:, s // 2, (s % 2) * S:(s % 2 + 1) * S], B[s % 2][:, :], ACT.Sigmoid)
                    act.activation(KF[:, s // 2, s % 2, :], B[s % 2][:, :], ACT.Sigmoid, scale=-1.0
                                   ).then_inc(evac[s % 2], 1)
                for s in range(2):
                    out2(L_QG, s, QH[:, s, :])
                for s in range(2, 4):
                    out2(L_QG, s, GG[:, s - 2, :], ACT.Silu)
                full(R0 + 4 * L_VCQ + 1)
                for b in range(2):
                    i = act.activation(VH[:, 2 * b:2 * b + 2, :].rearrange("p t n -> p (t n)"), B[2 + b][:, :], ACT.Identity)
                i.then_inc(vh_evac, 1)
                for s in range(2, 4):
                    out2(L_VCQ, s, CQ[:, s - 2, :])
                out2(L_KVX, 0, CKV)
                out2(L_KVX, 1, KR)
                for s in range(2, 4):
                    out2(L_KVX, s, GCX[:, s - 2, 1:1 + S])
                for s in range(2, 4):
                    out2(L_C, s, GB[:, s - 2, :])
                for n in range(12):
                    act.wait_ge(hg_ps, 44 * l + 33 + n)
                    if n < 4:
                        dst = AO7[:, n, :, :].rearrange("p i t -> p (i t)")
                        b = 4 + n
                    else:
                        ht, half, ii = (n - 4) // 4, (n - 4) % 4 // 2, n % 2
                        dst = AO8[:, 2 * ht + half, 2 * ii:2 * ii + 2, :].rearrange("p i t -> p (i t)")
                        b = 4 + 2 * ii + half
                    act.activation(dst, B[b][:, :], ACT.Identity).then_inc(hg_ev, 1)
                for ht in range(2):
                    act.wait_ge(o_full, 2 * l + ht + 1)
                    act.activation(CAT[:, 2 + ht, :], B[2 + ht][:, :], ACT.Identity).then_inc(oc_done, 1)
                    sq2(f"o{ht}", 0, B[2 + ht][:, :])
                    rstd2(f"o{ht}", HD)
                act.wait_ge(cen_done, l + 1)
                for q in range(2):
                    sq2("ln", q, CAT[:, q, :])
                rstd2("ln", 256)
                for q in range(2):
                    act.wait_ge(silu_in, 2 * l + q + 1)
                    act.activation(CAT[:, q, :], CAT[:, q, :], ACT.Silu, bias=p2("a_ln_b", q, q + 1)).then_inc(cat_done, 1)
                act.wait_ge(cat_done, 6 * l + 6)
                for g, job in enumerate(("bA", "bB", "bC")):
                    for q in range(2):
                        sq2(job, q, CAT[:, 2 * g + q, :])
                    rstd2(job, 256)
                for q in range(2):
                    sq2("qa", q, CQ[:, q, :])
                rstd2("qa", 256)
                sq2("kva", 0, CKV)
                rstd2("kva", P)

                def heads(i):
                    dst = (QM if i < 4 else KM)
                    if i < 4:
                        if i == 3:
                            full(R0 + 4 * L_UP)
                        else:
                            act.wait_ge(part_full, 6 + 14 * l + i + 1)
                        act.activation(dst[0:96, i, :], B[i % 2][0:96, :], ACT.Identity).then_inc(evac[i % 2], 1)
                    else:
                        act.wait_ge(part_full, 6 + 14 * l + i)
                        act.activation(dst[64:96, i % 4, :], KR[64:96, :], ACT.Identity)
                        act.activation(dst[0:64, i % 4, :], B[i % 2][0:64, :], ACT.Identity).then_inc(evac[i % 2], 1)
                    act.drain()
                    sq2(f"hd{i}", 0, dst[0:96, i % 4, :], 96)

                for i in range(8):
                    heads(i)
                    rstd2(f"hd{i}", 96, 96)
                for b in range(2):
                    if b == 0:
                        act.wait_ge(part_full, 6 + 14 * l + 8)
                    else:
                        full(R0 + 4 * L_UP + 3)
                    act.activation(VM[:, 2 * b:2 * b + 2, :].rearrange("p t n -> p (t n)"), B[b][:, :], ACT.Identity
                                   ).then_inc(evac[b], 1)
                n = 128 + 32 * l
                run_attention(n, 64 + 16 * l, [S] * 16)
                for f in range(2):
                    act.wait_ge(ot_full, 4 * l + f + 1)
                    act.activation(CAT[:, 6 + f, :], B[4 + f][:, :], ACT.Identity).then_inc(ot_done, 1)
                act.drain()
                for q in range(2):
                    sq2("bD", q, CAT[:, 6 + q, :])
                rstd2("bD", 256)
                act.wait_ge(mem_in, 16)
                for q in range(KT):
                    sq2("mem", q, MEM[:, q, :], cols=NM)
                rstd2("mem", D, cols=NM)
                for f in range(2):
                    full(R0 + 4 * L_XKV + f)
                    act.activation(XK[:, f, :], B[f][:, 0:NM], ACT.Identity)
                    act.wait_ge(sq_used, 32 + NSQ2 * l + JOBS[f"xk{f}"][1] + 1)
                    act.activation(HS[JOBS[f"xk{f}"][1] % 2][:, 0:NM], B[f][:, 0:NM], ACT.Square).then_inc(sq_full, 1)
                    act.drain()
                    act.sem_inc(evac[f], 1)
                full(R0 + 4 * L_XKV + 3)
                for t in range(2):
                    i = act.activation(XV[:, t, :], B[2 + t][:, 0:256], ACT.Identity)
                i.then_inc(xv_done, 1)
                for f in range(2):
                    rstd2(f"xk{f}", HD, cols=NM)
                for k in range(KT):
                    act.wait_ge(evac[k % 2], M0 + N_WOUT + k // 2 + 2)
                    sq2("xq", k, X[:, k, :])
                rstd2("xq", D)
                for f in range(2):
                    full(R0 + 4 * L_XQO + f)
                    act.activation(XQ[:, f, :], B[f][:, :], ACT.Identity)
                    act.wait_ge(sq_used, 32 + NSQ2 * l + JOBS[f"xh{f}"][1] + 1)
                    act.activation(HS[JOBS[f"xh{f}"][1] % 2], B[f][:, :], ACT.Square).then_inc(sq_full, 1)
                    act.drain()
                    act.sem_inc(evac[f], 1)
                for f in range(2):
                    rstd2(f"xh{f}", HD)
                run_attention(n + 16, 72 + 16 * l, [256] * 16)
                for f in range(2):
                    act.wait_ge(ot_full, 4 * l + 2 + f + 1)
                    act.activation(OXT[:, f, :], B[4 + f][:, :], ACT.Identity).then_inc(ot_done, 1)
                for k in range(KT):
                    act.wait_ge(evac[k % 2], M0 + N_XO + k // 2 + 2)
                    sq2("ffn", k, X[:, k, :])
                rstd2("ffn", D)
                act.preload_act_table(ACT.Silu)
                with act.Fori(0, FT // 2) as i:
                    for u in range(2):
                        m = M0 + 2 * i + u + N_FFN
                        full(R0 + 4 * L_FFN + 4 * i + 2 * u)
                        act.wait_ge(evac[1], m)
                        act.activation(SG[u], B[0][:, :], ACT.Silu).then_inc(evac[0], 1)
                act.sem_inc(sq_full, 1)

        @block.vector
        def _(dve):
            dve.sem_inc(evac[1], 1)
            dve.sem_inc(sc_done, 2)
            dve.sem_inc(pt_dve, 2)
            dve.sem_inc(o_done, 2)
            dve.wait_ge(const_in, 32)
            dve.scalar_tensor_tensor(lru[:, 0, :], p1("lam"), -1.0, p1("lam"), ALU.mult, ALU.max).then_inc(coef_e, 1)
            dve.tensor_scalar(lru[:, 5, :], p1("ba"), 0.5, None, ALU.mult)
            dve.tensor_scalar(lru[:, 6, :], p1("bx"), 0.5, None, ALU.mult)
            dve.wait_ge(rstd_done, 1)
            for k in range(KT):
                dve.scalar_tensor_tensor(H[:, k, :], X[:, k, :], p1("mix_pre", k, k + 1), rstd, ALU.mult, ALU.mult
                                         ).then_inc(h_done, 1)
            dve.wait_ge(coef_e, 2)
            e, z, w = lru[:, 1, :], lru[:, 2, :], lru[:, 7, :]
            dve.tensor_scalar(z, e, 2.0, None, ALU.add)
            dve.drain()
            dve.reciprocal(z, z)
            dve.drain()
            dve.tensor_tensor(z, z, e, ALU.mult)
            dve.drain()
            dve.tensor_tensor(e, z, z, ALU.mult)
            dve.memset(w, 1.0 / 17)
            for q in (15, 13, 11, 9, 7, 5, 3, 1):
                dve.drain()
                dve.tensor_tensor(w, w, e, ALU.mult)
                dve.drain()
                dve.tensor_scalar(w, w, 1.0 / q, None, ALU.add)
            dve.drain()
            dve.tensor_tensor(w, w, z, ALU.mult)
            dve.drain()
            dve.tensor_scalar(z, p1("lam"), -1.0, 0.0, ALU.mult, ALU.max)
            dve.drain()
            dve.scalar_tensor_tensor(w, w, 2.0, z, ALU.mult, ALU.add)
            dve.drain()
            dve.tensor_scalar(lru[:, 3, :], w, 4.0, None, ALU.mult)
            dve.tensor_scalar(lru[:, 4, :], w, -4.0, None, ALU.mult).then_inc(coef_done, 1)
            dve.wait_ge(pad_done, 1)

            def conv(t):
                dve.wait_ge(evac[t % 2], t // 2 + 2)
                if t >= 2:
                    dve.wait_ge(gate_full, t - 1)
                o = tmp[t % 2]
                cw = lambda i: p1("conv_w", i * KT + t, i * KT + t + 1)
                dve.drain()
                dve.tensor_scalar(o, XR[:, t, 0:S], cw(0), p1("conv_b", t, t + 1), ALU.mult, ALU.add)
                for i in range(1, 4):
                    dve.drain()
                    a = dve.scalar_tensor_tensor(o, XR[:, t, i:i + S], cw(i), o, ALU.mult, ALU.add)
                a.then_inc(conv_done, 1)

            def lru_mid(t):
                a = tmp[5 + t % 2]
                dve.wait_ge(lru_a, t + 1)
                dve.tensor_tensor(tmp[9], a, a, ALU.mult)
                dve.drain()
                dve.scalar_tensor_tensor(tmp[9], tmp[9], 1.0, tmp[4], ALU.add, ALU.mult)
                dve.scalar_tensor_tensor(tmp[7 + t % 2], tmp[3], 1.0, tmp[t % 2], ALU.add, ALU.mult
                                         ).then_inc(lru_t, 1)

            def lru_scan(t):
                i = tmp[7 + t % 2]
                dve.wait_ge(lru_sqrt, t + 1)
                dve.tensor_tensor(i, i, tmp[9], ALU.mult)
                dve.drain()
                dve.tensor_tensor_scan(tmp[10], tmp[5 + t % 2], i, 0.0, ALU.mult, ALU.add)
                dve.drain()
                if t == 0:
                    dve.wait_ge(evac[0], M_CMP_IN + 1)
                    dve.wait_ge(evac[1], M_CMP_IN + 1)
                dve.tensor_tensor(G[:, t, :], G[:, t, :], tmp[10], ALU.mult).then_inc(lru_y, 1)

            conv(0)
            for t in range(8):
                if t < 7:
                    conv(t + 1)
                if t:
                    lru_scan(t - 1)
                lru_mid(t)
            lru_scan(7)
            for h in range(HEADS):
                if h == 0:
                    dve.wait_ge(shuffled, 16 * 8)
                dve.scalar_tensor_tensor(CB[:, :, h, :], c("cmp_dist").rearrange("p (t c) -> p t c", t=TT),
                                         c("slopes", h, h + 1), c("cmp_neg").rearrange("p (t c) -> p t c", t=TT),
                                         ALU.mult, ALU.add)
            dve.drain()
            for t in range(8):
                dve.wait_ge(evac[t % 2], M_GMR + t // 2 + 2)
                dve.tensor_tensor(G[:, t, :], G[:, t, :], tmp[t % 2], ALU.mult).then_inc(lru_y, 1)
            mx = sml[:, 32:48]
            dn = sml[:, 48:64]
            for t in range(TT):
                sc = tmp[0].rearrange("p (h c) -> p h c", h=HEADS)
                dve.drain()
                dve.wait_ge(cs_full, t + 1)
                if t:
                    dve.wait_ge(ct_full, t)
                for half in range(2):
                    by_half = lambda ap: ap.rearrange("p (j f r c) -> p j f (r c)", j=2, f=2, r=4)[:, :, half, :]
                    dve.tensor_tensor(by_half(tmp[0]), B[4 + half][:, 0:256].rearrange("p (j n) -> p j n", j=2),
                                      by_half(CB[:, t, :, :].rearrange("p h c -> p (h c)")), ALU.add)
                dve.drain()
                dve.tensor_reduce(mx, sc, AX.X, ALU.max)
                dve.drain()
                dve.tensor_scalar(mx, mx, -1e20, None, ALU.max)
                dve.drain()
                dve.tensor_tensor(sc, sc, mx.unsqueeze(2).to_broadcast([P, HEADS, CC]), ALU.subtract).then_inc(cs_m, 1)
                dve.wait_ge(cs_e, t + 1)
                dve.tensor_reduce(dn, sc, AX.X, ALU.add)
                dve.drain()
                dve.tensor_scalar(dn, dn, 1e-30, None, ALU.max)
                dve.drain()
                dve.reciprocal(dn, dn)
                dve.drain()
                if t == 0:
                    dve.wait_ge(g_evac, 1)
                dve.tensor_tensor(dn, dn, GT[:, 0, :, t], ALU.mult)
                dve.drain()
                dve.tensor_tensor(sc, sc, dn.unsqueeze(2).to_broadcast([P, HEADS, CC]), ALU.mult).then_inc(cs_p, 1)
                dve.wait_ge(co_full, t + 1)
                dve.drain()
                dve.tensor_copy(YAT[:, t, 0:S], B[2][:, :])
                dve.tensor_copy(YAT[:, t, S:D], B[3][:, :]).then_inc(co_done, 1)

            def run_attention(n, pts, steps, finish):
                rc = sml[:, 64:68]
                for s in range(len(steps) + 3):
                    if s < len(steps):
                        w, in1, scale = steps[s]
                        waits(dve, (qk_full, n + s + 1), (exp_done, n + s + 1))
                        dve.tensor_tensor_reduce(tmp[s % 2][:, 0:w], B[4 + s % 2][:, 0:w], in1, -scale, 3e38,
                                                 ALU.add, ALU.min, sml[:, s:s + 1]).then_inc(sc_done, 1)
                    e = s - 2
                    if 0 <= e < len(steps) and e % 4 >= 2:
                        w = steps[e][0]
                        dve.wait_ge(tr_full, n + e + 3)
                        dve.wait_ge(pv_full, n + e + 1)
                        dve.tensor_copy(tmp[6 + e % 2][:, 0:w], B[6 + e % 2][:, 0:w]).then_inc(pt_dve, 1)
                    g = s - 3
                    if g >= 0 and g % 4 == 3:
                        finish(g // 4)

            def finish1(n, o0, j, r):
                def f(g):
                    br, half = g // 2, g % 2
                    h = 8 * j + 4 * half + r
                    rc = sml[:, 64:68]
                    dve.drain()
                    waits(dve, (pv_full, n + 4 * g + 6), (o_added, o0 + g + 1))
                    dve.reciprocal(rc, den[:, 4 * g:4 * g + 4])
                    dve.drain()
                    dve.tensor_tensor(rc, rc, GT[:, 1 + br, bass.ds(h, 1), :].rearrange("p o t -> p (o t)"), ALU.mult)
                    dve.drain()
                    ob = tmp[10 + half].rearrange("p (b t d) -> p b t d", b=2, t=TT)[:, br]
                    dve.tensor_tensor(ob, B[2 + g % 2][:, 0:256].rearrange("p (t d) -> p t d", t=TT),
                                      rc.unsqueeze(2).to_broadcast([P, TT, HD]), ALU.mult).then_inc(o_done, 1)
                return f

            if True:
                for j in range(2):
                    with dve.Fori(0, 4) as r:
                        dve.wait_ge(sd_done, 2 * r + 8 * j + 3)
                        steps = [(P * (t + 1), tmp[8 + half][:, 384 - P * t:512], 1.0)
                                 for _ in range(2) for half in range(2) for t in range(TT)]
                        run_attention(16 * r + 64 * j, 8 * r + 32 * j, steps, finish1(16 * r + 64 * j, 4 * r + 16 * j, j, r))

            for k in range(KT):
                dve.wait_ge(yt_full, k + 1)
                if k == 0:
                    dve.wait_ge(evac[0], M_W1K + 1)
                    dve.wait_ge(evac[1], M_W1K + 1)
                dve.tensor_tensor(tmp[k % 2], B[4 + k % 2][:, :], GA[:, k, :], ALU.mult)
                dve.drain()
                dve.tensor_tensor(G[:, k, :], G[:, k, :], tmp[k % 2], ALU.add).then_inc(yt_done, 1)

            def post_norm(n, base, gain):
                dve.wait_ge(rstd_done, n)
                for k in range(KT):
                    dve.scalar_tensor_tensor(H[:, k, :], H[:, k, :], p1(gain, k, k + 1), rstd, ALU.mult, ALU.mult)
                    dve.drain()
                    dve.tensor_tensor(X[:, k, :], X[:, k, :], H[:, k, :], ALU.add).then_inc(x_done, 1)

            post_norm(2, 0, "mix_post")
            dve.wait_ge(rstd_done, 3)
            for k in range(KT):
                dve.scalar_tensor_tensor(H[:, k, :], X[:, k, :], p1("ffn_pre", k, k + 1), rstd, ALU.mult, ALU.mult
                                         ).then_inc(h_done, 1)
            with dve.Fori(0, FT // 2) as i:
                for u in range(2):
                    m = 2 * i + u + M_FFN
                    dve.wait_ge(chunk_done, 4 * R_FFN + 4 * i + 2 * u + 2 + SLOTS)
                    dve.wait_ge(evac[0], m + 2)
                    dve.tensor_tensor(ACTB[:, bass.ds(2 * i + u, 1), :], B[1][:, :].unsqueeze(1), SG[u].unsqueeze(1),
                                      ALU.mult).then_inc(evac[1], 1)
            post_norm(4, 8, "ffn_post")
            for k in range(KT):
                if k % 4 == 3:
                    dve.wait_ge(chunk_done, 4 * R_PLEP + k // 4 + 1 + SLOTS)
                else:
                    dve.wait_ge(part_full, k - k // 4 + 1)
                if k == 0:
                    dve.wait_ge(evac[0], M_PLEP + 1)
                    dve.wait_ge(evac[1], M_PLEP + 1)
                dve.tensor_tensor(tmp[k % 2], B[k % 2][:, :], H[:, k, :], ALU.mult).then_inc(evac[k % 2], 1)
                dve.drain()
                dve.tensor_tensor(X[:, k, :], X[:, k, :], tmp[k % 2], ALU.add).then_inc(x_done, 1)

            TWO_PI = 6.283185307179586
            c1 = 6.28125
            c2 = float(np.float32(np.round((TWO_PI - c1) * 2.0 ** 21) / 2.0 ** 21))
            c3 = TWO_PI - c1 - c2
            dve.drain()
            dve.wait_ge(pos_in, 16)
            ang, tn = tm2[0], tm2[1]
            dve.tensor_copy(ang, SIN.bitcast(I32))
            dve.drain()
            dve.tensor_scalar(ang, ang, c("inv_freq"), None, ALU.mult)
            dve.drain()
            dve.tensor_scalar(tn, ang, 1.0 / TWO_PI, 12582912.0, ALU.mult, ALU.add)
            dve.drain()
            dve.tensor_scalar(tn, tn, -12582912.0, None, ALU.add)
            for part in (c1, c2, c3):
                dve.drain()
                dve.scalar_tensor_tensor(ang, tn, -part, ang, ALU.mult, ALU.add)
            dve.drain()
            dve.tensor_scalar(SIN, ang, 3.1415925, -3.1415925, ALU.min, ALU.max)
            dve.scalar_tensor_tensor(tn, ang, -1.0, ang, ALU.mult, ALU.max)
            dve.drain()
            dve.tensor_scalar(COS, tn, -1.0, 1.5707963267948966, ALU.mult, ALU.add).then_inc(rope_arg, 1)
            dve.wait_ge(par2_in, 32)
            mxg = LBS[:, 3, 0, :]
            dve.tensor_tensor(mxg, GAM[:, 0, :], GAM[:, 1, :], ALU.max)
            dve.drain()
            dve.tensor_tensor(LBS[:, 0], GAM, mxg.unsqueeze(1).to_broadcast([P, 2, 4]), ALU.subtract).then_inc(gam_e, 1)
            dve.wait_ge(gam_e, 2)
            dve.tensor_tensor(mxg, LBS[:, 1, 0, :], LBS[:, 1, 1, :], ALU.add)
            dve.drain()
            dve.reciprocal(mxg, mxg)
            dve.drain()
            dve.tensor_tensor(LBS[:, 2], LBS[:, 1], mxg.unsqueeze(1).to_broadcast([P, 2, 4]), ALU.mult)
            dve.drain()
            dve.tensor_tensor(LBS[:, 4, 0, :], LBS[:, 2, 0, :], LBS[:, 2, 0, :], ALU.subtract)
            dve.tensor_tensor(LBS[:, 4, 1, :], LBS[:, 2, 0, :], LBS[:, 2, 1, :], ALU.add)
            dve.drain()
            dve.tensor_tensor(LBS[:, 4, 1, :], LBS[:, 4, 1, :], LBS[:, 2, 0, :], ALU.subtract)
            dve.drain()
            dve.tensor_scalar(LBS[:, 5], LBS[:, 4], -1.0, 1.0, ALU.mult, ALU.add).then_inc(lb_done, 1)
            dve.drain().then_inc(layer_end, 1)

            with dve.Fori(0, LAYERS) as l:
                R0 = 4 * ROUNDS1 + 4 * ROUNDS2 * l + SLOTS
                M0 = PAIRS1 + PAIRS2 * l

                def apply(job, pairs, gain, parts=P, cols=S, done=None):
                    waits(dve, (rstd_done, 4 + NJOBS * l + JOBS[job][0] + 1))
                    for k, (o, i) in enumerate(pairs):
                        x = dve.scalar_tensor_tensor(o, i, p2(gain, k, k + 1)[0:parts], rstd[0:parts, 0:cols],
                                                     ALU.mult, ALU.mult)
                        if done is not None:
                            x.then_inc(done, 1)
                    dve.drain().then_inc(ap_done, 1)

                dve.wait_ge(cur_done, l + 1)
                apply("mix", [(H[:, k, :], X[:, k, :]) for k in range(KT)], "g_mix", done=h2_done)
                for s in range(2):
                    dve.wait_ge(evac[s], M0 + N_A + 3)
                    dve.wait_ge(edge_done, 1)
                    i = dve.tensor_tensor(AH[:, s, 15:15 + S], AH[:, s, 15:15 + S], tm2[s], ALU.mult)
                i.then_inc(ah_done, 1)
                dve.wait_ge(evac[0], M0 + N_Z + 3)
                dve.wait_ge(evac[1], M0 + N_Z + 3)
                for d in range(2):
                    for t in range(2):
                        pre = PS[:, d, t * S:(t + 1) * S]
                        dve.scalar_tensor_tensor(pre, KF[:, d, t, :], LBC[:, 0, 2 * d + t:2 * d + t + 1], pre,
                                                 ALU.mult, ALU.add)
                dve.drain()
                for d in range(2):
                    for t in range(2):
                        dve.tensor_scalar(KF[:, d, t, :], KF[:, d, t, :], LBC[:, 1, 2 * d + t:2 * d + t + 1], None, ALU.mult)
                dve.drain()
                flat = lambda ap: ap.rearrange("p a n -> p (a n)")
                dve.tensor_tensor(KC[0], flat(KF[:, 0]), flat(KF[:, 1]), ALU.add)
                waits(dve, (evac[0], M0 + N_QG + 2), (evac[1], M0 + N_QG + 2))
                dve.drain().then_inc(hg_qk, 1)

                def sides(ap, m):
                    return ap.rearrange("p (n s m) -> p s n m", s=2, m=m)

                def hg_mul(lev):
                    m = 1 << lev
                    st = lev + 1
                    q, k = sides(QC[st % 2], m), sides(KC[st % 2], m)
                    if lev:
                        dve.wait_ge(hg_up, 9 * l + lev + 1)
                    else:
                        dve.wait_ge(hg_up, 9 * l + 1)
                    if st >= 2:
                        dve.wait_ge(hg_ps, 44 * l + 4 * (st - 1))
                    ql = sides(flat(QH), m)
                    kf, kb = sides(flat(KF[:, 0]), m), sides(flat(KF[:, 1]), m)
                    pf, pb, sf, sb_ = (sides(PS[:, i, :], m) for i in range(4))
                    dve.tensor_tensor(q[:, 1], ql[:, 1], pf[:, 1], ALU.mult)
                    dve.tensor_tensor(q[:, 0], ql[:, 0], pb[:, 0], ALU.mult)
                    dve.tensor_tensor(k[:, 0], kf[:, 0], sf[:, 0], ALU.mult)
                    dve.tensor_tensor(k[:, 1], kb[:, 1], sb_[:, 1], ALU.mult)
                    dve.drain().then_inc(hg_qk, 1)

                def hg_merge(st):
                    for bk in range(4):
                        waits(dve, (hg_ps, 44 * l + 4 * st + bk + 1))
                        dst = AD[:, bk % 2, 2 * (bk // 2):2 * (bk // 2) + 2, :].rearrange("p i n -> p (i n)")
                        if st == 0:
                            dve.tensor_copy(dst, B[4 + bk][:, :]).then_inc(hg_mg, 1)
                        else:
                            lv = c("levels", (st - 1) * P, st * P).bitcast(I32).unsqueeze(1).to_broadcast([P, 4, P])
                            dve.copy_predicated(dst.rearrange("p (a t) -> p a t", a=4), lv,
                                                B[4 + bk][:, :].rearrange("p (a t) -> p a t", a=4)).then_inc(hg_mg, 1)

                taps = [(t, k) for k in range(31) for t in range(2)]

                def conv_taps(a, b):
                    for t, k in taps[a:b]:
                        w = p2("a_dw_w", 2 * k + t, 2 * k + t + 1)
                        if t == 0:
                            dve.drain()
                        if k == 0:
                            i = dve.tensor_scalar(CAT[:, t, :], AH[:, t, 0:S], w, p2("a_dw_b", t, t + 1), ALU.mult, ALU.add)
                        else:
                            i = dve.scalar_tensor_tensor(CAT[:, t, :], AH[:, t, k:k + S], w, CAT[:, t, :], ALU.mult, ALU.add)
                    if b >= 62:
                        i.then_inc(ah_done, 1)

                for st in range(1, 10):
                    hg_mul(st - 1)
                    if st <= 8:
                        dve.drain()
                        hg_merge(st - 1)
                    conv_taps(7 * (st - 1), 7 * st if st < 9 else 62)
                for t in range(2):
                    dve.wait_ge(chunk_done, R0 + 4 * L_C + t + 1)
                    dve.wait_ge(evac[t], M0 + N_KVX + 3)
                    dve.tensor_tensor(GCX[:, t, 1:1 + S], GCX[:, t, 1:1 + S], B[t][:, :], ALU.mult).then_inc(evac[t], 1)
                dve.drain()
                for t in range(2):
                    o = CAT[:, 4 + t, :]
                    w = lambda k: p2("c_dw_w", 2 * k + t, 2 * k + t + 1)
                    dve.tensor_scalar(o, GCX[:, t, 0:S], w(0), p2("c_dw_b", t, t + 1), ALU.mult, ALU.add)
                    for k in (1, 2):
                        dve.drain()
                        dve.scalar_tensor_tensor(o, GCX[:, t, k:k + S], w(k), o, ALU.mult, ALU.add)
                    dve.drain()
                    dve.wait_ge(evac[t], M0 + N_C + 3)
                    dve.tensor_tensor(o, o, GB[:, t, :], ALU.mult).then_inc(cat_done, 1)
                for ht in range(2):
                    o = CAT[:, 2 + ht, :]
                    dve.wait_ge(oc_done, 2 * l + ht + 1)
                    dve.wait_ge(rstd_done, 4 + NJOBS * l + JOBS[f"o{ht}"][0] + 1)
                    dve.scalar_tensor_tensor(o, o, p2("h_onorm", ht, ht + 1), rstd, ALU.mult, ALU.mult
                                             ).then_inc(ap_done, 1)
                    dve.drain()
                    dve.tensor_tensor(o, o, GG[:, ht, :], ALU.mult).then_inc(cat_done, 1)
                dve.wait_ge(mean_full, l + 1)
                for t in range(2):
                    i = dve.scalar_tensor_tensor(CAT[:, t, :], B[6][:, :], -1.0 / 256, CAT[:, t, :], ALU.mult, ALU.add)
                i.then_inc(cen_done, 1)
                dve.drain()
                apply("ln", [(CAT[:, q, :], CAT[:, q, :]) for q in range(2)], "a_ln_g", done=silu_in)
                for g, job in enumerate(("bA", "bB", "bC")):
                    waits(dve, (rstd_done, 4 + NJOBS * l + JOBS[job][0] + 1))
                    for q in range(2):
                        o = CAT[:, 2 * g + q, :]
                        dve.scalar_tensor_tensor(o, o, p2("g_branch", 2 * g + q, 2 * g + q + 1), rstd, ALU.mult, ALU.mult)
                    dve.drain().then_inc(ap_done, 1)
                apply("qa", [(CQ[:, q, :], CQ[:, q, :]) for q in range(2)], "qa")
                apply("kva", [(CKV, CKV)], "kva")
                for i in range(8):
                    t = (QM if i < 4 else KM)[0:96, i % 4, :]
                    gain = p2("qn" if i < 4 else "kn")[0:96]
                    dve.wait_ge(rstd_done, 4 + NJOBS * l + JOBS[f"hd{i}"][0] + 1)
                    dve.scalar_tensor_tensor(t, t, gain, rstd[0:96, :], ALU.mult, ALU.mult).then_inc(ap_done, 1)
                    dve.drain().then_inc(qk_ready, 1)
                    dve.wait_ge(rot_full, 8 * l + i + 1)
                    dve.tensor_tensor(t, t, COS[0:96, :], ALU.mult)
                    dve.tensor_tensor(RB[0:96, :], B[4 + i % 2][0:96, :], SIN[0:96, :], ALU.mult)
                    dve.drain()
                    dve.tensor_tensor(t, t, RB[0:96, :], ALU.add)
                    dve.drain().then_inc(qk_ready, 1)

                def finish2(n, dst):
                    def f(g):
                        rc = sml[:, 64:68]
                        dve.drain()
                        waits(dve, (pv_full, n + 4 * g + 6))
                        dve.reciprocal(rc, den[:, 4 * g:4 * g + 4])
                        dve.drain()
                        dve.tensor_tensor(dst[:, :, g * HD:(g + 1) * HD],
                                          B[2 + g % 2][:, 0:256].rearrange("p (t d) -> p t d", t=TT),
                                          rc.unsqueeze(2).to_broadcast([P, TT, HD]), ALU.mult).then_inc(o_done, 1)
                    return f

                n = 128 + 32 * l
                run_attention(n, 0, [(S, c("zeros"), 96 ** -0.5)] * 16, finish2(n, OM))
                waits(dve, (rstd_done, 4 + NJOBS * l + JOBS["bD"][0] + 1))
                for q in range(2):
                    o = CAT[:, 6 + q, :]
                    dve.scalar_tensor_tensor(o, o, p2("g_branch", 6 + q, 7 + q), rstd, ALU.mult, ALU.mult)
                dve.drain().then_inc(ap_done, 1)
                apply("mem", [(MN[:, k, :], MEM[:, k, :]) for k in range(KT)], "g_mem", cols=NM, done=mn_done)
                for f in range(2):
                    apply(f"xk{f}", [(XK[:, f, :], XK[:, f, :])], "x_kn", cols=NM)

                def add_x(k, ready):
                    ready(k)
                    dve.tensor_tensor(X[:, k, :], X[:, k, :], B[k % 2][:, :], ALU.add).then_inc(evac[k % 2], 1)

                for k in range(KT):
                    add_x(k, lambda k: dve.wait_ge(chunk_done, R0 + 4 * L_WOUT + k + 1))
                dve.drain()
                apply("xq", [(H[:, k, :], X[:, k, :]) for k in range(KT)], "g_xq", done=h2_done)
                for f in range(2):
                    apply(f"xh{f}", [(XQ[:, f, :], XQ[:, f, :])], "x_qn")
                run_attention(n + 16, 0, [(256, c("zeros")[:, 0:256], HD ** -0.5)] * 16, finish2(n + 16, OX))

                def xo_ready(k):
                    if k % 4 == 3:
                        dve.wait_ge(chunk_done, R0 + 4 * L_XQO + 2 + k // 4 + 1)
                    else:
                        dve.wait_ge(part_full, 6 + 14 * l + 8 + k - k // 4 + 1)

                for k in range(KT):
                    add_x(k, xo_ready)
                dve.drain()
                apply("ffn", [(H[:, k, :], X[:, k, :]) for k in range(KT)], "g_ffn", done=h2_done)
                with dve.Fori(0, FT // 2) as i:
                    for u in range(2):
                        m = M0 + 2 * i + u + N_FFN
                        dve.wait_ge(chunk_done, R0 + 4 * L_FFN + 4 * i + 2 * u + 2)
                        dve.wait_ge(evac[0], m + 2)
                        dve.tensor_tensor(AC2[:, bass.ds(2 * i + u, 1), :], B[1][:, :].unsqueeze(1), SG[u].unsqueeze(1),
                                          ALU.mult).then_inc(evac[1], 1)
                for k in range(KT):
                    add_x(k, lambda k: dve.wait_ge(chunk_done, R0 + 4 * L_DOWN + 3 * k + 3))
                dve.drain().then_inc(layer_end, 1)

        @block.gpsimd
        def _(pool):
            pool.sem_inc(sq_used, 2)
            pool.sem_inc(sd_done, 1)
            pool.sem_inc(tr_full, 2)
            pool.sem_inc(pv_full, 2)
            pool.sem_inc(o_added, 4)
            pool.memset(XR[:, :, 0:3], 0.0).then_inc(pad_done, 1)
            pool.memset(K2, 0.0)
            pool.memset(VBD, 0.0)
            pool.drain()
            pool.wait_ge(evac[0], M_CMP_IN + 3)
            pool.wait_ge(evac[1], M_CMP_IN + 3)
            for kv in range(2):
                for gg in range(2):
                    for par in range(2):
                        pool.dma_start(KCD[64 * par:64 * par + 64, kv].rearrange("p (j g) m -> p j g m", g=2)[:, :, gg, :],
                                       KST[64 * gg:64 * gg + 64, 2 * kv:2 * kv + 2, par, :]).then_inc(shuffled, 16)
            pool.wait_ge(shuffled, 16 * 8)
            for kv in range(2):
                if kv:
                    pool.wait_ge(chunk_done, 4 * R_W1K + 4 + SLOTS)
                pos = p1("pos_k" if kv == 0 else "pos_v")
                for a in range(2):
                    i = pool.tensor_tensor(
                        K2[:, 8 * a:8 * a + 8, :, 0:31],
                        KCD[:, kv].rearrange("p g (c b) -> p b g c", b=8)[:, :, :, a:a + 31],
                        pos[:, 8 * a:8 * a + 8].unsqueeze(2).unsqueeze(3).to_broadcast([P, 8, 4, 31]), ALU.add)
                i.then_inc(k2_done, 1)
            pool.drain()
            pool.sem_inc(k2_done, 1)

            for j in range(2):
                with pool.Fori(0, 4) as r:
                    waits(pool, (q_cur, r + 4 * j + 1), (sc_done, 16 * r + 64 * j + 2))
                    for half in range(2):
                        pool.tensor_scalar(tmp[8 + half], c("dist"), sml[:, 20 + half:21 + half], 0.0,
                                           ALU.mult, ALU.add).then_inc(sd_done, 1)
                    for g in range(4):
                        br, half = g // 2, g % 2
                        pool.drain()
                        waits(pool, (o_done, 4 * r + 16 * j + g + 3))
                        ob = tmp[10 + half].rearrange("p (b t d) -> p b t d", b=2, t=TT)[:, br]
                        ya = YAT[:, :, bass.ds((8 * j + 4 * half) * HD + r * HD, HD)]
                        pool.tensor_tensor(ya, ya, ob, ALU.add).then_inc(o_added, 1)
            pool.wait_ge(yt_full, KT)
            pool.wait_ge(chunk_done, 4 * R_WOUT + KT + SLOTS)
            pool.dma_start(PP, pT.rearrange("(k p) n -> p k n", p=P)).then_inc(p_in, 16)
            pool.wait_ge(lru_y, 8)
            pool.wait_ge(chunk_done, 4 * R_PLEP + 2 + SLOTS)
            pool.wait_ge(x_done, 24)
            pool.dma_start(PALL, par2_d).then_inc(par2_in, 16)
            pool.dma_start(GAM, gamma_d).then_inc(par2_in, 16)
            pool.dma_start(SIN.bitcast(I32), pos_d.to_broadcast([P, S])).then_inc(pos_in, 16)
            pool.dma_start(MEM, memT.rearrange("(k p) n -> p k n", p=P)).then_inc(mem_in, 16)
            pool.memset(AH[:, :, 0:15], 0.0)
            pool.memset(AH[:, :, 15 + S:], 0.0)
            pool.memset(GCX[:, :, 0:1], 0.0)
            pool.memset(GCX[:, :, 1 + S:], 0.0)
            pool.drain()
            pool.sem_inc(edge_done, 1)
            with pool.Fori(0, LAYERS) as l:
                M0 = PAIRS1 + PAIRS2 * l
                waits(pool, (layer_end, l + 1), (chunk_done, 4 * ROUNDS1 + 4 * ROUNDS2 * l + SLOTS + 1))
                pool.memset(PS[:, 2:4, :], 1.0)
                pool.drain()
                pool.wait_ge(evac[0], M0 + N_QG + 2)
                pool.sem_inc(hg_up, 1)
                for lev in range(HLEV - 1):
                    m = 1 << lev
                    pool.wait_ge(hg_qk, 10 * l + lev + 2)
                    pf, pb, sf, sb_ = (PS[:, i, :].rearrange("p (n s m) -> p s n m", s=2, m=m) for i in range(4))
                    nb = 2 * S // (2 * m)
                    whole = lambda ap, at: ap[:, :, at:at + 1].to_broadcast([P, nb, m])
                    pool.tensor_tensor(sf[:, 0], sf[:, 0], whole(pf[:, 1], m - 1), ALU.mult)
                    pool.tensor_tensor(sb_[:, 1], sb_[:, 1], whole(pb[:, 0], 0), ALU.mult)
                    pool.drain()
                    pool.tensor_tensor(pf[:, 1], pf[:, 1], whole(pf[:, 0], m - 1), ALU.mult)
                    pool.tensor_tensor(pb[:, 0], pb[:, 0], whole(pb[:, 1], 0), ALU.mult)
                    pool.drain()
                    pool.sem_inc(hg_up, 1)
            pool.wait_ge(layer_end, LAYERS + 1)
            pool.dma_start(out.rearrange("(k p) n -> p k n", p=P), X).then_inc(out_done, 16)
            pool.wait_ge(out_done, 16)


def constants():
    f = np.float32
    t = {}
    t["ident"] = np.eye(P)
    t["ones"] = np.ones((P, P))
    t["halves"] = np.kron(np.eye(2), np.ones((64, 64)))
    p = np.arange(P)[:, None]
    d = np.arange(512)[None, :] - 384 - p
    t["dist"] = np.where(d > 0, -BIG, d)
    t["zeros"] = np.zeros((P, 512))
    tok = (np.arange(TT)[None, :, None] * P + p[:, :, None])
    cd = np.arange(CC)[None, None, :] * 16 + 31 - tok
    t["cmp_dist"] = np.where(cd > 0, 0, cd).reshape(P, -1)
    t["cmp_neg"] = np.where(cd > 0, -BIG, 0).reshape(P, -1)
    t["slopes"] = np.tile(np.exp2(-8.0 * np.arange(1, HEADS + 1) / HEADS)[None], (P, 1))
    t["eps"] = np.full((P, 1), EPS)
    rot = np.zeros((P, 96))
    for i in range(16):
        rot[80 + i, 64 + i] = -1
        rot[64 + i, 80 + i] = 1
    t["rot"] = rot
    inv = np.zeros((P, 1))
    inv[64:80, 0] = inv[80:96, 0] = 10000.0 ** (-np.arange(0, 32, 2) / 32.0)
    t["inv_freq"] = inv
    row = np.zeros((P, 1))
    t["rope_row"] = row
    s_, t_ = np.arange(P)[:, None], np.arange(P)[None, :]
    lv = [((s_ >> (l + 1)) == (t_ >> (l + 1))) & ((s_ >> l) != (t_ >> l)) for l in range(7)]
    t["levels"] = np.concatenate([x.astype(f) for x in lv], axis=1)
    return np.ascontiguousarray(np.concatenate([t[n].astype(f) for n, _ in CONST_FIELDS], axis=1))


def tiles(w, cols=P):
    k, n = w.shape
    return w.reshape(k // P, P, n // cols, cols).transpose(2, 1, 0, 3).reshape(n // cols, P, -1)


def vec(v):
    return v.reshape(-1, P).T


def block_diag(w):
    z = np.zeros((w.shape[0] // 2, P, P), w.dtype)
    z[:, 0:64, 0:64] = w[0::2]
    z[:, 64:128, 64:128] = w[1::2]
    return z.transpose(1, 0, 2).reshape(P, -1)


def first_stream(i):
    w = i["w_in"][0]
    at = np.cumsum([0, D, D, D, 256, 256, 256, 256, 256, 256, 48, D, D])
    sec = [w[:, a:b] for a, b in zip(at[:-1], at[1:])]
    xr, gr, q, kc, vc, ks, vs, kw, vw, gn, gmr, gma = sec
    q = q.reshape(D, 2, 2, 4, HD).transpose(0, 1, 3, 2, 4).reshape(D, D)
    ffn = i["ffn_w_gate_up"][0].reshape(D, 2, FT, P).transpose(0, 2, 1, 3).reshape(D, -1)
    vv = np.concatenate([vs, vw], axis=1).reshape(4, 2, P, S).transpose(0, 2, 1, 3).reshape(4, P, CH)
    w1 = [i[n][0].reshape(4, 4, P, 256).transpose(0, 2, 1, 3).reshape(4, P, CH) for n in ("cmp_k_w1", "cmp_v_w1")]
    dn = down_chunks(i["ffn_w_down"][0])
    pp = i["ple_w_proj"][0].reshape(2, P, 2, 4, P).transpose(2, 1, 3, 0, 4).reshape(2, P, CH)
    parts = [tiles(xr), tiles(gr), tiles(kc), tiles(vc), tiles(ks), tiles(kw), vv, tiles(q), tiles(gmr), tiles(gma),
             w1[0], w1[1], tiles(i["w_out"][0]), tiles(ffn), dn, tiles(i["ple_w_gate"][0]), pp,
             np.zeros((2, P, CH), np.float32)]
    return parts


def down_chunks(w):
    w = np.concatenate([w, np.zeros((24 * P - FF, D), w.dtype)])
    return w.reshape(3, 8, P, 8, P).transpose(3, 0, 2, 1, 4).reshape(24, P, CH)


def first_params(i):
    t = {"mix_pre": vec(i["norm_mix_pre"][0]), "mix_post": vec(i["norm_mix_post"][0]),
         "ffn_pre": vec(i["norm_ffn_pre"][0]), "ffn_post": vec(i["norm_ffn_post"][0]),
         "conv_w": i["conv_w"][0].reshape(4, KT, P).transpose(2, 0, 1).reshape(P, -1),
         "conv_b": vec(i["conv_b"][0]), "ba": vec(i["lru_ba"][0]), "bx": vec(i["lru_bx"][0]),
         "lam": vec(i["lru_lambda"][0]), "ple_b": vec(i["ple_b_gate"][0]),
         "wa": block_diag(i["lru_wa"][0]), "wx": block_diag(i["lru_wx"][0]),
         "w2k": np.concatenate([i["cmp_k_w2"][0].reshape(2, P, 1, HD)] * 2, axis=2).transpose(1, 0, 2, 3).reshape(P, -1),
         "w2v": i["cmp_v_w2"][0].reshape(2, P, HD).transpose(1, 0, 2).reshape(P, -1),
         "pos_k": i["cmp_pos_k"][0].reshape(16, P).T, "pos_v": i["cmp_pos_v"][0].reshape(16, P).T,
         "w_gate": i["w_in"][0][:, 4608:4656].reshape(KT, P, 48).transpose(1, 0, 2).reshape(P, -1)}
    return np.ascontiguousarray(np.concatenate([t[n] for n, _ in PAR1_FIELDS], axis=1))


def vec2(v):
    return v.reshape(v.shape[0], -1, P).transpose(2, 0, 1)


def second_stream(i, l):
    w = i["w_in_2"][l]
    at = np.cumsum([0] + [256] * 10 + [256, 128, 32])
    a, g, q, zf, zb, v, gg, gb, gc, xin, cq, ckv, kr = [w[:, x:y] for x, y in zip(at[:-1], at[1:])]
    z = np.zeros((D, P), w.dtype)
    z[:, 64:96] = kr
    token = lambda m: m.reshape(2, 4, P, 256).transpose(0, 2, 1, 3).reshape(2, P, CH)
    up = np.zeros((4, P, CH), w.dtype)
    up[0, :, :768] = i["m_wuq_2"][l].reshape(2, P, 384).transpose(1, 0, 2).reshape(P, 768)
    up[1, :, :512] = i["m_wukv_2"][l].reshape(P, 4, 2, HD).transpose(0, 2, 1, 3).reshape(P, 512)
    xkv = i["x_wkv_2"][l].reshape(D, 4, 2, HD).transpose(0, 2, 1, 3).reshape(D, 2, 256)
    xo = i["x_wo_2"][l].reshape(2, P, 2, 4, P).transpose(2, 1, 3, 0, 4).reshape(2, P, CH)
    ffn = i["f_w13_2"][l].reshape(D, 2, FT, P).transpose(0, 2, 1, 3).reshape(D, -1)
    return [tiles(a), tiles(g), tiles(zf), tiles(zb), tiles(q), tiles(gg), token(v), tiles(cq), tiles(ckv), tiles(z),
            tiles(xin), tiles(gc), tiles(gb), up, tiles(xkv[:, 0]), token(xkv[:, 1]), tiles(i["w_out_2"][l]),
            tiles(i["x_wq_2"][l]), xo, tiles(ffn), down_chunks(i["f_w2_2"][l])]


def second_params(i):
    rows = lambda v: np.pad(v, ((0, 0), (0, P - v.shape[1]))).T[:, :, None]
    taps = lambda w: w.reshape(2, -1, 2, P).transpose(3, 0, 1, 2).reshape(P, 2, -1)
    t = {"g_mix": vec2(i["g_mix_2"]), "a_dw_w": taps(i["a_dw_w_2"]), "a_dw_b": vec2(i["a_dw_b_2"]),
         "a_ln_g": vec2(i["a_ln_g_2"]), "a_ln_b": vec2(i["a_ln_b_2"]), "h_onorm": vec2(i["h_onorm_g_2"]),
         "c_dw_w": taps(i["c_dw_w_2"]), "c_dw_b": vec2(i["c_dw_b_2"]), "qa": vec2(i["m_qa_g_2"]),
         "kva": vec2(i["m_kva_g_2"]), "qn": rows(i["m_qn_g_2"]), "kn": rows(i["m_kn_g_2"]),
         "g_branch": vec2(i["g_branch_2"]), "g_xq": vec2(i["g_xq_2"]), "g_mem": vec2(i["g_mem_2"]),
         "x_qn": vec2(np.concatenate([i["x_qn_g_2"]] * 2, axis=1)),
         "x_kn": vec2(np.concatenate([i["x_kn_g_2"]] * 2, axis=1)), "g_ffn": vec2(i["g_ffn_2"])}
    return np.ascontiguousarray(np.concatenate([t[n] for n, _ in PAR2_FIELDS], axis=2))


def kernel(**inputs):
    import concourse.bacc as _bacc
    from concourse.bass_utils import run_bass_kernel_spmd as _run

    i = {n: np.asarray(a) for n, a in inputs.items()}
    arrays = {
        "wstream": np.concatenate(first_stream(i) + second_stream(i, 0) + second_stream(i, 1)),
        "consts": constants(),
        "par1": first_params(i),
        "xT": np.ascontiguousarray(i["x"][0].T),
        "pT": np.ascontiguousarray(i["p"][0, 0].T),
        "par2": second_params(i),
        "gamma": np.ascontiguousarray(i["h_gamma_2"].reshape(2, 2, 2, P).transpose(3, 1, 0, 2).reshape(P, 2, 4)),
        "memT": np.ascontiguousarray(i["mem_2"][0].T),
        "positions": np.ascontiguousarray(i["positions_2"].astype(np.int32)),
    }
    nc = _bacc.Bacc("TRN2", target_bir_lowering=False, num_devices=1)
    args = [nc.dram_tensor(n, a.shape, mybir.dt.from_np(a.dtype), kind="ExternalInput").ap() for n, a in arrays.items()]
    out = nc.dram_tensor("out", (D, S), F32, kind="ExternalOutput").ap()
    program(nc, *args, out)
    r = _run(nc, [arrays], core_ids=[0])
    got = r.results[0]["out"]
    return np.ascontiguousarray(got.T)[None]
```

```python
from contextlib import ExitStack

import numpy as np
import concourse.bass as bass
from concourse import mybir

F32 = mybir.dt.float32
I32 = mybir.dt.int32
F32R = mybir.dt.float32r
ALU = mybir.AluOpType
ACT = mybir.ActivationFunctionType
AX = mybir.AxisListType

P = 128
S = 512
D = 1024
KT = D // P
TT = S // P
HEADS = 16
HD = 64
FF = 2816
FT = FF // P
CC = 32
EPS = 1e-6
BIG = 1e30
SLOTS = 4
CH = 1024


def table(fields):
    at, out = 0, {}
    for name, n in fields:
        out[name] = (at, n)
        at += n
    return out, at


CONST_FIELDS = [("ident", 128), ("ones", 128), ("halves", 128), ("dist", 512), ("zeros", 512),
                ("cmp_dist", TT * CC), ("cmp_neg", TT * CC), ("slopes", HEADS), ("eps", 1),
                ("rot", 96), ("inv_freq", 1), ("levels", 7 * 128)]
CONST, NCONST = table(CONST_FIELDS)
PAR1_FIELDS = [("mix_pre", KT), ("mix_post", KT), ("ffn_pre", KT), ("ffn_post", KT), ("conv_w", 4 * KT),
               ("conv_b", KT), ("ba", KT), ("bx", KT), ("lam", KT), ("ple_b", KT), ("wa", KT * P),
               ("wx", KT * P), ("w2k", 2 * P), ("w2v", 2 * HD), ("pos_k", 16), ("pos_v", 16),
               ("w_gate", KT * 48)]
PAR1, NPAR1 = table(PAR1_FIELDS)

PAR2_FIELDS = [("g_mix", KT), ("a_dw_w", 31 * 2), ("a_dw_b", 2), ("a_ln_g", 2), ("a_ln_b", 2), ("h_onorm", 2),
               ("c_dw_w", 3 * 2), ("c_dw_b", 2), ("qa", 2), ("kva", 1), ("qn", 1), ("kn", 1), ("g_branch", KT),
               ("g_xq", KT), ("g_mem", KT), ("x_qn", 1), ("x_kn", 1), ("g_ffn", KT)]
PAR2, NPAR2 = table(PAR2_FIELDS)

R_XR, R_GR, R_CMP_IN, R_KK, R_V, R_Q, R_GMR, R_GMA, R_W1K, R_W1V, R_WOUT = 0, 2, 4, 5, 6, 7, 9, 11, 13, 14, 15
R_FFN, R_DOWN, R_PLEG, R_PLEP = 17, 28, 34, 36
ROUNDS1 = 37
M_XR, M_GR, M_CMP_IN, M_KK, M_Q, M_GMR, M_GMA, M_W1K, M_W1V, M_WOUT = 0, 4, 8, 10, 12, 16, 20, 24, 25, 26
M_FFN, M_DOWN, M_PLEG, M_PLEP = 30, 52, 56, 60
PAIRS1 = 64
L_A, L_Z, L_QG, L_VCQ, L_KVX, L_C, L_UP, L_XKV, L_WOUT, L_XQO, L_FFN, L_DOWN = 0, 1, 2, 3, 4, 5, 6, 7, 8, 10, 11, 22
ROUNDS2 = 28
N_A, N_Z, N_QG, N_CQ, N_KVX, N_C, N_UQ, N_UK, N_UV, N_XK, N_WOUT, N_XQ, N_XO, N_FFN, N_DOWN = (
    0, 2, 4, 6, 7, 9, 11, 13, 15, 16, 17, 21, 22, 26, 48)
PAIRS2 = 52
JOBS = {}
for _name, _n in [("mix", 8), ("o0", 1), ("o1", 1), ("ln", 2), ("bA", 2), ("bB", 2), ("bC", 2), ("qa", 2), ("kva", 1),
                  *[(f"hd{i}", 1) for i in range(8)], ("bD", 2), ("mem", 8), ("xk0", 1), ("xk1", 1), ("xq", 8),
                  ("xh0", 1), ("xh1", 1), ("ffn", 8)]:
    JOBS[_name] = (len(JOBS), sum(n for _, _, n in JOBS.values()), _n)
NJOBS, NSQ2 = len(JOBS), 60
NM = 256
LAYERS = 2
LN_EXP = "natural_log_exp_and_others"
NSPLIT1 = 4 * R_W1K
NSPLIT = 68
NSPLIT2 = 12 + 8
HLEV = 9


def program(nc, wstream, const_d, par1_d, xT, pT, par2_d, gamma_d, memT, pos_d, out):
    with ExitStack() as ctx:
        def sb(name, n):
            return ctx.enter_context(nc.sbuf_tensor(name, [P, n], F32))

        def sem(name):
            return ctx.enter_context(nc.semaphore(name))

        X = sb("X", KT * S)[:, :].rearrange("p (k n) -> p k n", k=KT)
        CT = sb("CT", NCONST)
        rstd = sb("rstd", S)[:, :]
        small = sb("small", 416)
        PT1 = sb("PT1", NPAR1)
        SHARED = [("H", KT * S), ("W", SLOTS * CH), ("WORK", 34208)]
        with ExitStack() as earlier:
            H, W, WORK = (earlier.enter_context(nc.sbuf_tensor(name, [P, n], F32)) for name, n in SHARED)
        COLS = [("H_c", KT * S), ("W_c", SLOTS * CH), ("conv_in", 8216), ("W_a0", CH), ("W_a1", CH), ("held", 12288),
                ("H_lo_a", KT * S), ("held2", 1024), ("W_b0", CH), ("W_b1", CH)]
        with ExitStack() as earlier:
            _, _, _, WA0, WA1, _, HLA, _, WB0, WB1 = (
                earlier.enter_context(nc.sbuf_tensor(name, [P, n], F32R)) for name, n in COLS)
        HLA = HLA[:, :].rearrange("p (k n) -> p k n", n=S)
        WHA, WHB = [WA0[:, :], WA1[:, :]], [WB0[:, :], WB1[:, :]]
        LAYER = [("H_y", KT * S), ("W_y", SLOTS * CH), ("kept_y", 3072), ("W_y0", CH), ("W_y1", CH), ("held_y", 8256),
                 ("H_hi_y", KT * S), ("H_lo_y", KT * S)]
        with ExitStack() as earlier:
            _, _, _, WY0, WY1, _, HHY, HLY = (
                earlier.enter_context(nc.sbuf_tensor(name, [P, n], F32R)) for name, n in LAYER)
        HHY, HLY = (t[:, :].rearrange("p (k n) -> p k n", n=S) for t in (HHY, HLY))
        WHY = [WY0[:, :], WY1[:, :]]
        MIXED = [("H_z", KT * S), ("W_z", SLOTS * CH), ("kept_z", 3072), ("mixed_hi", KT * S), ("held_z", 6208),
                 ("W_z0", CH), ("held_z1", 4096), ("W_z1", CH), ("held_z2", 2048), ("mixed_lo", KT * S)]
        with ExitStack() as earlier:
            _, _, _, CATH, _, WZ0, _, WZ1, _, CATL = (
                earlier.enter_context(nc.sbuf_tensor(name, [P, n], F32R)) for name, n in MIXED)
        CATH, CATL = (t[:, :].rearrange("p (k n) -> p k n", n=S) for t in (CATH, CATL))
        WHZ = [WZ0[:, :], WZ1[:, :]]
        PARTS = [("H_r", KT * S), ("W_r", SLOTS * CH), ("kept", 3072), ("inside_hi", FT * S), ("inside_lo", FT * S),
                 ("H_lo", KT * S), ("W_hi1", CH), ("gates", 2112), ("W_hi0", CH), ("rest", 34208 - 33856)]
        H_R, W_R, _, ACH, ACL, HL, WH1, _, WH0, _ = (
            ctx.enter_context(nc.sbuf_tensor(name, [P, n], F32R)) for name, n in PARTS)
        ACH, ACL, HL = (t[:, :].rearrange("p (k n) -> p k n", n=S) for t in (ACH, ACL, HL))
        WH = [WH0[:, :], WH1[:, :]]
        H, H_R = (t[:, :].rearrange("p (k n) -> p k n", k=KT) for t in (H, H_R))
        W, W_R = (t[:, :].rearrange("p (s n) -> p s n", s=SLOTS) for t in (W, W_R))

        def c(name, a=0, b=None):
            at, n = CONST[name]
            return CT[:, at + a:at + (n if b is None else b)]

        def p1(name, a=0, b=None):
            at, n = PAR1[name]
            return PT1[:, at + a:at + (n if b is None else b)]

        def area(at, *shape):
            n = int(np.prod(shape))
            ap = WORK[:, at:at + n]
            if len(shape) == 2:
                return ap.rearrange("p (a b) -> p a b", a=shape[0])
            if len(shape) == 3:
                return ap.rearrange("p (a b c) -> p a b c", a=shape[0], b=shape[1])
            return ap

        ident = c("ident")
        ones = c("ones")

        G = area(0, KT, S)
        XR = area(4096, KT, 515)
        GA = area(4096, KT, S)
        Q = area(8216, KT, S)
        KK = area(12312, 4, S)
        KST = area(14360, 4, 2, 256)
        CB = area(14360, TT, HEADS, CC)
        KCD = area(16408, 2, 4, 256)
        K2 = area(18456, 16, 4, CC)
        V = area(20504, TT, S)
        YC = area(22552, KT, S)
        T0 = 26648
        tmp = [area(T0 + i * S, S) for i in range(12)]
        VBD = area(T0 + 12 * S, 4, 256)
        HFA = area(22552, KT, S)
        HF = area(25600, KT, S)
        PP = area(1024, 2, S)
        SQ = [tmp[10], tmp[11]]
        SG = [tmp[8], tmp[9]]
        QT = [tmp[3], tmp[2]]
        SD = [[tmp[8], tmp[9]], [area(14360, S), area(14872, S)]]
        YT = [tmp[10], tmp[11]]
        GT = small[:, 0:192].rearrange("p (b h t) -> p b h t", b=3, h=HEADS)
        lru = small[:, 192:192 + 8 * KT].rearrange("p (f k) -> p f k", f=8)
        den = small[:, 256:256 + 64]
        sml = small[:, 320:416]
        slope = small[:, 192:196].rearrange("p (u f) -> p u f", u=2)
        gts = small[:, 196:228].rearrange("p (u b f t) -> p u b f t", u=2, b=2, f=2)
        gsteps = small[:, 196:228]
        KCT = area(T0 + 14 * S, 4 * CC)
        HK = area(T0 + 14 * S + 128, 2, 128)

        B = [ctx.enter_context(nc.psum_tensor(f"B{i}", [P, 512], F32)) for i in range(8)]

        const_in = sem("const_in")
        x_in = sem("x_in")
        p_in = sem("p_in")
        w_loaded = [sem(f"w_loaded{s}") for s in range(SLOTS)]
        chunk_done = sem("chunk_done")
        evac = [sem("evac0"), sem("evac1")]
        sq_full = sem("sq_full")
        sq_used = sem("sq_used")
        rstd_done = sem("rstd_done")
        h_done = sem("h_done")
        x_done = sem("x_done")
        pad_done = sem("pad_done")
        coef_done = sem("coef_done")
        coef_e = sem("coef_e")
        conv_done = sem("conv_done")
        gate_full = sem("gate_full")
        gate_read = sem("gate_read")
        lru_a = sem("lru_a")
        lru_t = sem("lru_t")
        lru_sqrt = sem("lru_sqrt")
        lru_y = sem("lru_y")
        v_evac = sem("v_evac")
        g_full = sem("g_full")
        g_evac = sem("g_evac")
        shuffled = sem("shuffled")
        k2_done = sem("k2_done")
        part_full = sem("part_full")
        kv2_full = sem("kv2_full")
        kv2_done = sem("kv2_done")
        cs_full = sem("cs_full")
        cs_m = sem("cs_m")
        cs_e = sem("cs_e")
        cs_p = sem("cs_p")
        ct_full = sem("ct_full")
        ct_done = sem("ct_done")
        co_full = sem("co_full")
        co_done = sem("co_done")
        q_cur = sem("q_cur")
        sd_done = sem("sd_done")
        qk_full = sem("qk_full")
        sc_done = sem("sc_done")
        exp_done = sem("exp_done")
        tr_full = sem("tr_full")
        p_scaled = sem("p_scaled")
        pt_done = sem("pt_done")
        pv_full = sem("pv_full")
        o_done = sem("o_done")
        o_added = sem("o_added")
        out_done = sem("out_done")

        SIN, COS = area(0, S), area(S, S)
        MEM = area(1024, KT, NM)
        CAT = area(3072, KT, S)
        CATF = area(21568, KT, S)
        AH = area(7168, 2, 542)
        KF = area(8256, 2, 2, S)
        QH = area(10304, 2, S)
        GG = area(11328, 2, S)
        VH = area(12352, TT, 256)
        AD = area(13376, 2, TT, 2 * P)
        AO7 = area(15424, 4, TT, P)
        AO8 = area(17472, 4, TT, 256)
        PS = area(21568, 4, 2 * S)
        T1 = 25664
        tm2 = [area(T1 + i * S, S) for i in range(16)]
        QC = [area(T1 + i * 1024, 2 * S) for i in range(2)]
        KC = [area(T1 + 2048 + i * 1024, 2 * S) for i in range(2)]
        CQ = area(T1 + 4096, 2, S)
        CKV, KR = tm2[10], tm2[11]
        HS = [tm2[12], tm2[13]]
        QM = area(8256, 4, S)
        KM = area(10304, 4, S)
        VM = area(12352, TT, 256)
        MN = area(14400, KT, NM)
        XK = area(16448, 2, NM)
        XV = area(16960, 2, 256)
        XQ = area(17472, 2, S)
        OXT = area(19520, 2, S)
        RB = area(20544, S)
        late = PAR1["wa"][0]
        PALL = PT1[:, late:late + LAYERS * NPAR2].rearrange("p (l n) -> p l n", l=LAYERS)
        late += LAYERS * NPAR2
        GAM = PT1[:, late:late + 8].rearrange("p (l n) -> p l n", l=2)
        LBS = PT1[:, late + 8:late + 56].rearrange("p (f l n) -> p f l n", f=6, l=2)
        LBC = PT1[:, late + 56:late + 64].rearrange("p (f n) -> p f n", f=2)
        PCUR = PT1[:, late + 64:late + 64 + NPAR2]
        late += 64 + NPAR2
        GCX = PT1[:, late:late + 2 * 514].rearrange("p (a n) -> p a n", a=2)
        GB = PT1[:, late + 1028:late + 1028 + 2 * S].rearrange("p (a n) -> p a n", a=2)

        def p2(name, a=0, b=None):
            at, n = PAR2[name]
            return PCUR[:, at + a:at + (n if b is None else b)]

        par2_in = sem("par2_in")
        mem_in = sem("mem_in")
        pos_in = sem("pos_in")
        rope_arg = sem("rope_arg")
        rope_done = sem("rope_done")
        gam_e = sem("gam_e")
        lb_done = sem("lb_done")
        cur_done = sem("cur_done")
        ap_done = sem("ap_done")
        h2_done = sem("h2_done")
        ah_done = sem("ah_done")
        edge_done = sem("edge_done")
        hg_qk = sem("hg_qk")
        hg_up = sem("hg_up")
        hg_ps = sem("hg_ps")
        hg_mg = sem("hg_mg")
        hg_ev = sem("hg_ev")
        vh_evac = sem("vh_evac")
        o_full = sem("o_full")
        oc_done = sem("oc_done")
        mean_full = sem("mean_full")
        cen_done = sem("cen_done")
        silu_in = sem("silu_in")
        cat_done = sem("cat_done")
        rot_full = sem("rot_full")
        qk_ready = sem("qk_ready")
        mn_done = sem("mn_done")
        xv_done = sem("xv_done")
        layer_end = sem("layer_end")
        split_done = sem("split_done")
        ac_done = sem("ac_done")

        block = ctx.enter_context(nc.Block())

        def waits(eng, *them):
            them = [(sm, v if isinstance(v, int) else eng.to_reg(v)) for sm, v in them]
            eng.wait_ge(const_in, 32)
            for sm, v in them:
                eng.wait_ge(sm, v)

        @block.sync
        def _(sp):
            sp.dma_start(X, xT.rearrange("(k p) n -> p k n", p=P)).then_inc(x_in, 16)
            sp.dma_start(CT[:, :], const_d).then_inc(const_in, 16)
            sp.dma_start(PT1[:, :], par1_d).then_inc(const_in, 16)
            with sp.Fori(0, wstream.shape[0] // SLOTS) as i:
                for s in range(SLOTS):
                    sp.wait_ge(chunk_done, i * SLOTS + s + 1)
                    sp.dma_start(W[:, s, :], wstream[bass.ds(i * SLOTS + s, 1), :, :].rearrange("o p n -> p (o n)")
                                 ).then_inc(w_loaded[s], 16)
            for s in range(SLOTS):
                sp.wait_ge(w_loaded[s], 16 * (wstream.shape[0] // SLOTS))

        @block.tensor
        def _(pe):
            pe.sem_inc(chunk_done, SLOTS)

            def chunk(rnd, s):
                pe.wait_ge(w_loaded[s], 16 * (rnd + 1))

            def bank(pair, b):
                pe.wait_ge(evac[b], pair + 1)

            def three(dst, wh, wl, hi, lo, first, last):
                pe.matmul(dst, wh, hi, start=first, stop=False, skip_group_check=True)
                pe.matmul(dst, wh, lo, start=False, stop=False, skip_group_check=True)
                return pe.matmul(dst, wl, hi, start=False, stop=last, skip_group_check=True)

            def split_columns(n, pair, wh, hi, lo, first=None, after=None):
                for s in range(4):
                    pe.wait_ge(split_done, n + s + 1)
                    bank(pair + s // 2, s % 2)
                    for k in range(KT):
                        if s == 0 and first is not None:
                            first(k)
                        mm = three(B[s % 2][:, :], wh[s % 2][:, k * P:(k + 1) * P], W_R[:, s, k * P:(k + 1) * P],
                                   hi(k), lo(k), k == 0, k == KT - 1)
                    mm.then_inc(chunk_done, 1)
                    if after is not None:
                        after(s)

            def columns(rnd, pair, rhs, first=None, after=None):
                for s in range(4):
                    chunk(rnd, s)
                    bank(pair + s // 2, s % 2)
                    for k in range(KT):
                        if s == 0 and first is not None:
                            first(k)
                        mm = pe.matmul(B[s % 2][:, :], W[:, s, k * P:(k + 1) * P], rhs(k),
                                       start=(k == 0), stop=(k == KT - 1))
                    mm.then_inc(chunk_done, 1)
                    if after is not None:
                        after(s)

            def stat(n, first, last):
                pe.wait_ge(sq_full, n + 1)
                mm = pe.matmul(B[7][:, :], ones, SQ[n % 2], start=first, stop=last)
                mm.then_inc(sq_used, 1)

            h_tile = lambda k: H[:, k, :]
            hr_tile = lambda k: H_R[:, k, :]
            hl_tile = lambda k: HLA[:, k, :]

            def h_first(base):
                return lambda k: pe.wait_ge(h_done, base + k + 1)

            pe.wait_ge(const_in, 32)
            for k in range(KT):
                stat(k, k == 0, k == KT - 1)
            with pe.Fori(0, 2) as i:
                split_columns(4 * R_XR + 4 * i, M_XR + 2 * i, WHA, hr_tile, hl_tile, h_first(0))
            with pe.Fori(0, 2) as i:
                split_columns(4 * R_GR + 4 * i, M_GR + 2 * i, WHA, hr_tile, hl_tile)

            def gates(t):
                pe.wait_ge(conv_done, t + 1)
                if t:
                    pe.wait_ge(gate_read, t)
                pe.matmul(B[4][:, :], p1("wa", t * P, (t + 1) * P), tmp[t % 2], start=True, stop=True)
                pe.matmul(B[5][:, :], p1("wx", t * P, (t + 1) * P), tmp[t % 2], start=True, stop=True
                          ).then_inc(gate_full, 1)

            split_columns(4 * R_CMP_IN, M_CMP_IN, WHA, hr_tile, hl_tile, after=lambda s: gates(s))
            split_columns(4 * R_KK, M_KK, WHA, hr_tile, hl_tile, after=lambda s: gates(4 + s))
            VB = [2, 3, 6, 7]
            for s in range(4):
                pe.wait_ge(split_done, 4 * R_V + s + 1)
                for t in range(TT):
                    for kk in range(2):
                        k = 2 * s + kk
                        tok, col = slice(t * P, (t + 1) * P), slice(kk * S, (kk + 1) * S)
                        mm = three(B[VB[t]][:, :], H_R[:, k, tok], HLA[:, k, tok], WHA[s % 2][:, col], W_R[:, s, col],
                                   k == 0, k == KT - 1)
                mm.then_inc(chunk_done, 1)
            pe.wait_ge(v_evac, 1)
            for t in range(TT):
                for k in range(KT):
                    for part in (H_R, HLA):
                        mm = pe.matmul(B[2][:, t * 48:(t + 1) * 48], part[:, k, t * P:(t + 1) * P].bitcast(F32),
                                       p1("w_gate", k * 48, (k + 1) * 48), start=(k == 0 and part is H_R),
                                       stop=(k == KT - 1 and part is HLA))
            mm.then_inc(g_full, 1)
            with pe.Fori(0, 2) as i:
                split_columns(4 * R_Q + 4 * i, M_Q + 2 * i, WHB, hr_tile, hl_tile)
            with pe.Fori(0, 2) as i:
                split_columns(4 * R_GMR + 4 * i, M_GMR + 2 * i, WHB, hr_tile, hl_tile)
            with pe.Fori(0, 2) as i:
                split_columns(4 * R_GMA + 4 * i, M_GMA + 2 * i, WHB, hr_tile, hl_tile)

            for kv, (rnd, pair) in enumerate([(R_W1K, M_W1K), (R_W1V, M_W1V)]):
                pe.wait_ge(k2_done, kv + 1)
                bank(pair, 0)
                bank(pair, 1)
                for s in range(4):
                    chunk(rnd, s)
                    for jj in range(4):
                        jp = 4 * s + jj
                        for ht in range(2):
                            mm = pe.matmul(B[ht][:, 0:128], W[:, s, jj * 256 + ht * P:jj * 256 + (ht + 1) * P],
                                           K2[:, jp, :, :].rearrange("p g c -> p (g c)"),
                                           start=(jp == 0), stop=(jp == 15), skip_group_check=True)
                    mm.then_inc(chunk_done, 1)
                pe.wait_ge(evac[0], pair + 2)
                pe.wait_ge(evac[1], pair + 2)
                if kv == 0:
                    for ht in range(2):
                        mm = pe.matmul(B[3][:, 0:128], p1("w2k", ht * P, (ht + 1) * P), HK[:, ht, :],
                                       start=(ht == 0), stop=(ht == 1))
                    mm.then_inc(kv2_full, 1)
                else:
                    pe.wait_ge(g_evac, 1)
                    for g in range(4):
                        for hh in range(4):
                            for ht in range(2):
                                mm = pe.matmul(B[2][32 * hh:32 * hh + 32, g * HD:(g + 1) * HD],
                                               HK[:, ht, g * CC:(g + 1) * CC], p1("w2v", ht * HD, (ht + 1) * HD),
                                               start=(ht == 0), stop=(ht == 1), skip_group_check=True)
                    mm.then_inc(kv2_full, 1)

            pe.wait_ge(kv2_done, 2)

            def compressed_scores(t):
                if t:
                    pe.wait_ge(cs_m, t)
                for h in range(HEADS):
                    g = h // 4
                    half = g % 2
                    tile = 4 * (g // 2) + h % 4
                    at = (4 * (g // 2) + h % 4) * CC
                    mm = pe.matmul(B[4 + half][:, at:at + CC], Q[64 * half:64 * half + 64, tile, t * P:(t + 1) * P],
                                   KCT[64 * half:64 * half + 64, g * CC:(g + 1) * CC], start=True, stop=True)
                mm.then_inc(cs_full, 1)

            compressed_scores(0)
            for t in range(TT):
                if t + 1 < TT:
                    compressed_scores(t + 1)
                pe.wait_ge(cs_p, t + 1)
                for g in range(4):
                    mm = pe.transpose(B[6][:, g * P:(g + 1) * P], tmp[2 * (t % 2)][:, g * P:(g + 1) * P], ident)
                mm.then_inc(ct_full, 1)
                pe.wait_ge(ct_done, t + 1)
                for g in range(4):
                    for hh in range(4):
                        mm = pe.matmul(B[2 + g // 2][64 * (g % 2):64 * (g % 2) + 64, hh * P:(hh + 1) * P],
                                       VBD[:, g, hh * HD:(hh + 1) * HD], tmp[1][:, g * P:(g + 1) * P],
                                       start=True, stop=True)
                mm.then_inc(co_full, 1)
                pe.wait_ge(co_done, t + 1)

            def run_attention(n, groups, per, steps):
                def do_qk(s):
                    lhsT, rhs = steps[s][:2]
                    pe.wait_ge(sc_done, n + s + 1)
                    pe.matmul(B[4 + s % 2][:, 0:rhs.shape[-1]], lhsT, rhs, start=True, stop=True
                              ).then_inc(qk_full, 1)

                def do_tr(s):
                    pe.wait_ge(p_scaled, n + s + 2)
                    pe.wait_ge(pt_done, n + s + 1)
                    for kt in range(steps[s][2]):
                        mm = pe.transpose(B[6 + s % 2][:, kt * P:(kt + 1) * P],
                                          tmp[4 + s % 2][:, kt * P:(kt + 1) * P], ident)
                    mm.then_inc(tr_full, 1)

                def do_pv(s):
                    kts, v, half, t, opens, closes = steps[s][2:]
                    if s % per == 0:
                        pe.wait_ge(o_done, groups + s // per + 1)
                    pe.wait_ge(pt_done, n + s + 3)
                    for kt in range(kts):
                        mm = pe.matmul(B[2 + (s // per) % 2][64 * half:64 * half + 64, t * P:(t + 1) * P], v(kt),
                                       tmp[6 + s % 2][:, kt * P:(kt + 1) * P], start=(opens and kt == 0),
                                       stop=(closes and kt == kts - 1), skip_group_check=True)
                    mm.then_inc(pv_full, 1)

                for s in range(len(steps) + 3):
                    if s < len(steps):
                        do_qk(s)
                    if 2 <= s < len(steps) + 2:
                        do_tr(s - 2)
                    if s >= 3:
                        do_pv(s - 3)

            for j in range(2):
                with pe.Fori(0, 2) as i:
                    pe.wait_ge(q_cur, i + 2 * j + 1)
                    steps = []
                    for u in range(2):
                        for br in range(2):
                            for half in range(2):
                                for t in range(TT):
                                    h0 = 64 * half
                                    steps.append((QT[u][h0:h0 + 64, t * P:(t + 1) * P],
                                                  KK[h0:h0 + 64, 2 * br + j, 0:(t + 1) * P], t + 1,
                                                  lambda kt, br=br, g=2 * j + half:
                                                  V[:, kt, br * 256 + g * HD:br * 256 + (g + 1) * HD],
                                                  half, t, br == 0 and t == 0, br == 1))
                    run_attention(32 * i + 64 * j, 2 * i + 4 * j, 16, steps)

            pe.wait_ge(o_added, 2 + KT)

            g_tile = lambda k: G[:, k, :]
            for i in range(2):
                columns(R_WOUT + i, M_WOUT + 2 * i, g_tile,
                        after=lambda s, i=i: stat(8 + 4 * i + s - 1, 4 * i + s - 1 == 0, False) if 4 * i + s else None)
            stat(15, False, True)
            for k in range(KT):
                if k == 0:
                    pe.wait_ge(rstd_done, 2)
                stat(16 + k, k == 0, k == KT - 1)
            with pe.Fori(0, FT // 2) as i:
                split_columns(NSPLIT1 + 4 * i, M_FFN + 2 * i, WH, hr_tile, lambda k: HL[:, k, :], h_first(8))

            def down(n0, pair0, nsq, wh, hi, lo):
                for cix in range(4):
                    bank(pair0 + cix // 2, cix % 2)
                    for q in range(3):
                        ch = 3 * cix + q
                        pe.wait_ge(split_done, n0 + ch + 1)
                        for kk in range(min(KT, FT - 8 * q)):
                            k = 8 * q + kk
                            mm = three(B[cix % 2][:, :], wh[ch % 2][:, kk * P:(kk + 1) * P],
                                       W_R[:, ch % 4, kk * P:(kk + 1) * P], hi[:, k, :], lo[:, k, :],
                                       k == 0, k == FT - 1)
                        mm.then_inc(chunk_done, 1)
                    if nsq is not None and cix:
                        nsq(cix - 1)
                if nsq is not None:
                    nsq(3)

            pe.wait_ge(ac_done, FT)
            for i in range(2):
                down(NSPLIT1 + 4 * FT // 2 + 12 * i, M_DOWN + 2 * i,
                     lambda q, i=i: stat(24 + 4 * i + q, 4 * i + q == 0, 4 * i + q == 7), WH, ACH, ACL)
            with pe.Fori(0, 2) as i:
                columns(R_PLEG + i, M_PLEG + 2 * i, lambda k: X[:, k, :], lambda k: pe.wait_ge(x_done, 8 + k + 1))
            pe.wait_ge(p_in, 16)
            for n in range(KT):
                if n % 4 == 0:
                    chunk(R_PLEP, n // 4)
                if n == KT - 1:
                    chunk(R_PLEP, 2)
                    chunk(R_PLEP, 3)
                bank(M_PLEP + n // 2, n % 2)
                for k in range(2):
                    at = (n % 4) * 256 + k * P
                    mm = pe.matmul(B[n % 2][:, :], W[:, n // 4, at:at + P], PP[:, k, :], start=(k == 0), stop=(k == 1))
                if n == KT - 1:
                    mm.then_inc(chunk_done, 3)
                else:
                    mm.then_inc(chunk_done if n % 4 == 3 else part_full, 1)

            with pe.Fori(0, LAYERS) as l:
                R0 = ROUNDS1 + ROUNDS2 * l
                M0 = PAIRS1 + PAIRS2 * l

                def stat2(job, q, lhsT=ones, parts=P, cols=S):
                    j, sq0, n = JOBS[job]
                    if q == 0:
                        pe.wait_ge(rstd_done, 4 + NJOBS * l + j)
                    pe.wait_ge(sq_full, 32 + NSQ2 * l + sq0 + q + 1)
                    pe.matmul(B[7][0:lhsT.shape[-1], 0:cols], lhsT, HS[(sq0 + q) % 2][0:parts, 0:cols],
                              start=(q == 0), stop=(q == n - 1)).then_inc(sq_used, 1)

                def h_wait(base):
                    return lambda k: pe.wait_ge(h2_done, 24 * l + base + k + 1)

                def one(rnd, s, pair, rhs, first=None):
                    chunk(R0 + rnd, s)
                    bank(M0 + pair, s % 2)
                    for k in range(KT):
                        if first is not None:
                            first(k)
                        r = rhs(k)
                        mm = pe.matmul(B[s % 2][:, 0:r.shape[-1]], W[:, s, k * P:(k + 1) * P], r,
                                       start=(k == 0), stop=(k == KT - 1))
                    mm.then_inc(chunk_done, 1)

                for q in range(KT):
                    stat2("mix", q)
                NS = NSPLIT1 + NSPLIT + (NSPLIT + NSPLIT2) * l
                for rnd, pair in ((L_A, N_A), (L_Z, N_Z), (L_QG, N_QG)):
                    split_columns(NS + 4 * rnd, M0 + pair, WHY, lambda k: HHY[:, k, :], lambda k: HLY[:, k, :],
                                  h_wait(0) if rnd == L_A else None)

                def hg_step(st):
                    pe.wait_ge(hg_qk, 10 * l + st + 1)
                    q = QH.rearrange("p a n -> p (a n)") if st == 0 else QC[st % 2]
                    k = KC[st % 2]
                    for hi in range(2):
                        for half in range(2):
                            bk = 2 * hi + half
                            if st:
                                pe.wait_ge(hg_mg, 32 * l + 4 * (st - 1) + bk + 1)
                            elif hi == 0 and half == 0:
                                pe.wait_ge(rstd_done, 4 + NJOBS * l + 1)
                            r = slice(64 * half, 64 * half + 64)
                            for i2 in range(2):
                                for ht in range(2):
                                    at = ht * S + (2 * hi + i2) * P
                                    mm = pe.matmul(B[4 + bk][:, (2 * i2 + ht) * P:(2 * i2 + ht + 1) * P],
                                                   k[r, at:at + P], q[r, at:at + P], start=True, stop=True)
                            mm.then_inc(hg_ps, 1)

                def chunk_of(n):
                    rnd, s = L_VCQ + n // 4, n % 4
                    if n < 2:
                        chunk(R0 + rnd, s)
                        for t in range(TT):
                            for kk in range(4):
                                k = 4 * s + kk
                                mm = pe.matmul(B[2 + t // 2][:, (t % 2) * 256:(t % 2) * 256 + 256],
                                               H[:, k, t * P:(t + 1) * P], W[:, s, kk * 256:(kk + 1) * 256],
                                               start=(k == 0 and t % 2 == 0), stop=(k == KT - 1),
                                               skip_group_check=True)
                        mm.then_inc(chunk_done, 1)
                    else:
                        one(rnd, s, {0: N_CQ, 1: N_KVX + s // 2, 2: N_C + s // 2}[n // 4], h_tile)

                for n in range(12):
                    chunk_of(n)
                    if n < 8:
                        hg_step(n)
                for st in (8, 9):
                    pe.wait_ge(hg_qk, 10 * l + st + 1)
                    q, k = QC[st % 2], KC[st % 2]
                    for ht in range(2):
                        for half in range(2):
                            r = slice(64 * half, 64 * half + 64)
                            if st == 8:
                                pe.wait_ge(hg_mg, 32 * l + 32)
                                for i in range(TT):
                                    mm = pe.matmul(B[4 + 2 * ht + half][:, i * P:(i + 1) * P],
                                                   k[r, ht * S + i * P:ht * S + (i + 1) * P],
                                                   q[r, ht * S + (i ^ 1) * P:ht * S + (i ^ 1) * P + P],
                                                   start=True, stop=True)
                                mm.then_inc(hg_ps, 1)
                            else:
                                for ii in range(2):
                                    bk = 4 + 2 * ii + half
                                    pe.wait_ge(hg_ev, 12 * l + 4 * ht + 2 * ii + half + 1)
                                    for i2 in range(2):
                                        i = 2 * ii + i2
                                        o = ht * S + (1 - ii) * 256
                                        mm = pe.matmul(B[bk][:, i2 * 256:i2 * 256 + 256],
                                                       k[r, ht * S + i * P:ht * S + (i + 1) * P], q[r, o:o + 256],
                                                       start=True, stop=True)
                                    mm.then_inc(hg_ps, 1)
                pe.wait_ge(hg_ev, 12 * l + 12)
                pe.wait_ge(vh_evac, l + 1)
                for ht in range(2):
                    for half in range(2):
                        hd = 2 * ht + half
                        for t in range(TT):
                            for i in range(TT):
                                if i == t:
                                    a = AD[:, half, i, ht * P:(ht + 1) * P]
                                elif i == t ^ 1:
                                    a = AO7[:, 2 * ht + half, i, :]
                                else:
                                    a = AO8[:, 2 * ht + half, i, (t % 2) * P:(t % 2 + 1) * P]
                                mm = pe.matmul(B[2 + ht][64 * half:64 * half + 64, t * P:(t + 1) * P],
                                               VH[:, i, hd * HD:(hd + 1) * HD], a, start=(i == 0), stop=(i == TT - 1))
                    mm.then_inc(o_full, 1)
                for ht in range(2):
                    stat2(f"o{ht}", 0, c("halves"))
                pe.wait_ge(ah_done, 2 * l + 2)
                for t in range(2):
                    mm = pe.matmul(B[6][:, :], ones, CAT[:, t, :], start=(t == 0), stop=(t == 1))
                mm.then_inc(mean_full, 1)
                for q in range(2):
                    stat2("ln", q)
                for job in ("bA", "bB", "bC"):
                    for q in range(2):
                        stat2(job, q)
                for q in range(2):
                    stat2("qa", q)
                stat2("kva", 0)
                chunk(R0 + L_UP, 0)
                pe.wait_ge(ap_done, NJOBS * l + JOBS["qa"][0] + 1)

                def head_rope(i):
                    stat2(f"hd{i}", 0, ones[0:96, 0:96], 96)
                    pe.wait_ge(qk_ready, 16 * l + 2 * i + 1)
                    dst = (QM if i < 4 else KM)[0:96, i % 4, :]
                    pe.matmul(B[4 + i % 2][0:96, :], c("rot")[0:96, :], dst, start=True, stop=True).then_inc(rot_full, 1)

                for i in range(8):
                    h = i % 4
                    pair = (N_UQ if i < 4 else N_UK) + h // 2
                    bank(M0 + pair, i % 2)
                    if i < 4:
                        for k in range(2):
                            mm = pe.matmul(B[i % 2][0:96, :], W[:, 0, k * 384 + h * 96:k * 384 + h * 96 + 96], CQ[:, k, :],
                                           start=(k == 0), stop=(k == 1))
                        mm.then_inc(chunk_done if i == 3 else part_full, 1)
                    else:
                        if i == 4:
                            chunk(R0 + L_UP, 1)
                            pe.wait_ge(ap_done, NJOBS * l + JOBS["kva"][0] + 1)
                        pe.matmul(B[i % 2][0:64, :], W[:, 1, h * HD:(h + 1) * HD], CKV, start=True, stop=True
                                  ).then_inc(part_full, 1)
                    if i:
                        head_rope(i - 1)
                chunk(R0 + L_UP, 2)
                chunk(R0 + L_UP, 3)
                for b in range(2):
                    bank(M0 + N_UV, b)
                    for t in range(2):
                        mm = pe.matmul(B[b][:, t * 256:(t + 1) * 256], CKV[:, (2 * b + t) * P:(2 * b + t + 1) * P],
                                       W[:, 1, 256:512], start=True, stop=True)
                    if b == 0:
                        mm.then_inc(part_full, 1)
                mm.then_inc(chunk_done, 3)
                head_rope(7)
                pe.wait_ge(qk_ready, 16 * l + 16)
                pe.wait_ge(evac[0], M0 + N_UV + 2)
                pe.wait_ge(evac[1], M0 + N_UV + 2)
                n = 128 + 32 * l
                run_attention(n, 8 + 4 * l, 8,
                              [(QM[0:96, h, t * P:(t + 1) * P], KM[0:96, h, :], TT,
                                lambda kt, h=h: VM[:, kt, h * HD:(h + 1) * HD], h % 2, t, True, True)
                               for h in range(4) for t in range(TT)])
                for q in range(2):
                    stat2("bD", q)
                for q in range(KT):
                    stat2("mem", q, cols=NM)
                for s in range(2):
                    one(L_XKV, s, N_XK, lambda k: MN[:, k, :],
                        (lambda k: pe.wait_ge(mn_done, KT * l + k + 1)) if s == 0 else None)
                for s in range(2, 4):
                    chunk(R0 + L_XKV, s)
                    for t in range(2):
                        for kk in range(4):
                            k = 4 * (s - 2) + kk
                            mm = pe.matmul(B[2 + t][:, 0:256], MN[:, k, t * P:(t + 1) * P],
                                           W[:, s, kk * 256:(kk + 1) * 256], start=(k == 0), stop=(k == KT - 1))
                    mm.then_inc(chunk_done, 1)
                for f in range(2):
                    stat2(f"xk{f}", 0, c("halves"), cols=NM)
                pe.wait_ge(ap_done, NJOBS * l + JOBS["bD"][0] + 1)
                for rnd in range(2):
                    split_columns(NS + 12 + 4 * rnd, M0 + N_WOUT + 2 * rnd, WHZ, lambda k: CATH[:, k, :],
                                  lambda k: CATL[:, k, :])
                for q in range(KT):
                    stat2("xq", q)
                for s in range(2):
                    one(L_XQO, s, N_XQ, h_tile, h_wait(8) if s == 0 else None)
                for f in range(2):
                    stat2(f"xh{f}", 0, c("halves"))
                pe.wait_ge(ap_done, NJOBS * l + JOBS["xh1"][0] + 1)
                pe.wait_ge(xv_done, l + 1)
                run_attention(n + 16, 10 + 4 * l, 8,
                              [(XQ[64 * (h % 2):64 * (h % 2) + 64, h // 2, t * P:(t + 1) * P],
                                XK[64 * (h % 2):64 * (h % 2) + 64, h // 2, :], 2,
                                lambda kt, h=h: XV[:, kt, h * HD:(h + 1) * HD], h % 2, t, True, True)
                               for h in range(4) for t in range(TT)])
                pe.wait_ge(o_done, 4 * l + 2 + 12)
                for i in range(KT):
                    if i % 4 == 0:
                        chunk(R0 + L_XQO, 2 + i // 4)
                    bank(M0 + N_XO + i // 2, i % 2)
                    for k in range(2):
                        at = (i % 4) * 256 + k * P
                        mm = pe.matmul(B[i % 2][:, :], W[:, 2 + i // 4, at:at + P], OXT[:, k, :],
                                       start=(k == 0), stop=(k == 1))
                    mm.then_inc(chunk_done if i % 4 == 3 else part_full, 1)
                for q in range(KT):
                    stat2("ffn", q)
                with pe.Fori(0, FT // 2) as i:
                    split_columns(NS + NSPLIT2 + 4 * i, M0 + N_FFN + 2 * i, WH, hr_tile,
                                  lambda k: HL[:, k, :], h_wait(16))
                pe.wait_ge(ac_done, FT * l + 2 * FT)
                for i in range(2):
                    down(NS + NSPLIT2 + 4 * FT // 2 + 12 * i, M0 + N_DOWN + 2 * i, None, WH, ACH, ACL)
                pe.sem_inc(sq_used, 1)

        @block.scalar
        def _(act):
            act.sem_inc(evac[0], 1)
            act.sem_inc(exp_done, 2)
            act.sem_inc(pt_done, 2)

            def full(n):
                act.wait_ge(chunk_done, n + 1 + SLOTS)

            def square(n, src):
                act.wait_ge(sq_used, n + 1)
                act.activation(SQ[n % 2], src, ACT.Square).then_inc(sq_full, 1)

            def rstds(n):
                act.wait_ge(sq_used, 2 + KT * (n + 1))
                act.activation(rstd, B[7][:, :], ACT.Ln, bias=c("eps"), scale=1.0 / D)
                act.drain()
                act.activation(rstd, rstd, ACT.Exp, scale=-0.5).then_inc(rstd_done, 1)

            act.preload_act_table_set(LN_EXP)
            act.wait_ge(const_in, 32)
            act.wait_ge(x_in, 16)
            for k in range(KT):
                square(k, X[:, k, :])
            rstds(0)
            act.wait_ge(coef_e, 1)
            act.activation(lru[:, 1, :], lru[:, 0, :], ACT.Exp, scale=-1.0).then_inc(coef_e, 1)
            with act.Fori(0, 2) as i:
                for s in range(4):
                    full(i * 4 + s + 4 * R_XR)
                    act.activation(XR[:, bass.ds(i * 4 + s, 1), 3:515], B[s % 2][:, :].unsqueeze(1), ACT.Identity
                                   ).then_inc(evac[s % 2], 1)
            act.preload_act_table(ACT.Gelu_apprx_tanh)
            with act.Fori(0, 2) as i:
                for s in range(4):
                    full(i * 4 + s + 4 * R_GR)
                    act.activation(G[:, bass.ds(i * 4 + s, 1), :], B[s % 2][:, :].unsqueeze(1), ACT.Gelu_apprx_tanh
                                   ).then_inc(evac[s % 2], 1)

            def lru_gates(t):
                act.wait_ge(gate_full, t + 1)
                if t == 0:
                    act.wait_ge(coef_done, 1)
                if t:
                    act.wait_ge(lru_t, t)
                act.activation(tmp[2], B[4][:, :], ACT.Tanh, bias=lru[:, 5, t:t + 1], scale=0.5)
                act.activation(tmp[3], B[5][:, :], ACT.Tanh, bias=lru[:, 6, t:t + 1], scale=0.5).then_inc(gate_read, 1)
                act.drain()
                if t >= 2:
                    act.wait_ge(lru_y, t - 1)
                act.activation(tmp[4], tmp[2], ACT.Tanh, bias=lru[:, 3, t:t + 1], scale=lru[:, 3, t:t + 1])
                act.activation(tmp[5 + t % 2], tmp[2], ACT.Exp, bias=lru[:, 4, t:t + 1], scale=lru[:, 4, t:t + 1]
                               ).then_inc(lru_a, 1)

            def lru_root(t):
                act.wait_ge(lru_t, t + 1)
                act.activation(tmp[9], tmp[9], ACT.Sqrt, scale=0.25).then_inc(lru_sqrt, 1)

            for t in range(8):
                full(4 * R_CMP_IN + t)
                if t < 4:
                    act.activation(KST[:, t, :, :], B[t % 2][:, :].rearrange("p (m r) -> p r m", r=2), ACT.Identity
                                   ).then_inc(evac[t % 2], 1)
                else:
                    act.activation(KK[:, t - 4, :], B[t % 2][:, :], ACT.Identity).then_inc(evac[t % 2], 1)
                if t:
                    lru_root(t - 1)
                lru_gates(t)
            lru_root(7)
            full(4 * R_V + 3)
            for t, b in enumerate([2, 3, 6, 7]):
                a = act.activation(V[:, t, :], B[b][:, :], ACT.Identity)
            a.then_inc(v_evac, 1)
            act.wait_ge(g_full, 1)
            act.activation(GT.rearrange("p b h t -> p t h b"),
                           B[2][:, 0:192].rearrange("p (t h b) -> p t h b", t=TT, h=HEADS), ACT.Sigmoid
                           ).then_inc(g_evac, 1)
            with act.Fori(0, 2) as i:
                for s in range(4):
                    full(i * 4 + s + 4 * R_Q)
                    act.activation(Q[:, bass.ds(i * 4 + s, 1), :], B[s % 2][:, :].unsqueeze(1), ACT.Identity,
                                   scale=HD ** -0.5).then_inc(evac[s % 2], 1)
            act.preload_act_table(ACT.Sigmoid)
            for t in range(8):
                full(4 * R_GMR + t)
                if t == 0:
                    act.wait_ge(lru_y, 8)
                if t >= 2:
                    act.wait_ge(lru_y, 8 + t - 1)
                act.activation(tmp[t % 2], B[t % 2][:, :], ACT.Sigmoid).then_inc(evac[t % 2], 1)
            with act.Fori(0, 2) as i:
                for s in range(4):
                    full(i * 4 + s + 4 * R_GMA)
                    act.activation(GA[:, bass.ds(i * 4 + s, 1), :], B[s % 2][:, :].unsqueeze(1), ACT.Sigmoid
                                   ).then_inc(evac[s % 2], 1)
            for kv, rnd in enumerate([R_W1K, R_W1V]):
                full(4 * rnd + 3)
                if kv:
                    act.wait_ge(kv2_full, 1)
                for ht in range(2):
                    act.activation(HK[:, ht, :], B[ht][:, 0:128], ACT.Gelu_apprx_tanh).then_inc(evac[ht], 1)
                act.wait_ge(kv2_full, kv + 1)
                if kv == 0:
                    act.activation(KCT, B[3][:, 0:128], ACT.Identity).then_inc(kv2_done, 1)
                else:
                    act.wait_ge(k2_done, 3)
                    for hh in range(4):
                        r = slice(32 * hh, 32 * hh + 32)
                        a = act.activation(VBD[r, :, hh * HD:(hh + 1) * HD],
                                           B[2][r, 0:256].rearrange("p (g d) -> p g d", g=4), ACT.Identity)
                    a.then_inc(kv2_done, 1)
            def exponents(t):
                act.wait_ge(cs_m, t + 1)
                act.activation(tmp[2 * (t % 2)], tmp[2 * (t % 2)], ACT.Exp).then_inc(cs_e, 1)

            exponents(0)
            for t in range(TT):
                if t + 1 < TT:
                    exponents(t + 1)
                act.wait_ge(ct_full, t + 1)
                act.activation(tmp[1], B[6][:, :], ACT.Identity).then_inc(ct_done, 1)

            def run_attention(n, widths):
                for s in range(len(widths) + 2):
                    e = s - 2
                    if e >= 0:
                        act.wait_ge(tr_full, n + e + 3)
                        act.wait_ge(pv_full, n + e + 1)
                        act.activation(tmp[6 + e % 2][:, 0:widths[e]], B[6 + e % 2][:, 0:widths[e]], ACT.Identity
                                       ).then_inc(pt_done, 1)
                    if s < len(widths):
                        w = widths[s]
                        act.wait_ge(sc_done, n + s + 3)
                        act.wait_ge(tr_full, n + s + 1)
                        act.activation(tmp[4 + s % 2][:, 0:w], tmp[s % 2][:, 0:w], ACT.Exp, scale=-1.0,
                                       bias=sml[:, s:s + 1], accum_out=den[:, s:s + 1]).then_inc(exp_done, 1)

            act.preload_act_table(ACT.Exp)
            act.wait_ge(co_done, TT)
            for j in range(2):
                with act.Fori(0, 2) as i:
                    act.wait_ge(p_scaled, 32 * i + 64 * j + 1)
                    for u in range(2):
                        r = 2 * i + u
                        act.activation(QT[u], Q[:, bass.ds(r + 4 * j, 1), :].rearrange("p o n -> p (o n)"), ACT.Identity)
                        act.activation(slope[:, u, :], c("slopes").rearrange("p (a r) -> p a r", r=4)[
                            :, 2 * j:2 * j + 2, bass.ds(r, 1)].rearrange("p a o -> p (a o)"), ACT.Identity)
                        for b in range(2):
                            a = act.activation(gts[:, u, b], GT[:, 1 + b].rearrange("p (a r) t -> p a r t", r=4)[
                                :, 2 * j:2 * j + 2, bass.ds(r, 1), :].rearrange("p a o t -> p a (o t)"), ACT.Identity)
                    a.then_inc(q_cur, 1)
                    run_attention(32 * i + 64 * j, [P * (t + 1) for _ in range(8) for t in range(TT)])

            def out_tile(ch, k, nsq):
                full(ch)
                act.wait_ge(sq_used, nsq + 1)
                act.activation(SQ[nsq % 2], B[k % 2][:, :], ACT.Square).then_inc(sq_full, 1)
                act.activation(H[:, k, :], B[k % 2][:, :], ACT.Identity).then_inc(evac[k % 2], 1)

            act.preload_act_table_set(LN_EXP)
            for k in range(KT):
                out_tile(4 * R_WOUT + k, k, 8 + k)
            rstds(1)
            for k in range(KT):
                act.wait_ge(x_done, k + 1)
                square(16 + k, X[:, k, :])
            act.wait_ge(h_done, 8)
            rstds(2)
            act.preload_act_table(ACT.Silu)
            with act.Fori(0, FT // 2) as i:
                for u in range(2):
                    m = 2 * i + u + M_FFN
                    full(4 * R_FFN + 4 * i + 2 * u)
                    act.wait_ge(evac[1], m)
                    act.activation(SG[u], B[0][:, :], ACT.Silu).then_inc(evac[0], 1)
            act.preload_act_table_set(LN_EXP)
            for k in range(KT):
                out_tile(4 * R_DOWN + 3 * k + 2, k, 24 + k)
                if k == 2:
                    act.wait_ge(rope_arg, 1)
                    act.activation(SIN, SIN, ACT.Sin)
                    act.activation(COS, COS, ACT.Sin).then_inc(rope_done, 1)
                    act.wait_ge(gam_e, 1)
                    act.activation(LBS[:, 1], LBS[:, 0], ACT.Exp).then_inc(gam_e, 1)
                    act.preload_act_table_set(LN_EXP)
            rstds(3)
            act.preload_act_table(ACT.Sigmoid)
            for k in range(KT):
                full(4 * R_PLEG + k)
                if k == 0:
                    act.wait_ge(x_done, 2 * KT)
                act.activation(H[:, k, :], B[k % 2][:, :], ACT.Sigmoid, bias=p1("ple_b", k, k + 1)
                               ).then_inc(evac[k % 2], 1)

            with act.Fori(0, LAYERS) as l:
                R0 = 4 * ROUNDS1 + 4 * ROUNDS2 * l
                M0 = PAIRS1 + PAIRS2 * l
                act.preload_act_table_set(LN_EXP)
                act.wait_ge(lb_done, 1)
                act.wait_ge(x_done, 24)
                act.wait_ge(layer_end, l + 1)
                act.activation(PCUR, PALL[:, bass.ds(l, 1), :].rearrange("p o n -> p (o n)"), ACT.Identity)
                act.activation(LBC, LBS[:, 4:6, bass.ds(l, 1), :].rearrange("p f o n -> p f (o n)"), ACT.Identity
                               ).then_inc(cur_done, 1)

                def sq2(job, q, src, parts=P, cols=S):
                    j, sq0, n = JOBS[job]
                    act.wait_ge(sq_used, 32 + NSQ2 * l + sq0 + q + 1)
                    act.activation(HS[(sq0 + q) % 2][0:parts, 0:cols], src, ACT.Square).then_inc(sq_full, 1)

                def rstd2(job, dim, parts=P, cols=S):
                    j, sq0, n = JOBS[job]
                    act.wait_ge(sq_used, 2 + 32 + NSQ2 * l + sq0 + n)
                    if j:
                        act.wait_ge(ap_done, NJOBS * l + j)
                    r = rstd[0:parts, 0:cols]
                    act.activation(r, B[7][0:parts, 0:cols], ACT.Ln, bias=c("eps")[0:parts], scale=1.0 / dim)
                    act.drain()
                    act.activation(r, r, ACT.Exp, scale=-0.5).then_inc(rstd_done, 1)

                def out2(rnd, s, dst, func=ACT.Identity, n=None):
                    full(R0 + 4 * rnd + s)
                    b = B[s % 2][:, :] if n is None else B[s % 2][:, 0:n]
                    act.activation(dst, b, func).then_inc(evac[s % 2], 1)

                for k in range(KT):
                    act.wait_ge(evac[k % 2], M0 + k // 2 - 4 + 2)
                    if k == 0:
                        act.wait_ge(layer_end, l + 1)
                    sq2("mix", k, X[:, k, :])
                rstd2("mix", D)
                for s in range(2):
                    out2(L_A, s, AH[:, s, 15:15 + S])
                for s in range(2, 4):
                    out2(L_A, s, tm2[s - 2], ACT.Sigmoid)
                for s in range(4):
                    full(R0 + 4 * L_Z + s)
                    act.activation(PS[:, s // 2, (s % 2) * S:(s % 2 + 1) * S], B[s % 2][:, :], ACT.Sigmoid)
                    act.activation(KF[:, s // 2, s % 2, :], B[s % 2][:, :], ACT.Sigmoid, scale=-1.0
                                   ).then_inc(evac[s % 2], 1)
                for s in range(2):
                    out2(L_QG, s, QH[:, s, :])
                for s in range(2, 4):
                    out2(L_QG, s, GG[:, s - 2, :], ACT.Silu)
                full(R0 + 4 * L_VCQ + 1)
                for b in range(2):
                    i = act.activation(VH[:, 2 * b:2 * b + 2, :].rearrange("p t n -> p (t n)"), B[2 + b][:, :], ACT.Identity)
                i.then_inc(vh_evac, 1)
                for s in range(2, 4):
                    out2(L_VCQ, s, CQ[:, s - 2, :])
                out2(L_KVX, 0, CKV)
                out2(L_KVX, 1, KR)
                for s in range(2, 4):
                    out2(L_KVX, s, GCX[:, s - 2, 1:1 + S])
                for s in range(2, 4):
                    out2(L_C, s, GB[:, s - 2, :])
                act.preload_act_table_set(LN_EXP)
                for n in range(12):
                    act.wait_ge(hg_ps, 44 * l + 33 + n)
                    if n < 4:
                        dst = AO7[:, n, :, :].rearrange("p i t -> p (i t)")
                        b = 4 + n
                    else:
                        ht, half, ii = (n - 4) // 4, (n - 4) % 4 // 2, n % 2
                        dst = AO8[:, 2 * ht + half, 2 * ii:2 * ii + 2, :].rearrange("p i t -> p (i t)")
                        b = 4 + 2 * ii + half
                    act.activation(dst, B[b][:, :], ACT.Identity).then_inc(hg_ev, 1)
                for ht in range(2):
                    act.wait_ge(o_full, 2 * l + ht + 1)
                    act.activation(CAT[:, 2 + ht, :], B[2 + ht][:, :], ACT.Identity).then_inc(oc_done, 1)
                    sq2(f"o{ht}", 0, B[2 + ht][:, :])
                    rstd2(f"o{ht}", HD)
                act.wait_ge(cen_done, l + 1)
                for q in range(2):
                    sq2("ln", q, CAT[:, q, :])
                rstd2("ln", 256)
                for q in range(2):
                    act.wait_ge(silu_in, 2 * l + q + 1)
                    act.activation(CAT[:, q, :], CAT[:, q, :], ACT.Silu, bias=p2("a_ln_b", q, q + 1)).then_inc(cat_done, 1)
                act.preload_act_table_set(LN_EXP)
                act.wait_ge(cat_done, 6 * l + 6)
                norms = [("bA", [CAT[:, 0, :], CAT[:, 1, :]]), ("bB", [CAT[:, 2, :], CAT[:, 3, :]]),
                         ("bC", [CAT[:, 4, :], CAT[:, 5, :]]), ("qa", [CQ[:, 0, :], CQ[:, 1, :]]), ("kva", [CKV])]
                for at in range(len(norms) + 1):
                    if at < len(norms):
                        for q, src in enumerate(norms[at][1]):
                            sq2(norms[at][0], q, src)
                    if at:
                        rstd2(norms[at - 1][0], P * len(norms[at - 1][1]))

                def heads(i):
                    dst = (QM if i < 4 else KM)
                    if i < 4:
                        if i == 3:
                            full(R0 + 4 * L_UP)
                        else:
                            act.wait_ge(part_full, 6 + 14 * l + i + 1)
                        act.activation(dst[0:96, i, :], B[i % 2][0:96, :], ACT.Identity).then_inc(evac[i % 2], 1)
                    else:
                        act.wait_ge(part_full, 6 + 14 * l + i)
                        act.activation(dst[64:96, i % 4, :], KR[64:96, :], ACT.Identity)
                        act.activation(dst[0:64, i % 4, :], B[i % 2][0:64, :], ACT.Identity).then_inc(evac[i % 2], 1)
                    act.drain()
                    sq2(f"hd{i}", 0, dst[0:96, i % 4, :], 96)

                for i in range(9):
                    if i < 8:
                        heads(i)
                    if i:
                        rstd2(f"hd{i - 1}", 96, 96)
                for b in range(2):
                    if b == 0:
                        act.wait_ge(part_full, 6 + 14 * l + 8)
                    else:
                        full(R0 + 4 * L_UP + 3)
                    act.activation(VM[:, 2 * b:2 * b + 2, :].rearrange("p t n -> p (t n)"), B[b][:, :], ACT.Identity
                                   ).then_inc(evac[b], 1)
                n = 128 + 32 * l
                run_attention(n, [S] * 16)
                act.wait_ge(o_done, 4 * l + 12)
                for q in range(2):
                    sq2("bD", q, CAT[:, 6 + q, :])
                rstd2("bD", 256)
                act.wait_ge(mem_in, 16)
                for q in range(KT):
                    sq2("mem", q, MEM[:, q, :], cols=NM)
                rstd2("mem", D, cols=NM)
                for f in range(2):
                    full(R0 + 4 * L_XKV + f)
                    act.activation(XK[:, f, :], B[f][:, 0:NM], ACT.Identity)
                    act.wait_ge(sq_used, 32 + NSQ2 * l + JOBS[f"xk{f}"][1] + 1)
                    act.activation(HS[JOBS[f"xk{f}"][1] % 2][:, 0:NM], B[f][:, 0:NM], ACT.Square).then_inc(sq_full, 1)
                    act.drain()
                    act.sem_inc(evac[f], 1)
                full(R0 + 4 * L_XKV + 3)
                for t in range(2):
                    i = act.activation(XV[:, t, :], B[2 + t][:, 0:256], ACT.Identity)
                i.then_inc(xv_done, 1)
                for f in range(2):
                    rstd2(f"xk{f}", HD, cols=NM)
                for k in range(KT):
                    act.wait_ge(evac[k % 2], M0 + N_WOUT + k // 2 + 2)
                    sq2("xq", k, X[:, k, :])
                rstd2("xq", D)
                for f in range(2):
                    full(R0 + 4 * L_XQO + f)
                    act.activation(XQ[:, f, :], B[f][:, :], ACT.Identity)
                    act.wait_ge(sq_used, 32 + NSQ2 * l + JOBS[f"xh{f}"][1] + 1)
                    act.activation(HS[JOBS[f"xh{f}"][1] % 2], B[f][:, :], ACT.Square).then_inc(sq_full, 1)
                    act.drain()
                    act.sem_inc(evac[f], 1)
                for f in range(2):
                    rstd2(f"xh{f}", HD)
                run_attention(n + 16, [256] * 16)
                for k in range(KT):
                    act.wait_ge(evac[k % 2], M0 + N_XO + k // 2 + 2)
                    sq2("ffn", k, X[:, k, :])
                rstd2("ffn", D)
                act.preload_act_table(ACT.Silu)
                with act.Fori(0, FT // 2) as i:
                    for u in range(2):
                        m = M0 + 2 * i + u + N_FFN
                        full(R0 + 4 * L_FFN + 4 * i + 2 * u)
                        act.wait_ge(evac[1], m)
                        act.activation(SG[u], B[0][:, :], ACT.Silu).then_inc(evac[0], 1)
                act.sem_inc(sq_full, 1)

        @block.vector
        def _(dve):
            dve.sem_inc(evac[1], 1)
            dve.sem_inc(sc_done, 2)
            dve.sem_inc(p_scaled, 1)
            dve.sem_inc(o_done, 2)
            dve.wait_ge(const_in, 32)
            dve.scalar_tensor_tensor(lru[:, 0, :], p1("lam"), -1.0, p1("lam"), ALU.mult, ALU.max).then_inc(coef_e, 1)
            dve.tensor_scalar(lru[:, 5, :], p1("ba"), 0.5, None, ALU.mult)
            dve.tensor_scalar(lru[:, 6, :], p1("bx"), 0.5, None, ALU.mult)
            def split(rnd, s, wh):
                dve.wait_ge(w_loaded[s], 16 * (rnd + 1))
                dve.wait_ge(chunk_done, 4 * rnd + s - 1 + SLOTS)
                dve.tensor_copy(wh[s % 2], W[:, s, :])
                dve.drain()
                dve.tensor_tensor(W_R[:, s, :], W[:, s, :], wh[s % 2].bitcast(F32), ALU.subtract).then_inc(split_done, 1)

            def split_norm(gain, full, hi, lo, done):
                for k in range(KT + 2):
                    if k < KT:
                        dve.scalar_tensor_tensor(full[:, k, :], X[:, k, :], gain(k), rstd, ALU.mult, ALU.mult)
                    if 1 <= k <= KT:
                        dve.tensor_copy(hi[:, k - 1, :], full[:, k - 1, :])
                    if k >= 2:
                        dve.tensor_tensor(lo[:, k - 2, :], full[:, k - 2, :], hi[:, k - 2, :].bitcast(F32), ALU.subtract
                                          ).then_inc(done, 1)
                    dve.drain()

            split(R_XR, 0, WHA)
            split(R_XR, 1, WHA)
            dve.wait_ge(rstd_done, 1)
            split_norm(lambda k: p1("mix_pre", k, k + 1), HFA, H_R, HLA, h_done)
            with dve.Fori(0, 4) as i:
                for s in range(2, 6):
                    split(R_XR + i + s // 4, s % 4, WHA)
            dve.wait_ge(coef_e, 2)
            e, z, w = lru[:, 1, :], lru[:, 2, :], lru[:, 7, :]
            dve.tensor_scalar(z, e, 2.0, None, ALU.add)
            dve.drain()
            dve.reciprocal(z, z)
            dve.drain()
            dve.tensor_tensor(z, z, e, ALU.mult)
            dve.drain()
            dve.tensor_tensor(e, z, z, ALU.mult)
            dve.memset(w, 1.0 / 17)
            for q in (15, 13, 11, 9, 7, 5, 3, 1):
                dve.drain()
                dve.tensor_tensor(w, w, e, ALU.mult)
                dve.drain()
                dve.tensor_scalar(w, w, 1.0 / q, None, ALU.add)
            dve.drain()
            dve.tensor_tensor(w, w, z, ALU.mult)
            dve.drain()
            dve.tensor_scalar(z, p1("lam"), -1.0, 0.0, ALU.mult, ALU.max)
            dve.drain()
            dve.scalar_tensor_tensor(w, w, 2.0, z, ALU.mult, ALU.add)
            dve.drain()
            dve.tensor_scalar(lru[:, 3, :], w, 4.0, None, ALU.mult)
            dve.tensor_scalar(lru[:, 4, :], w, -4.0, None, ALU.mult).then_inc(coef_done, 1)
            dve.wait_ge(pad_done, 1)

            def conv(t):
                dve.wait_ge(evac[t % 2], t // 2 + 2)
                if t >= 2:
                    dve.wait_ge(gate_full, t - 1)
                o = tmp[t % 2]
                cw = lambda i: p1("conv_w", i * KT + t, i * KT + t + 1)
                dve.drain()
                dve.tensor_scalar(o, XR[:, t, 0:S], cw(0), p1("conv_b", t, t + 1), ALU.mult, ALU.add)
                for i in range(1, 4):
                    dve.drain()
                    a = dve.scalar_tensor_tensor(o, XR[:, t, i:i + S], cw(i), o, ALU.mult, ALU.add)
                a.then_inc(conv_done, 1)

            def lru_mid(t):
                a = tmp[5 + t % 2]
                dve.wait_ge(lru_a, t + 1)
                dve.tensor_tensor(tmp[9], a, a, ALU.mult)
                dve.drain()
                dve.scalar_tensor_tensor(tmp[9], tmp[9], 1.0, tmp[4], ALU.add, ALU.mult)
                dve.scalar_tensor_tensor(tmp[7 + t % 2], tmp[3], 1.0, tmp[t % 2], ALU.add, ALU.mult
                                         ).then_inc(lru_t, 1)

            def lru_scan(t):
                i = tmp[7 + t % 2]
                dve.wait_ge(lru_sqrt, t + 1)
                dve.tensor_tensor(i, i, tmp[9], ALU.mult)
                dve.drain()
                dve.tensor_tensor_scan(tmp[10], tmp[5 + t % 2], i, 0.0, ALU.mult, ALU.add)
                dve.drain()
                if t == 0:
                    dve.wait_ge(evac[0], M_CMP_IN + 1)
                    dve.wait_ge(evac[1], M_CMP_IN + 1)
                dve.tensor_tensor(G[:, t, :], G[:, t, :], tmp[10], ALU.mult).then_inc(lru_y, 1)

            conv(0)
            for t in range(8):
                if t < 7:
                    conv(t + 1)
                split(R_CMP_IN + (t + 2) // 4, (t + 2) % 4, WHA)
                if t:
                    lru_scan(t - 1)
                lru_mid(t)
            split(R_V, 2, WHA)
            lru_scan(7)
            split(R_V, 3, WHA)
            split(R_Q, 0, WHB)
            split(R_Q, 1, WHB)
            for h in range(HEADS):
                if h == 0:
                    dve.wait_ge(shuffled, 16 * 8)
                dve.scalar_tensor_tensor(CB[:, :, h, :], c("cmp_dist").rearrange("p (t c) -> p t c", t=TT),
                                         c("slopes", h, h + 1), c("cmp_neg").rearrange("p (t c) -> p t c", t=TT),
                                         ALU.mult, ALU.add)
            dve.drain()
            with dve.Fori(0, 2) as i:
                for s in range(2, 6):
                    split(R_Q + i + s // 4, s % 4, WHB)
            for t in range(8):
                split(R_GMR + (t + 2) // 4, (t + 2) % 4, WHB)
                dve.wait_ge(evac[t % 2], M_GMR + t // 2 + 2)
                dve.tensor_tensor(G[:, t, :], G[:, t, :], tmp[t % 2], ALU.mult).then_inc(lru_y, 1)
            for n in range(2, 8):
                split(R_GMA + n // 4, n % 4, WHB)
            mx = sml[:, 32:48]
            dn = sml[:, 48:64]

            def weigh(t):
                full = tmp[2 * (t % 2)]
                sc = full.rearrange("p (h c) -> p h c", h=HEADS)
                dve.drain()
                dve.wait_ge(cs_full, t + 1)
                if t >= 2:
                    dve.wait_ge(ct_full, t - 1)
                for half in range(2):
                    by_half = lambda ap: ap.rearrange("p (j f r c) -> p j f (r c)", j=2, f=2, r=4)[:, :, half, :]
                    dve.tensor_tensor(by_half(full), B[4 + half][:, 0:256].rearrange("p (j n) -> p j n", j=2),
                                      by_half(CB[:, t, :, :].rearrange("p h c -> p (h c)")), ALU.add)
                dve.drain()
                dve.tensor_reduce(mx, sc, AX.X, ALU.max)
                dve.drain()
                dve.tensor_scalar(mx, mx, -1e20, None, ALU.max)
                dve.drain()
                dve.tensor_tensor(sc, sc, mx.unsqueeze(2).to_broadcast([P, HEADS, CC]), ALU.subtract).then_inc(cs_m, 1)

            weigh(0)
            for t in range(TT):
                if t + 1 < TT:
                    weigh(t + 1)
                sc = tmp[2 * (t % 2)].rearrange("p (h c) -> p h c", h=HEADS)
                dve.wait_ge(cs_e, t + 1)
                dve.tensor_reduce(dn, sc, AX.X, ALU.add)
                dve.drain()
                dve.tensor_scalar(dn, dn, 1e-30, None, ALU.max)
                dve.drain()
                dve.reciprocal(dn, dn)
                dve.drain()
                if t == 0:
                    dve.wait_ge(g_evac, 1)
                dve.tensor_tensor(dn, dn, GT[:, 0, :, t], ALU.mult)
                dve.drain()
                dve.tensor_tensor(sc, sc, dn.unsqueeze(2).to_broadcast([P, HEADS, CC]), ALU.mult).then_inc(cs_p, 1)
                dve.wait_ge(co_full, t + 1)
                dve.drain()
                for j in range(2):
                    i = dve.tensor_copy(YC[:, 4 * j:4 * j + 4, t * P:(t + 1) * P],
                                        B[2 + j][:, :].rearrange("p (r n) -> p r n", r=4))
                i.then_inc(co_done, 1)

            def run_attention(n, per, steps, finish, gates=None, ready=None):
                rc = sml[:, 64:66]
                for s in range(len(steps) + 4):
                    if s < len(steps):
                        w, in1, scale = steps[s]
                        waits(dve, *([] if ready is None else ready(s)), (qk_full, n + s + 1), (exp_done, n + s + 1))
                        dve.tensor_tensor_reduce(tmp[s % 2][:, 0:w], B[4 + s % 2][:, 0:w], in1, -scale, 3e38,
                                                 ALU.add, ALU.min, sml[:, s:s + 1]).then_inc(sc_done, 1)
                    e = s - 1
                    if 0 <= e < len(steps):
                        w = steps[e][0]
                        dve.wait_ge(exp_done, n + e + 3)
                        r = rc[:, e % 2:e % 2 + 1]
                        dve.reciprocal(r, den[:, e:e + 1])
                        dve.drain()
                        p = tmp[4 + e % 2][:, 0:w]
                        if gates is None:
                            dve.tensor_scalar(p, p, r, None, ALU.mult).then_inc(p_scaled, 1)
                        else:
                            dve.tensor_scalar(p, p, r, gates[:, e:e + 1], ALU.mult, ALU.mult).then_inc(p_scaled, 1)
                    g = s - 4
                    if g >= 0 and g % per == per - 1:
                        finish(g // per)

            for j in range(2):
                with dve.Fori(0, 2) as i:
                    n = 32 * i + 64 * j

                    def result(u):
                        t = 2 * i + 4 * j + u
                        dve.wait_ge(pv_full, n + 16 * u + 16 + 2)
                        dve.wait_ge(o_added, t + 1)
                        dve.tensor_tensor(YT[u].unsqueeze(1), B[2 + u][:, :].unsqueeze(1), YC[:, bass.ds(t, 1), :],
                                          ALU.add).then_inc(o_done, 1)

                    def distances(s):
                        return [(sd_done, 2 * i + 4 * j + s // 16 + 1)] if s % 16 == 0 else []

                    steps = [(P * (t + 1), SD[u][half][:, 384 - P * t:512], 1.0)
                             for u in range(2) for _ in range(2) for half in range(2) for t in range(TT)]
                    run_attention(n, 16, steps, result, gsteps, distances)

            def post_norm(n, gain):
                dve.wait_ge(rstd_done, n)
                for k in range(KT):
                    dve.scalar_tensor_tensor(H[:, k, :], H[:, k, :], p1(gain, k, k + 1), rstd, ALU.mult, ALU.mult)
                    dve.drain()
                    dve.tensor_tensor(X[:, k, :], X[:, k, :], H[:, k, :], ALU.add).then_inc(x_done, 1)

            def feed_forward(rnd, pair, wh, sg, hi, lo):
                with dve.Fori(0, FT // 2) as i:
                    for u in range(2):
                        split(rnd + i + u, 2 - 2 * u, wh)
                        split(rnd + i + u, 3 - 2 * u, wh)
                        dve.wait_ge(evac[0], pair + 2 * i + u + 2)
                        dve.tensor_tensor(rstd, B[1][:, :], sg[u], ALU.mult).then_inc(evac[1], 1)
                        dve.drain()
                        at = bass.ds(2 * i + u, 1)
                        dve.tensor_copy(hi[:, at, :], rstd.unsqueeze(1))
                        dve.drain()
                        dve.tensor_tensor(lo[:, at, :], rstd.unsqueeze(1), hi[:, at, :].bitcast(F32), ALU.subtract
                                          ).then_inc(ac_done, 1)

            post_norm(2, "mix_post")
            split(R_FFN, 0, WH)
            split(R_FFN, 1, WH)
            dve.wait_ge(rstd_done, 3)
            split_norm(lambda k: p1("ffn_pre", k, k + 1), HF, H_R, HL, h_done)
            feed_forward(R_FFN, M_FFN, WH, SG, ACH, ACL)

            def second_block_tables():
                TWO_PI = 6.283185307179586
                c1 = 6.28125
                c2 = float(np.float32(np.round((TWO_PI - c1) * 2.0 ** 21) / 2.0 ** 21))
                c3 = TWO_PI - c1 - c2
                dve.drain()
                dve.wait_ge(pos_in, 16)
                ang, tn = area(2048, S), area(2560, S)
                dve.tensor_copy(ang, SIN.bitcast(I32))
                dve.drain()
                dve.tensor_scalar(ang, ang, c("inv_freq"), None, ALU.mult)
                dve.drain()
                dve.tensor_scalar(tn, ang, 1.0 / TWO_PI, 12582912.0, ALU.mult, ALU.add)
                dve.drain()
                dve.tensor_scalar(tn, tn, -12582912.0, None, ALU.add)
                for part in (c1, c2, c3):
                    dve.drain()
                    dve.scalar_tensor_tensor(ang, tn, -part, ang, ALU.mult, ALU.add)
                dve.drain()
                dve.tensor_scalar(SIN, ang, 3.1415925, -3.1415925, ALU.min, ALU.max)
                dve.scalar_tensor_tensor(tn, ang, -1.0, ang, ALU.mult, ALU.max)
                dve.drain()
                dve.tensor_scalar(COS, tn, -1.0, 1.5707963267948966, ALU.mult, ALU.add).then_inc(rope_arg, 1)
                dve.wait_ge(par2_in, 32)
                mxg = LBS[:, 3, 0, :]
                dve.tensor_tensor(mxg, GAM[:, 0, :], GAM[:, 1, :], ALU.max)
                dve.drain()
                dve.tensor_tensor(LBS[:, 0], GAM, mxg.unsqueeze(1).to_broadcast([P, 2, 4]), ALU.subtract).then_inc(gam_e, 1)
                dve.wait_ge(rope_done, 1)
                dve.wait_ge(gam_e, 2)
                dve.tensor_tensor(mxg, LBS[:, 1, 0, :], LBS[:, 1, 1, :], ALU.add)
                dve.drain()
                dve.reciprocal(mxg, mxg)
                dve.drain()
                dve.tensor_tensor(LBS[:, 2], LBS[:, 1], mxg.unsqueeze(1).to_broadcast([P, 2, 4]), ALU.mult)
                dve.drain()
                dve.tensor_tensor(LBS[:, 4, 0, :], LBS[:, 2, 0, :], LBS[:, 2, 0, :], ALU.subtract)
                dve.tensor_tensor(LBS[:, 4, 1, :], LBS[:, 2, 0, :], LBS[:, 2, 1, :], ALU.add)
                dve.drain()
                dve.tensor_tensor(LBS[:, 4, 1, :], LBS[:, 4, 1, :], LBS[:, 2, 0, :], ALU.subtract)
                dve.drain()
                dve.tensor_scalar(LBS[:, 5], LBS[:, 4], -1.0, 1.0, ALU.mult, ALU.add).then_inc(lb_done, 1)

            for n in range(2, 24):
                split(R_DOWN + n // 4, n % 4, WH)
                if n == 10:
                    second_block_tables()
            post_norm(4, "ffn_post")
            for k in range(KT):
                if k % 4 == 3:
                    dve.wait_ge(chunk_done, 4 * R_PLEP + k // 4 + 1 + SLOTS)
                else:
                    dve.wait_ge(part_full, k - k // 4 + 1)
                if k == 0:
                    dve.wait_ge(evac[0], M_PLEP + 1)
                    dve.wait_ge(evac[1], M_PLEP + 1)
                dve.tensor_tensor(tmp[k % 2], B[k % 2][:, :], H[:, k, :], ALU.mult).then_inc(evac[k % 2], 1)
                dve.drain()
                dve.tensor_tensor(X[:, k, :], X[:, k, :], tmp[k % 2], ALU.add).then_inc(x_done, 1)

            dve.drain().then_inc(layer_end, 1)

            with dve.Fori(0, LAYERS) as l:
                RN = ROUNDS1 + ROUNDS2 * l
                R0 = 4 * ROUNDS1 + 4 * ROUNDS2 * l + SLOTS
                M0 = PAIRS1 + PAIRS2 * l

                def apply(job, pairs, gain, parts=P, cols=S, done=None):
                    waits(dve, (rstd_done, 4 + NJOBS * l + JOBS[job][0] + 1))
                    for k, (o, i) in enumerate(pairs):
                        x = dve.scalar_tensor_tensor(o, i, p2(gain, k, k + 1)[0:parts], rstd[0:parts, 0:cols],
                                                     ALU.mult, ALU.mult)
                        if done is not None:
                            x.then_inc(done, 1)
                    dve.drain().then_inc(ap_done, 1)

                split(RN + L_A, 0, WHY)
                split(RN + L_A, 1, WHY)
                waits(dve, (cur_done, l + 1), (rstd_done, 4 + NJOBS * l + JOBS["mix"][0] + 1))
                split_norm(lambda k: p2("g_mix", k, k + 1), H, HHY, HLY, h2_done)
                dve.drain().then_inc(ap_done, 1)
                for s in range(2, 6):
                    split(RN + L_A + s // 4, s % 4, WHY)
                for s in range(2):
                    dve.wait_ge(evac[s], M0 + N_A + 3)
                    dve.wait_ge(edge_done, l + 1)
                    i = dve.tensor_tensor(AH[:, s, 15:15 + S], AH[:, s, 15:15 + S], tm2[s], ALU.mult)
                i.then_inc(ah_done, 1)
                for s in range(2, 6):
                    split(RN + L_Z + s // 4, s % 4, WHY)
                dve.wait_ge(evac[0], M0 + N_Z + 3)
                dve.wait_ge(evac[1], M0 + N_Z + 3)
                for d in range(2):
                    for t in range(2):
                        pre = PS[:, d, t * S:(t + 1) * S]
                        dve.scalar_tensor_tensor(pre, KF[:, d, t, :], LBC[:, 0, 2 * d + t:2 * d + t + 1], pre,
                                                 ALU.mult, ALU.add)
                dve.drain()
                for d in range(2):
                    for t in range(2):
                        dve.tensor_scalar(KF[:, d, t, :], KF[:, d, t, :], LBC[:, 1, 2 * d + t:2 * d + t + 1], None, ALU.mult)
                dve.drain()
                for s in range(2, 4):
                    split(RN + L_QG, s, WHY)
                flat = lambda ap: ap.rearrange("p a n -> p (a n)")
                dve.tensor_tensor(KC[0], flat(KF[:, 0]), flat(KF[:, 1]), ALU.add)
                waits(dve, (evac[0], M0 + N_QG + 2), (evac[1], M0 + N_QG + 2))
                dve.drain().then_inc(hg_qk, 1)

                def sides(ap, m):
                    return ap.rearrange("p (n s m) -> p s n m", s=2, m=m)

                def hg_mul(lev):
                    m = 1 << lev
                    st = lev + 1
                    q, k = sides(QC[st % 2], m), sides(KC[st % 2], m)
                    if lev:
                        dve.wait_ge(hg_up, 9 * l + lev + 1)
                    else:
                        dve.wait_ge(hg_up, 9 * l + 1)
                    if st >= 2:
                        dve.wait_ge(hg_ps, 44 * l + 4 * (st - 1))
                    ql = sides(flat(QH), m)
                    kf, kb = sides(flat(KF[:, 0]), m), sides(flat(KF[:, 1]), m)
                    pf, pb, sf, sb_ = (sides(PS[:, i, :], m) for i in range(4))
                    dve.tensor_tensor(q[:, 1], ql[:, 1], pf[:, 1], ALU.mult)
                    dve.tensor_tensor(q[:, 0], ql[:, 0], pb[:, 0], ALU.mult)
                    dve.tensor_tensor(k[:, 0], kf[:, 0], sf[:, 0], ALU.mult)
                    dve.tensor_tensor(k[:, 1], kb[:, 1], sb_[:, 1], ALU.mult)
                    dve.drain().then_inc(hg_qk, 1)

                def hg_merge(st):
                    for bk in range(4):
                        waits(dve, (hg_ps, 44 * l + 4 * st + bk + 1))
                        dst = AD[:, bk % 2, 2 * (bk // 2):2 * (bk // 2) + 2, :].rearrange("p i n -> p (i n)")
                        if st == 0:
                            dve.tensor_copy(dst, B[4 + bk][:, :]).then_inc(hg_mg, 1)
                        else:
                            lv = c("levels", (st - 1) * P, st * P).bitcast(I32).unsqueeze(1).to_broadcast([P, 4, P])
                            dve.copy_predicated(dst.rearrange("p (a t) -> p a t", a=4), lv,
                                                B[4 + bk][:, :].rearrange("p (a t) -> p a t", a=4)).then_inc(hg_mg, 1)

                taps = [(t, k) for k in range(31) for t in range(2)]

                def conv_taps(a, b):
                    for t, k in taps[a:b]:
                        w = p2("a_dw_w", 2 * k + t, 2 * k + t + 1)
                        if t == 0:
                            dve.drain()
                        if k == 0:
                            i = dve.tensor_scalar(CAT[:, t, :], AH[:, t, 0:S], w, p2("a_dw_b", t, t + 1), ALU.mult, ALU.add)
                        else:
                            i = dve.scalar_tensor_tensor(CAT[:, t, :], AH[:, t, k:k + S], w, CAT[:, t, :], ALU.mult, ALU.add)
                    if b >= 62:
                        i.then_inc(ah_done, 1)

                for st in range(1, 10):
                    hg_mul(st - 1)
                    if st <= 8:
                        dve.drain()
                        hg_merge(st - 1)
                    conv_taps(7 * (st - 1), 7 * st if st < 9 else 62)
                for t in range(2):
                    dve.wait_ge(chunk_done, R0 + 4 * L_C + t + 1)
                    dve.wait_ge(evac[t], M0 + N_KVX + 3)
                    dve.tensor_tensor(GCX[:, t, 1:1 + S], GCX[:, t, 1:1 + S], B[t][:, :], ALU.mult).then_inc(evac[t], 1)
                dve.drain()
                for t in range(2):
                    o = CAT[:, 4 + t, :]
                    w = lambda k: p2("c_dw_w", 2 * k + t, 2 * k + t + 1)
                    dve.tensor_scalar(o, GCX[:, t, 0:S], w(0), p2("c_dw_b", t, t + 1), ALU.mult, ALU.add)
                    for k in (1, 2):
                        dve.drain()
                        dve.scalar_tensor_tensor(o, GCX[:, t, k:k + S], w(k), o, ALU.mult, ALU.add)
                    dve.drain()
                    dve.wait_ge(evac[t], M0 + N_C + 3)
                    dve.tensor_tensor(o, o, GB[:, t, :], ALU.mult).then_inc(cat_done, 1)
                for ht in range(2):
                    o = CAT[:, 2 + ht, :]
                    dve.wait_ge(oc_done, 2 * l + ht + 1)
                    dve.wait_ge(rstd_done, 4 + NJOBS * l + JOBS[f"o{ht}"][0] + 1)
                    dve.scalar_tensor_tensor(o, o, p2("h_onorm", ht, ht + 1), rstd, ALU.mult, ALU.mult
                                             ).then_inc(ap_done, 1)
                    dve.drain()
                    dve.tensor_tensor(o, o, GG[:, ht, :], ALU.mult).then_inc(cat_done, 1)
                dve.wait_ge(mean_full, l + 1)
                for t in range(2):
                    i = dve.scalar_tensor_tensor(CAT[:, t, :], B[6][:, :], -1.0 / 256, CAT[:, t, :], ALU.mult, ALU.add)
                i.then_inc(cen_done, 1)
                dve.drain()
                apply("ln", [(CAT[:, q, :], CAT[:, q, :]) for q in range(2)], "a_ln_g", done=silu_in)

                def split_mixed(tiles):
                    for k in tiles:
                        dve.tensor_copy(CATH[:, k, :], CATF[:, k, :])
                    dve.drain()
                    for k in tiles:
                        dve.tensor_tensor(CATL[:, k, :], CATF[:, k, :], CATH[:, k, :].bitcast(F32), ALU.subtract)

                for g, job in enumerate(("bA", "bB", "bC")):
                    waits(dve, (rstd_done, 4 + NJOBS * l + JOBS[job][0] + 1))
                    for q in range(2):
                        k = 2 * g + q
                        dve.scalar_tensor_tensor(CATF[:, k, :], CAT[:, k, :], p2("g_branch", k, k + 1), rstd,
                                                 ALU.mult, ALU.mult)
                    dve.drain().then_inc(ap_done, 1)
                    split_mixed((2 * g, 2 * g + 1))
                apply("qa", [(CQ[:, q, :], CQ[:, q, :]) for q in range(2)], "qa")
                apply("kva", [(CKV, CKV)], "kva")
                for i in range(8):
                    t = (QM if i < 4 else KM)[0:96, i % 4, :]
                    gain = p2("qn" if i < 4 else "kn")[0:96]
                    dve.wait_ge(rstd_done, 4 + NJOBS * l + JOBS[f"hd{i}"][0] + 1)
                    dve.scalar_tensor_tensor(t, t, gain, rstd[0:96, :], ALU.mult, ALU.mult).then_inc(ap_done, 1)
                    dve.drain().then_inc(qk_ready, 1)
                    dve.wait_ge(rot_full, 8 * l + i + 1)
                    dve.tensor_tensor(t, t, COS[0:96, :], ALU.mult)
                    dve.tensor_tensor(RB[0:96, :], B[4 + i % 2][0:96, :], SIN[0:96, :], ALU.mult)
                    dve.drain()
                    dve.tensor_tensor(t, t, RB[0:96, :], ALU.add)
                    dve.drain().then_inc(qk_ready, 1)

                def finish2(n, dst):
                    def f(g):
                        dve.wait_ge(pv_full, n + 8 * g + 8 + 2)
                        dve.tensor_copy(dst(g), B[2 + g][:, :]).then_inc(o_done, 1)
                    return f

                n = 128 + 32 * l
                run_attention(n, 8, [(S, c("zeros"), 96 ** -0.5)] * 16, finish2(n, lambda g: CAT[:, 6 + g, :]))
                waits(dve, (rstd_done, 4 + NJOBS * l + JOBS["bD"][0] + 1))
                for k in (6, 7):
                    dve.scalar_tensor_tensor(CATF[:, k, :], CAT[:, k, :], p2("g_branch", k, k + 1), rstd,
                                             ALU.mult, ALU.mult)
                dve.drain()
                split_mixed((6, 7))
                dve.drain().then_inc(ap_done, 1)
                apply("mem", [(MN[:, k, :], MEM[:, k, :]) for k in range(KT)], "g_mem", cols=NM, done=mn_done)
                split(RN + L_WOUT, 0, WHZ)
                split(RN + L_WOUT, 1, WHZ)
                for f in range(2):
                    apply(f"xk{f}", [(XK[:, f, :], XK[:, f, :])], "x_kn", cols=NM)

                def add_x(k, ready):
                    ready(k)
                    dve.tensor_tensor(X[:, k, :], X[:, k, :], B[k % 2][:, :], ALU.add).then_inc(evac[k % 2], 1)

                for k in range(KT):
                    if k + 2 < KT:
                        split(RN + L_WOUT + (k + 2) // 4, (k + 2) % 4, WHZ)
                    add_x(k, lambda k: dve.wait_ge(chunk_done, R0 + 4 * L_WOUT + k + 1))
                dve.drain()
                apply("xq", [(H[:, k, :], X[:, k, :]) for k in range(KT)], "g_xq", done=h2_done)
                for f in range(2):
                    apply(f"xh{f}", [(XQ[:, f, :], XQ[:, f, :])], "x_qn")
                run_attention(n + 16, 8, [(256, c("zeros")[:, 0:256], HD ** -0.5)] * 16,
                              finish2(n + 16, lambda g: OXT[:, g, :]))

                def xo_ready(k):
                    if k % 4 == 3:
                        dve.wait_ge(chunk_done, R0 + 4 * L_XQO + 2 + k // 4 + 1)
                    else:
                        dve.wait_ge(part_full, 6 + 14 * l + 8 + k - k // 4 + 1)

                for k in range(KT):
                    add_x(k, xo_ready)
                dve.drain()
                split(RN + L_FFN, 0, WH)
                split(RN + L_FFN, 1, WH)
                waits(dve, (rstd_done, 4 + NJOBS * l + JOBS["ffn"][0] + 1))
                split_norm(lambda k: p2("g_ffn", k, k + 1), HF, H_R, HL, h2_done)
                dve.drain().then_inc(ap_done, 1)
                feed_forward(RN + L_FFN, M0 + N_FFN, WH, SG, ACH, ACL)
                for n in range(2, 24):
                    split(RN + L_DOWN + n // 4, n % 4, WH)
                    if n % 3 == 1:
                        add_x(n // 3 - 1, lambda k: None)
                add_x(7, lambda k: dve.wait_ge(chunk_done, R0 + 4 * L_DOWN + 3 * k + 3))
                dve.drain().then_inc(layer_end, 1)

        @block.gpsimd
        def _(pool):
            pool.sem_inc(sq_used, 2)
            pool.sem_inc(tr_full, 2)
            pool.sem_inc(pv_full, 2)
            pool.sem_inc(o_added, 2)
            pool.memset(XR[:, :, 0:3], 0.0).then_inc(pad_done, 1)
            pool.memset(K2, 0.0)
            pool.memset(VBD, 0.0)
            pool.drain()
            pool.wait_ge(evac[0], M_CMP_IN + 3)
            pool.wait_ge(evac[1], M_CMP_IN + 3)
            for kv in range(2):
                for gg in range(2):
                    for par in range(2):
                        pool.dma_start(KCD[64 * par:64 * par + 64, kv].rearrange("p (j g) m -> p j g m", g=2)[:, :, gg, :],
                                       KST[64 * gg:64 * gg + 64, 2 * kv:2 * kv + 2, par, :]).then_inc(shuffled, 16)
            pool.wait_ge(shuffled, 16 * 8)
            for kv in range(2):
                if kv:
                    pool.wait_ge(chunk_done, 4 * R_W1K + 4 + SLOTS)
                pos = p1("pos_k" if kv == 0 else "pos_v")
                for a in range(2):
                    i = pool.tensor_tensor(
                        K2[:, 8 * a:8 * a + 8, :, 0:31],
                        KCD[:, kv].rearrange("p g (c b) -> p b g c", b=8)[:, :, :, a:a + 31],
                        pos[:, 8 * a:8 * a + 8].unsqueeze(2).unsqueeze(3).to_broadcast([P, 8, 4, 31]), ALU.add)
                i.then_inc(k2_done, 1)
            pool.drain()
            pool.sem_inc(k2_done, 1)

            pool.wait_ge(evac[0], M_W1K + 1)
            pool.wait_ge(evac[1], M_W1K + 1)
            for j in range(2):
                with pool.Fori(0, 2) as i:
                    waits(pool, (q_cur, i + 2 * j + 1), (sc_done, 32 * i + 64 * j + 2))
                    for u in range(2):
                        for half in range(2):
                            a = pool.tensor_scalar(SD[u][half], c("dist"), slope[:, u, half:half + 1], 0.0,
                                                   ALU.mult, ALU.add)
                        a.then_inc(sd_done, 1)
                    for u in range(2):
                        t = 2 * i + 4 * j + u
                        at = bass.ds(t, 1)
                        waits(pool, (o_done, t + 3))
                        pool.tensor_tensor(YT[u].unsqueeze(1), YT[u].unsqueeze(1), GA[:, at, :], ALU.mult)
                        pool.drain()
                        pool.tensor_tensor(G[:, at, :], G[:, at, :], YT[u].unsqueeze(1), ALU.add).then_inc(o_added, 1)
            pool.wait_ge(chunk_done, 4 * R_WOUT + KT + SLOTS)
            pool.dma_start(PP, pT.rearrange("(k p) n -> p k n", p=P)).then_inc(p_in, 16)
            pool.dma_start(PALL, par2_d).then_inc(par2_in, 16)
            pool.dma_start(GAM, gamma_d).then_inc(par2_in, 16)
            pool.dma_start(SIN.bitcast(I32), pos_d.to_broadcast([P, S])).then_inc(pos_in, 16)
            pool.wait_ge(chunk_done, 4 * R_PLEP + 2 + SLOTS)
            pool.dma_start(MEM, memT.rearrange("(k p) n -> p k n", p=P)).then_inc(mem_in, 16)
            with pool.Fori(0, LAYERS) as l:
                M0 = PAIRS1 + PAIRS2 * l
                waits(pool, (layer_end, l + 1), (chunk_done, 4 * ROUNDS1 + 4 * ROUNDS2 * l + SLOTS + 1))
                pool.memset(AH[:, :, 0:15], 0.0)
                pool.memset(AH[:, :, 15 + S:], 0.0)
                pool.memset(GCX[:, :, 0:1], 0.0)
                pool.memset(GCX[:, :, 1 + S:], 0.0)
                pool.drain()
                pool.sem_inc(edge_done, 1)
                pool.memset(PS[:, 2:4, :], 1.0)
                pool.drain()
                pool.wait_ge(evac[0], M0 + N_QG + 2)
                pool.sem_inc(hg_up, 1)
                for lev in range(HLEV - 1):
                    m = 1 << lev
                    pool.wait_ge(hg_qk, 10 * l + lev + 2)
                    pf, pb, sf, sb_ = (PS[:, i, :].rearrange("p (n s m) -> p s n m", s=2, m=m) for i in range(4))
                    nb = 2 * S // (2 * m)
                    whole = lambda ap, at: ap[:, :, at:at + 1].to_broadcast([P, nb, m])
                    pool.tensor_tensor(sf[:, 0], sf[:, 0], whole(pf[:, 1], m - 1), ALU.mult)
                    pool.tensor_tensor(sb_[:, 1], sb_[:, 1], whole(pb[:, 0], 0), ALU.mult)
                    pool.drain()
                    pool.tensor_tensor(pf[:, 1], pf[:, 1], whole(pf[:, 0], m - 1), ALU.mult)
                    pool.tensor_tensor(pb[:, 0], pb[:, 0], whole(pb[:, 1], 0), ALU.mult)
                    pool.drain()
                    pool.sem_inc(hg_up, 1)
            pool.wait_ge(layer_end, LAYERS + 1)
            pool.dma_start(out.rearrange("(k p) n -> p k n", p=P), X).then_inc(out_done, 16)
            pool.wait_ge(out_done, 16)


def constants():
    f = np.float32
    t = {}
    t["ident"] = np.eye(P)
    t["ones"] = np.ones((P, P))
    t["halves"] = np.kron(np.eye(2), np.ones((64, 64)))
    p = np.arange(P)[:, None]
    d = np.arange(512)[None, :] - 384 - p
    t["dist"] = np.where(d > 0, -BIG, d)
    t["zeros"] = np.zeros((P, 512))
    tok = (np.arange(TT)[None, :, None] * P + p[:, :, None])
    cd = np.arange(CC)[None, None, :] * 16 + 31 - tok
    t["cmp_dist"] = np.where(cd > 0, 0, cd).reshape(P, -1)
    t["cmp_neg"] = np.where(cd > 0, -BIG, 0).reshape(P, -1)
    t["slopes"] = np.tile(np.exp2(-8.0 * np.arange(1, HEADS + 1) / HEADS)[None], (P, 1))
    t["eps"] = np.full((P, 1), EPS)
    rot = np.zeros((P, 96))
    for i in range(16):
        rot[80 + i, 64 + i] = -1
        rot[64 + i, 80 + i] = 1
    t["rot"] = rot
    inv = np.zeros((P, 1))
    inv[64:80, 0] = inv[80:96, 0] = 10000.0 ** (-np.arange(0, 32, 2) / 32.0)
    t["inv_freq"] = inv
    s_, t_ = np.arange(P)[:, None], np.arange(P)[None, :]
    lv = [((s_ >> (l + 1)) == (t_ >> (l + 1))) & ((s_ >> l) != (t_ >> l)) for l in range(7)]
    t["levels"] = np.concatenate([x.astype(f) for x in lv], axis=1)
    return np.ascontiguousarray(np.concatenate([t[n].astype(f) for n, _ in CONST_FIELDS], axis=1))


def tiles(w, cols=P):
    k, n = w.shape
    return w.reshape(k // P, P, n // cols, cols).transpose(2, 1, 0, 3).reshape(n // cols, P, -1)


def vec(v):
    return v.reshape(-1, P).T


def block_diag(w):
    w = w.reshape(2, 2, 4, HD, HD).swapaxes(1, 2).reshape(w.shape)
    z = np.zeros((w.shape[0] // 2, P, P), w.dtype)
    z[:, 0:64, 0:64] = w[0::2]
    z[:, 64:128, 64:128] = w[1::2]
    return z.transpose(1, 0, 2).reshape(P, -1)


def by_turn(w):
    return w.reshape(*w.shape[:-1], 2, 2, 4, HD).swapaxes(-2, -3).reshape(w.shape)


def first_stream(i):
    w = i["w_in"][0]
    at = np.cumsum([0, D, D, D, 256, 256, 256, 256, 256, 256, 48, D, D])
    sec = [w[:, a:b] for a, b in zip(at[:-1], at[1:])]
    xr, gr, q, kc, vc, ks, vs, kw, vw, gn, gmr, gma = sec
    xr, gr, q, gmr, gma = (by_turn(m) for m in (xr, gr, q, gmr, gma))
    ffn = i["ffn_w_gate_up"][0].reshape(D, 2, FT, P).transpose(0, 2, 1, 3).reshape(D, -1)
    vv = np.concatenate([vs, vw], axis=1).reshape(4, 2, P, S).transpose(0, 2, 1, 3).reshape(4, P, CH)
    w1 = [i[n][0].reshape(4, 4, P, 256).transpose(0, 2, 1, 3).reshape(4, P, CH) for n in ("cmp_k_w1", "cmp_v_w1")]
    dn = down_chunks(i["ffn_w_down"][0])
    pp = i["ple_w_proj"][0].reshape(2, P, 2, 4, P).transpose(2, 1, 3, 0, 4).reshape(2, P, CH)
    parts = [tiles(xr), tiles(gr), tiles(kc), tiles(vc), tiles(ks), tiles(kw), vv, tiles(q), tiles(gmr), tiles(gma),
             w1[0], w1[1], tiles(np.ascontiguousarray(by_turn(i["w_out"][0].T).T)), tiles(ffn), dn, tiles(i["ple_w_gate"][0]), pp,
             np.zeros((2, P, CH), np.float32)]
    return parts


def down_chunks(w):
    w = np.concatenate([w, np.zeros((24 * P - FF, D), w.dtype)])
    return w.reshape(3, 8, P, 8, P).transpose(3, 0, 2, 1, 4).reshape(24, P, CH)


def first_params(i):
    t = {"mix_pre": vec(i["norm_mix_pre"][0]), "mix_post": vec(i["norm_mix_post"][0]),
         "ffn_pre": vec(i["norm_ffn_pre"][0]), "ffn_post": vec(i["norm_ffn_post"][0]),
         "conv_w": by_turn(i["conv_w"][0]).reshape(4, KT, P).transpose(2, 0, 1).reshape(P, -1),
         "conv_b": vec(by_turn(i["conv_b"][0])), "ba": vec(by_turn(i["lru_ba"][0])),
         "bx": vec(by_turn(i["lru_bx"][0])), "lam": vec(by_turn(i["lru_lambda"][0])), "ple_b": vec(i["ple_b_gate"][0]),
         "wa": block_diag(i["lru_wa"][0]), "wx": block_diag(i["lru_wx"][0]),
         "w2k": np.concatenate([i["cmp_k_w2"][0].reshape(2, P, 1, HD)] * 2, axis=2).transpose(1, 0, 2, 3).reshape(P, -1),
         "w2v": i["cmp_v_w2"][0].reshape(2, P, HD).transpose(1, 0, 2).reshape(P, -1),
         "pos_k": i["cmp_pos_k"][0].reshape(16, P).T, "pos_v": i["cmp_pos_v"][0].reshape(16, P).T,
         "w_gate": i["w_in"][0][:, 4608:4656].reshape(KT, P, 48).transpose(1, 0, 2).reshape(P, -1)}
    return np.ascontiguousarray(np.concatenate([t[n] for n, _ in PAR1_FIELDS], axis=1))


def vec2(v):
    return v.reshape(v.shape[0], -1, P).transpose(2, 0, 1)


def second_stream(i, l):
    w = i["w_in_2"][l]
    at = np.cumsum([0] + [256] * 10 + [256, 128, 32])
    a, g, q, zf, zb, v, gg, gb, gc, xin, cq, ckv, kr = [w[:, x:y] for x, y in zip(at[:-1], at[1:])]
    z = np.zeros((D, P), w.dtype)
    z[:, 64:96] = kr
    token = lambda m: m.reshape(2, 4, P, 256).transpose(0, 2, 1, 3).reshape(2, P, CH)
    up = np.zeros((4, P, CH), w.dtype)
    up[0, :, :768] = i["m_wuq_2"][l].reshape(2, P, 384).transpose(1, 0, 2).reshape(P, 768)
    up[1, :, :512] = i["m_wukv_2"][l].reshape(P, 4, 2, HD).transpose(0, 2, 1, 3).reshape(P, 512)
    xkv = i["x_wkv_2"][l].reshape(D, 4, 2, HD).transpose(0, 2, 1, 3).reshape(D, 2, 256)
    xo = i["x_wo_2"][l].reshape(2, P, 2, 4, P).transpose(2, 1, 3, 0, 4).reshape(2, P, CH)
    ffn = i["f_w13_2"][l].reshape(D, 2, FT, P).transpose(0, 2, 1, 3).reshape(D, -1)
    return [tiles(a), tiles(g), tiles(zf), tiles(zb), tiles(q), tiles(gg), token(v), tiles(cq), tiles(ckv), tiles(z),
            tiles(xin), tiles(gc), tiles(gb), up, tiles(xkv[:, 0]), token(xkv[:, 1]), tiles(i["w_out_2"][l]),
            tiles(i["x_wq_2"][l]), xo, tiles(ffn), down_chunks(i["f_w2_2"][l])]


def second_params(i):
    rows = lambda v: np.pad(v, ((0, 0), (0, P - v.shape[1]))).T[:, :, None]
    taps = lambda w: w.reshape(2, -1, 2, P).transpose(3, 0, 1, 2).reshape(P, 2, -1)
    t = {"g_mix": vec2(i["g_mix_2"]), "a_dw_w": taps(i["a_dw_w_2"]), "a_dw_b": vec2(i["a_dw_b_2"]),
         "a_ln_g": vec2(i["a_ln_g_2"]), "a_ln_b": vec2(i["a_ln_b_2"]), "h_onorm": vec2(i["h_onorm_g_2"]),
         "c_dw_w": taps(i["c_dw_w_2"]), "c_dw_b": vec2(i["c_dw_b_2"]), "qa": vec2(i["m_qa_g_2"]),
         "kva": vec2(i["m_kva_g_2"]), "qn": rows(i["m_qn_g_2"]), "kn": rows(i["m_kn_g_2"]),
         "g_branch": vec2(i["g_branch_2"]), "g_xq": vec2(i["g_xq_2"]), "g_mem": vec2(i["g_mem_2"]),
         "x_qn": vec2(np.concatenate([i["x_qn_g_2"]] * 2, axis=1)),
         "x_kn": vec2(np.concatenate([i["x_kn_g_2"]] * 2, axis=1)), "g_ffn": vec2(i["g_ffn_2"])}
    return np.ascontiguousarray(np.concatenate([t[n] for n, _ in PAR2_FIELDS], axis=2))


def kernel(**inputs):
    import concourse.bacc as _bacc
    from concourse.bass_utils import run_bass_kernel_spmd as _run

    i = {n: np.asarray(a) for n, a in inputs.items()}
    arrays = {
        "wstream": np.concatenate(first_stream(i) + second_stream(i, 0) + second_stream(i, 1)),
        "consts": constants(),
        "par1": first_params(i),
        "xT": np.ascontiguousarray(i["x"][0].T),
        "pT": np.ascontiguousarray(i["p"][0, 0].T),
        "par2": second_params(i),
        "gamma": np.ascontiguousarray(i["h_gamma_2"].reshape(2, 2, 2, P).transpose(3, 1, 0, 2).reshape(P, 2, 4)),
        "memT": np.ascontiguousarray(i["mem_2"][0].T),
        "positions": np.ascontiguousarray(i["positions_2"].astype(np.int32)),
    }
    nc = _bacc.Bacc("TRN2", target_bir_lowering=False, num_devices=1)
    args = [nc.dram_tensor(n, a.shape, mybir.dt.from_np(a.dtype), kind="ExternalInput").ap() for n, a in arrays.items()]
    out = nc.dram_tensor("out", (D, S), F32, kind="ExternalOutput").ap()
    program(nc, *args, out)
    r = _run(nc, [arrays], core_ids=[0])
    got = r.results[0]["out"]
    return np.ascontiguousarray(got.T)[None]
```
